# Optimizing a Trainium2 kernel written in Bass

```python
import jax, jax.numpy as jnp
from jax import lax
import numpy as np
import math

D_MODEL = 1024
BATCH = 1
SEQ = 256
DEPTH = 1

CHUNK = 64
N_META = 16
HEAD_DIM = 64
Q_BLOCK = 128
POOL_WINDOWS = (2, 4, 8, 16)
N_POOL_GROUPS = 4
POOL_WIDTH = D_MODEL // 4
POOL_GROUP = POOL_WIDTH // N_POOL_GROUPS
FOX_HEADS = (3 * D_MODEL // 8) // HEAD_DIM
FOX_WIDTH = FOX_HEADS * HEAD_DIM
SB_HEADS = (3 * D_MODEL // 8) // HEAD_DIM
SB_WIDTH = SB_HEADS * HEAD_DIM
MIX_WIDTH = POOL_WIDTH + FOX_WIDTH + SB_WIDTH
IN_WIDTH = POOL_WIDTH + 3 * FOX_WIDTH + FOX_HEADS + 3 * SB_WIDTH
IN_SPLITS = (
    POOL_WIDTH,
    POOL_WIDTH + FOX_WIDTH,
    POOL_WIDTH + 2 * FOX_WIDTH,
    POOL_WIDTH + 3 * FOX_WIDTH,
    POOL_WIDTH + 3 * FOX_WIDTH + FOX_HEADS,
    POOL_WIDTH + 3 * FOX_WIDTH + FOX_HEADS + SB_WIDTH,
    POOL_WIDTH + 3 * FOX_WIDTH + FOX_HEADS + 2 * SB_WIDTH,
)
D_FF = ((8 * D_MODEL // 3 + 255) // 256) * 256
EPS = 1e-6


def rmsnorm(x, g):
    x32 = x.astype(jnp.float32)
    y = x32 * lax.rsqrt(jnp.mean(x32 * x32, axis=-1, keepdims=True) + EPS)
    return (y * g.astype(jnp.float32)).astype(x.dtype)

def head_rmsnorm(y, gain, n_heads):
    b, l, _ = y.shape
    y32 = y.reshape(b, l, n_heads, HEAD_DIM).astype(jnp.float32)
    y32 = y32 * lax.rsqrt(jnp.mean(y32 * y32, axis=-1, keepdims=True) + EPS)
    return (y32.reshape(b, l, n_heads * HEAD_DIM) * gain.astype(jnp.float32)).astype(y.dtype)

def split_heads(t, n_heads):
    b, l, _ = t.shape
    return t.reshape(b, l, n_heads, HEAD_DIM).transpose(0, 2, 1, 3)

def query_blocks(t):
    l = t.shape[2]
    t = t.reshape(t.shape[:2] + (l // Q_BLOCK, Q_BLOCK) + t.shape[3:])
    return jnp.moveaxis(t, 2, 0)

def merge_blocks(o):
    nblk, b, h, q, d = o.shape
    o = jnp.moveaxis(o, 0, 2).reshape(b, h, nblk * q, d)
    return o.transpose(0, 2, 1, 3).reshape(b, nblk * q, h * d)

def multiscale_pool_mixer(u, pool_w, pool_scale):
    b, l, _ = u.shape
    ug = u.reshape(b, l, N_POOL_GROUPS, POOL_GROUP).astype(jnp.float32)
    cs = jnp.cumsum(ug, axis=1)
    cs0 = jnp.concatenate([jnp.zeros_like(cs[:, :1]), cs], axis=1)
    t1 = jnp.arange(1, l + 1)[:, None]
    win = jnp.array(POOL_WINDOWS, dtype=jnp.int32)[None, :]
    lo = jnp.maximum(t1 - win, 0)
    window_sum = cs - cs0[:, lo, jnp.arange(N_POOL_GROUPS)[None, :]]
    mean = window_sum / (t1 - lo).astype(jnp.float32)[None, :, :, None]
    d = (mean - ug).astype(u.dtype)
    mixed = jnp.einsum('blgc,gcd->blgd', d, pool_w)
    return mixed.reshape(b, l, POOL_WIDTH) * pool_scale

def forgetting_attention(q, k, v, log_f):
    c = jnp.cumsum(log_f.astype(jnp.float32), axis=1).transpose(0, 2, 1)
    l = q.shape[2]
    pos = jnp.arange(l)
    k32 = k.astype(jnp.float32)
    scale = HEAD_DIM ** -0.5

    def block(args):
        qb, cb, tq = args
        s = jnp.einsum('bhqd,bhkd->bhqk', qb.astype(jnp.float32), k32) * scale
        s = s + cb[..., None] - c[:, :, None, :]
        s = jnp.where(pos[None, :] <= tq[:, None], s, -jnp.inf)
        p = jax.nn.softmax(s, axis=-1)
        return jnp.einsum('bhqk,bhkd->bhqd', p.astype(v.dtype), v)

    o = lax.map(block, (query_blocks(q), query_blocks(c), pos.reshape(-1, Q_BLOCK)))
    return merge_blocks(o)

def stick_breaking_attention(q, k, v):
    l = q.shape[2]
    pos = jnp.arange(l)
    k32 = k.astype(jnp.float32)
    scale = HEAD_DIM ** -0.5

    def block(args):
        qb, tq = args
        z = jnp.einsum('bhqd,bhkd->bhqk', qb.astype(jnp.float32), k32) * scale
        strict = pos[None, :] < tq[:, None]
        log_beta = jax.nn.log_sigmoid(z)
        log_1m = jnp.where(strict, jax.nn.log_sigmoid(-z), 0.0)
        later = lax.cumsum(log_1m, axis=3, reverse=True) - log_1m
        a = jnp.where(strict, jnp.exp(log_beta + later), 0.0)
        return jnp.einsum('bhqk,bhkd->bhqd', a.astype(v.dtype), v)

    o = lax.map(block, (query_blocks(q), pos.reshape(-1, Q_BLOCK)))
    return merge_blocks(o)

def first_inputs(seed: int = 0) -> dict:
    key = jax.random.key(seed)
    ks = jax.random.split(key, 15)
    f32 = jnp.float32
    n = jax.random.normal
    return {
        'x': n(ks[0], (BATCH, SEQ, D_MODEL), f32),
        'meta_tokens': n(ks[1], (N_META, D_MODEL), f32),
        'norm1': 1.0 + 0.05 * n(ks[2], (DEPTH, D_MODEL), f32),
        'w_in': n(ks[3], (DEPTH, D_MODEL, IN_WIDTH), f32) * D_MODEL ** -0.5,
        'forget_bias': jax.random.uniform(ks[4], (DEPTH, FOX_HEADS), f32, 1.0, 4.0),
        'pool_w': n(ks[5], (DEPTH, N_POOL_GROUPS, POOL_GROUP, POOL_GROUP), f32) * POOL_GROUP ** -0.5,
        'pool_scale': 1.0 + 0.1 * n(ks[6], (DEPTH, POOL_WIDTH), f32),
        'fox_out_gain': 1.0 + 0.05 * n(ks[7], (DEPTH, FOX_WIDTH), f32),
        'sb_out_gain': 1.0 + 0.05 * n(ks[8], (DEPTH, SB_WIDTH), f32),
        'w_out': n(ks[9], (DEPTH, MIX_WIDTH, D_MODEL), f32) * MIX_WIDTH ** -0.5,
        'norm2': 1.0 + 0.05 * n(ks[10], (DEPTH, D_MODEL), f32),
        'w_gate': n(ks[11], (DEPTH, D_MODEL, D_FF), f32) * D_MODEL ** -0.5,
        'w_up': n(ks[12], (DEPTH, D_MODEL, D_FF), f32) * D_MODEL ** -0.5,
        'w_down': n(ks[13], (DEPTH, D_FF, D_MODEL), f32) * D_FF ** -0.5,
        'final_norm': 1.0 + 0.05 * n(ks[14], (D_MODEL,), f32),
    }

def first_block(x, meta_tokens, norm1, w_in, forget_bias, pool_w, pool_scale, fox_out_gain,
              sb_out_gain, w_out, norm2, w_gate, w_up, w_down, final_norm):
    b, s_len, _ = x.shape
    l = N_META + s_len
    l_pad = -(-l // Q_BLOCK) * Q_BLOCK
    meta = jnp.broadcast_to(meta_tokens[None].astype(x.dtype), (b, N_META, D_MODEL))
    h = jnp.concatenate([meta, x, jnp.zeros((b, l_pad - l, D_MODEL), x.dtype)], axis=1)

    for i in range(DEPTH):
        a = rmsnorm(h, norm1[i])
        proj = a @ w_in[i]
        u, qf, kf, vf, fl, qs, ks_, vs = jnp.split(proj, IN_SPLITS, axis=-1)
        y_pool = multiscale_pool_mixer(u, pool_w[i], pool_scale[i])
        log_f = jax.nn.log_sigmoid(fl.astype(jnp.float32) + forget_bias[i].astype(jnp.float32))
        y_fox = forgetting_attention(split_heads(qf, FOX_HEADS), split_heads(kf, FOX_HEADS),
                                     split_heads(vf, FOX_HEADS), log_f)
        y_fox = head_rmsnorm(y_fox, fox_out_gain[i], FOX_HEADS)
        y_sb = stick_breaking_attention(split_heads(qs, SB_HEADS), split_heads(ks_, SB_HEADS),
                                        split_heads(vs, SB_HEADS))
        y_sb = head_rmsnorm(y_sb, sb_out_gain[i], SB_HEADS)
        h = h + jnp.concatenate([y_pool, y_fox, y_sb], axis=-1) @ w_out[i]
        a = rmsnorm(h, norm2[i])
        h = h + (jax.nn.silu(a @ w_gate[i]) * (a @ w_up[i])) @ w_down[i]

    h = rmsnorm(h, final_norm)
    return h[:, N_META:N_META + s_len]


DEPTH_2 = 2

D_FF_2 = 4 * D_MODEL
CONV_CH = D_MODEL // 2
CONV_WIDTH = 31
ATTN_HEAD_DIM = 64
ATTN_HEADS = (D_MODEL // 2) // ATTN_HEAD_DIM
ATTN_WIDTH = ATTN_HEADS * ATTN_HEAD_DIM
MOBA_BLOCK = 256
MOBA_TOP_K = 3
MOBA_Q_CHUNK = 32
AB_IN_WIDTH = 2 * CONV_CH + 3 * ATTN_WIDTH
AB_OUT_WIDTH = CONV_CH + ATTN_WIDTH
LRU_WIDTH = D_MODEL
LRU_HEADS = 8
LRU_BLOCK = LRU_WIDTH // LRU_HEADS
LRU_CONV_WIDTH = 4
LRU_C = 8.0
N_EVEN = (DEPTH_2 + 1) // 2
N_ODD = DEPTH_2 // 2


def rmsnorm_2(x, g):
    xf = x.astype(jnp.float32)
    y = xf * lax.rsqrt(jnp.mean(xf * xf, axis=-1, keepdims=True) + EPS)
    return (y * g.astype(jnp.float32)).astype(x.dtype)

def layernorm(x, g, b):
    xf = x.astype(jnp.float32)
    mu = jnp.mean(xf, axis=-1, keepdims=True)
    var = jnp.mean(jnp.square(xf - mu), axis=-1, keepdims=True)
    y = (xf - mu) * lax.rsqrt(var + EPS)
    return (y * g.astype(jnp.float32) + b.astype(jnp.float32)).astype(x.dtype)

def causal_depthwise_conv(x, w):
    width, ch = w.shape
    return lax.conv_general_dilated(
        x, w[:, None, :].astype(x.dtype), window_strides=(1,),
        padding=[(width - 1, 0)], dimension_numbers=("NWC", "WIO", "NWC"),
        feature_group_count=ch)

def alibi_slopes(n_heads):
    return 2.0 ** (-8.0 * jnp.arange(1, n_heads + 1, dtype=jnp.float32) / n_heads)

def conformer_conv(u_val, u_gate, conv_w, ln_g, ln_b):
    z = u_val * jax.nn.sigmoid(u_gate)
    z = causal_depthwise_conv(z, conv_w)
    z = layernorm(z, ln_g, ln_b)
    return jax.nn.silu(z)

def moba_attention(q, k, v):
    b, s, h, dh = q.shape
    nb = -(-s // MOBA_BLOCK)
    sp = nb * MOBA_BLOCK
    pad = sp - s
    q, k, v = [jnp.pad(t.transpose(0, 2, 1, 3), ((0, 0), (0, 0), (0, pad), (0, 0)))
               for t in (q, k, v)]
    slopes = alibi_slopes(h)[None, :, None, None]
    scale = dh ** -0.5
    n_past = min(MOBA_TOP_K, nb - 1)
    offs = jnp.arange(MOBA_BLOCK)
    kb = k.reshape(b, h, nb, MOBA_BLOCK, dh)
    vb = v.reshape(b, h, nb, MOBA_BLOCK, dh)
    bi = jnp.arange(b)[:, None, None, None]
    hi = jnp.arange(h)[None, :, None, None]

    if n_past > 0:
        kbar = jnp.mean(kb.astype(jnp.float32), axis=3)
        gate = jnp.einsum("bhsd,bhnd->bhsn", q.astype(jnp.float32), kbar)
        qblk = jnp.arange(sp) // MOBA_BLOCK
        past = jnp.arange(nb)[None, :] < qblk[:, None]
        gate = jnp.where(past, gate, -jnp.inf)
        top_val, top_idx = lax.top_k(gate, n_past)
        top_ok = jnp.isfinite(top_val)

    def chunk(c):
        start = c * MOBA_Q_CHUNK
        t = start + jnp.arange(MOBA_Q_CHUNK)
        qc = lax.dynamic_slice_in_dim(q, start, MOBA_Q_CHUNK, axis=2)
        own0 = (start // MOBA_BLOCK) * MOBA_BLOCK
        k_own = lax.dynamic_slice_in_dim(k, own0, MOBA_BLOCK, axis=2)
        v_own = lax.dynamic_slice_in_dim(v, own0, MOBA_BLOCK, axis=2)
        dist_own = (t[:, None] - (own0 + offs)[None, :]).astype(jnp.float32)
        l_own = (jnp.einsum("bhqd,bhkd->bhqk", qc, k_own).astype(jnp.float32) * scale
                 - slopes * dist_own)
        l_own = jnp.where(dist_own >= 0, l_own, -jnp.inf)
        if n_past > 0:
            idx = lax.dynamic_slice_in_dim(top_idx, start, MOBA_Q_CHUNK, axis=2)
            ok = lax.dynamic_slice_in_dim(top_ok, start, MOBA_Q_CHUNK, axis=2)
            k_sel = kb[bi, hi, idx]
            v_sel = vb[bi, hi, idx]
            pos = idx[..., None] * MOBA_BLOCK + offs
            dist = (t[None, None, :, None, None] - pos).astype(jnp.float32)
            l_sel = (jnp.einsum("bhqd,bhqnkd->bhqnk", qc, k_sel).astype(jnp.float32) * scale
                     - slopes[..., None] * dist)
            l_sel = jnp.where(ok[..., None], l_sel, -jnp.inf)
            n_sel = n_past * MOBA_BLOCK
            logits = jnp.concatenate(
                [l_sel.reshape(b, h, MOBA_Q_CHUNK, n_sel), l_own], axis=-1)
            p = jax.nn.softmax(logits, axis=-1).astype(v.dtype)
            p_sel = p[..., :n_sel].reshape(b, h, MOBA_Q_CHUNK, n_past, MOBA_BLOCK)
            p_own = p[..., n_sel:]
            o = (jnp.einsum("bhqnk,bhqnkd->bhqd", p_sel, v_sel)
                 + jnp.einsum("bhqk,bhkd->bhqd", p_own, v_own))
        else:
            p_own = jax.nn.softmax(l_own, axis=-1).astype(v.dtype)
            o = jnp.einsum("bhqk,bhkd->bhqd", p_own, v_own)
        return o

    out = lax.map(chunk, jnp.arange(sp // MOBA_Q_CHUNK))
    out = out.transpose(1, 2, 0, 3, 4).reshape(b, h, sp, dh)[:, :, :s]
    return out.transpose(0, 2, 1, 3)

def rg_lru(x, w_r, b_r, w_i, b_i, lam):
    b, s, w = x.shape
    xb = x.reshape(b, s, LRU_HEADS, LRU_BLOCK)
    r = jax.nn.sigmoid(jnp.einsum("bshi,hij->bshj", xb, w_r) + b_r).reshape(b, s, w)
    i = jax.nn.sigmoid(jnp.einsum("bshi,hij->bshj", xb, w_i) + b_i).reshape(b, s, w)
    log_a = -LRU_C * r.astype(jnp.float32) * jax.nn.softplus(-lam.astype(jnp.float32))
    a = jnp.exp(log_a)
    mult = jnp.sqrt(-jnp.expm1(2.0 * log_a))
    bx = mult * (i * x).astype(jnp.float32)

    def combine(e1, e2):
        a1, b1 = e1
        a2, b2 = e2
        return a1 * a2, a2 * b1 + b2

    _, hseq = lax.associative_scan(combine, (a, bx), axis=1)
    return hseq.astype(x.dtype)

def mixer_ab(h, w_in, conv_w, ln_g, ln_b, w_out):
    b, s, _ = h.shape
    u = h @ w_in
    u_val, u_gate, q, k, v = jnp.split(
        u, np.cumsum([CONV_CH, CONV_CH, ATTN_WIDTH, ATTN_WIDTH]).tolist(), axis=-1)
    ya = conformer_conv(u_val, u_gate, conv_w, ln_g, ln_b)
    shp = (b, s, ATTN_HEADS, ATTN_HEAD_DIM)
    yb = moba_attention(q.reshape(shp), k.reshape(shp), v.reshape(shp)).reshape(b, s, ATTN_WIDTH)
    return jnp.concatenate([ya, yb], axis=-1) @ w_out

def mixer_c(h, w_in, conv_w, conv_b, w_r, b_r, w_i, b_i, lam, w_out):
    u = h @ w_in
    gate, xr = jnp.split(u, 2, axis=-1)
    xr = causal_depthwise_conv(xr, conv_w) + conv_b
    y = rg_lru(xr, w_r, b_r, w_i, b_i, lam) * jax.nn.gelu(gate)
    return y @ w_out

def sq_relu_mlp(h, w_up, w_down):
    return jnp.square(jax.nn.relu(h @ w_up)) @ w_down

def second_inputs(seed: int = 0) -> dict:
    key = jax.random.key(seed)
    ks = iter(jax.random.split(key, 32))
    f32 = jnp.float32

    def nrm(shape, fan_in):
        return jax.random.normal(next(ks), shape, f32) * (fan_in ** -0.5)

    def gain(shape):
        return 1.0 + 0.02 * jax.random.normal(next(ks), shape, f32)

    def bias(shape):
        return 0.01 * jax.random.normal(next(ks), shape, f32)

    x = jax.random.normal(next(ks), (BATCH, SEQ, D_MODEL), f32)
    a_c = jax.random.uniform(next(ks), (N_ODD, LRU_WIDTH), f32, 0.9, 0.999)
    a_base = a_c ** (1.0 / LRU_C)
    lam = jnp.log(a_base) - jnp.log1p(-a_base)
    return {
        "x": x,
        "mix_norm": gain((DEPTH_2, D_MODEL)),
        "mlp_norm": gain((DEPTH_2, D_MODEL)),
        "w_up": nrm((DEPTH_2, D_MODEL, D_FF_2), D_MODEL),
        "w_down": nrm((DEPTH_2, D_FF_2, D_MODEL), D_FF_2),
        "ab_w_in": nrm((N_EVEN, D_MODEL, AB_IN_WIDTH), D_MODEL),
        "ab_conv_w": nrm((N_EVEN, CONV_WIDTH, CONV_CH), CONV_WIDTH),
        "ab_ln_g": gain((N_EVEN, CONV_CH)),
        "ab_ln_b": bias((N_EVEN, CONV_CH)),
        "ab_w_out": nrm((N_EVEN, AB_OUT_WIDTH, D_MODEL), AB_OUT_WIDTH),
        "c_w_in": nrm((N_ODD, D_MODEL, 2 * LRU_WIDTH), D_MODEL),
        "c_conv_w": nrm((N_ODD, LRU_CONV_WIDTH, LRU_WIDTH), LRU_CONV_WIDTH),
        "c_conv_b": bias((N_ODD, LRU_WIDTH)),
        "c_w_r": nrm((N_ODD, LRU_HEADS, LRU_BLOCK, LRU_BLOCK), LRU_BLOCK),
        "c_b_r": bias((N_ODD, LRU_HEADS, LRU_BLOCK)),
        "c_w_i": nrm((N_ODD, LRU_HEADS, LRU_BLOCK, LRU_BLOCK), LRU_BLOCK),
        "c_b_i": bias((N_ODD, LRU_HEADS, LRU_BLOCK)),
        "c_lambda": lam,
        "c_w_out": nrm((N_ODD, LRU_WIDTH, D_MODEL), LRU_WIDTH),
        "final_norm": gain((D_MODEL,)),
    }

def second_block(x, mix_norm, mlp_norm, w_up, w_down, ab_w_in, ab_conv_w, ab_ln_g, ab_ln_b,
              ab_w_out, c_w_in, c_conv_w, c_conv_b, c_w_r, c_b_r, c_w_i, c_b_i, c_lambda,
              c_w_out, final_norm):
    for layer in range(DEPTH_2):
        j = layer // 2
        h = rmsnorm_2(x, mix_norm[layer])
        if layer % 2 == 0:
            y = mixer_ab(h, ab_w_in[j], ab_conv_w[j], ab_ln_g[j], ab_ln_b[j], ab_w_out[j])
        else:
            y = mixer_c(h, c_w_in[j], c_conv_w[j], c_conv_b[j], c_w_r[j], c_b_r[j],
                        c_w_i[j], c_b_i[j], c_lambda[j], c_w_out[j])
        x = x + y
        x = x + sq_relu_mlp(rmsnorm_2(x, mlp_norm[layer]), w_up[layer], w_down[layer])
    return rmsnorm_2(x, final_norm)


def setup_inputs(seed=0):
    out = dict(first_inputs(seed))
    for name, value in second_inputs(seed + 1).items():
        if name != "x":
            out[name + "_2"] = value
    return out


def reference(
    x, meta_tokens, norm1, w_in, forget_bias, pool_w, pool_scale, fox_out_gain, sb_out_gain,
    w_out, norm2, w_gate, w_up, w_down, final_norm, mix_norm_2, mlp_norm_2, w_up_2, w_down_2,
    ab_w_in_2, ab_conv_w_2, ab_ln_g_2, ab_ln_b_2, ab_w_out_2, c_w_in_2, c_conv_w_2, c_conv_b_2,
    c_w_r_2, c_b_r_2, c_w_i_2, c_b_i_2, c_lambda_2, c_w_out_2, final_norm_2,
):
    x = first_block(
        x, meta_tokens, norm1, w_in, forget_bias, pool_w, pool_scale, fox_out_gain, sb_out_gain,
        w_out, norm2, w_gate, w_up, w_down, final_norm,
    )
    return second_block(
        x, mix_norm_2, mlp_norm_2, w_up_2, w_down_2, ab_w_in_2, ab_conv_w_2, ab_ln_g_2,
        ab_ln_b_2, ab_w_out_2, c_w_in_2, c_conv_w_2, c_conv_b_2, c_w_r_2, c_b_r_2, c_w_i_2,
        c_b_i_2, c_lambda_2, c_w_out_2, final_norm_2,
    )


_drawn_inputs = setup_inputs


def setup_inputs(seed=0):
    import zlib

    import numpy as np

    out = dict(_drawn_inputs(seed))
    spreads = {}
    factors = {'mix_norm_2': 2.914,
     'ab_ln_g_2': 13.902,
     'ab_ln_b_2': 29.233,
     'c_conv_b_2': 22.279,
     'c_b_r_2': 64.0,
     'c_b_i_2': 28.981,
     'mlp_norm_2': 5.035}
    for name, (base, spread) in spreads.items():
        noise = np.random.default_rng([zlib.crc32(name.encode()), seed]).standard_normal(out[name].shape)
        drawn = base * np.exp(spread * noise) if base else spread * noise
        out[name] = __import__('jax').numpy.asarray(drawn.astype(out[name].dtype))
    for name, factor in factors.items():
        out[name] = (out[name] * factor).astype(out[name].dtype)
    return out
```

```python
from contextlib import ExitStack

import concourse.bass as bass
from concourse import mybir

F32 = mybir.dt.float32
F32R = mybir.dt.float32r
ALU = mybir.AluOpType
ACT = mybir.ActivationFunctionType
AX = mybir.AxisListType.X

P = 128
DM = 1024
KC = DM // P
SEQ = 256
NMETA = 16
T1 = NMETA + SEQ
EPS = 1e-6
BIG = 1.0e30

FOX_HEADS = SB_HEADS = 6
HD = 64
QSCALE = HD ** -0.5
POOL_W = 256
FOX_W = FOX_HEADS * HD
FL0 = POOL_W + 3 * FOX_W
SB0 = FL0 + FOX_HEADS
MOBA_HEADS = 8
CONV_T = 31
CONV_C = 4
LRU_T = 4
LRU_C = 8.0

FF1 = 2816 // P
FF2 = 4096 // P

R = 4
LOOKAHEAD = R - 1
SL = KC * P

IN1 = 0
OUT1 = IN1 + 20
MLP1 = OUT1 + KC
IN2 = MLP1 + 3 * FF1
OUT2 = IN2 + 20
MLP2 = OUT2 + KC
IN3 = MLP2 + 2 * FF2
GATES = IN3 + 16
OUT3 = GATES + 2
MLP3 = OUT3 + KC
NSLABS = MLP3 + 2 * FF2

E_IN1 = 0
E_MLP1 = E_IN1 + 20
E_IN2 = E_MLP1 + 2 * FF1
E_MLP2 = E_IN2 + 20
E_IN3 = E_MLP2 + FF2
E_MLP3 = E_IN3 + 16

A_NORM1, A_MIX1, A_NORM2, A_MIX0, A_CAT2, A_MLP0, A_MIXC, A_CONV, A_LRU, A_MLPC = range(10)
(N_NORM1, N_NORM2, N_FINAL1, N_MIX0, N_MLP0, N_MIXC, N_MLPC, N_FINAL2) = range(8)
G_NORM = [KC * n for n in range(8)]
G_CONVB, G_BR, G_BI, G_LAM = (64 + KC * n for n in range(4))
G_PSCALE, G_FOX, G_SB, G_LNG, G_LNB = 96, 98, 101, 104, 108
PAR_A = 112
G_CONVW = PAR_A
G_CCONVW = G_CONVW + CONV_T * CONV_C
PAR_N = G_CCONVW + LRU_T * KC

SBQ = [0, 112, 240]
SBC = [0, 256, 400]
SBN = [256, 144, 16]
SBW = 416


def build(nc, A, out):
    w_in, w_out = A["w_in"][0], A["w_out"][0]
    w_gate, w_up, w_down = A["w_gate"][0], A["w_up"][0], A["w_down"][0]

    def cols(w, c0):
        return w.rearrange("(k p) n -> p k n", p=P)[:, :, bass.ds(c0, P)]

    def rows(w, r0):
        return w[bass.ds(r0, P), :].rearrange("p (n c) -> p n c", c=P)

    with ExitStack() as ctx:
        def sb(name, shape, dt=F32):
            return ctx.enter_context(nc.sbuf_tensor(name, shape, dt))

        def sem(name):
            return ctx.enter_context(nc.semaphore(name))

        bank = [ctx.enter_context(nc.psum_tensor(f"bank{i}", [P, 512], F32)) for i in range(8)]
        gemm_bank = bank[0:2]
        acc_bank = bank[2:6]
        stat_bank = bank[6]
        aux_bank = bank[7]

        raw = sb("raw", [P, R, KC, P])
        whi = sb("whi", [P, R, KC, P], F32R)
        wlo = sb("wlo", [P, R, KC, P], F32R)
        h = sb("h", [P, KC, T1])
        hq = h[:, :, NMETA:T1]
        af = sb("af", [P, KC, T1])
        ahi = sb("ahi", [P, KC, T1], F32R)
        alo = sb("alo", [P, KC, T1], F32R)
        sq = sb("sq", [P, KC, T1])
        std = sb("std", [P, T1])
        rstd = sb("rstd", [P, T1])
        proj = sb("proj", [P, 20, T1])
        hid = sb("hid", [P, 2, SEQ])
        hid2 = sb("hid2", [P, 2, SEQ])
        hidhi = sb("hidhi", [P, 2, SEQ], F32R)
        hidlo = sb("hidlo", [P, 2, SEQ], F32R)
        par_rows = sb("par_rows", [P, 3, P])
        par = sb("par", [P, PAR_N])
        wfl = sb("wfl", [P, KC, FOX_HEADS])
        fbias = sb("fbias", [FOX_HEADS, 1])
        poolw = sb("poolw", [P, 2, HD])
        ident = sb("ident", [P, P])
        ones = sb("ones", [P, P])
        block64 = sb("block64", [P, P])
        tri = sb("tri", [P, P])
        eps = sb("eps", [P, 1])
        zero6 = sb("zero6", [FOX_HEADS, T1])
        sel = sb("sel", [FOX_HEADS, FOX_HEADS, T1])
        nsel = sb("nsel", [FOX_HEADS, FOX_HEADS, P])
        fmask = sb("fmask", [P, 2, T1])
        sbneg = sb("sbneg", [P, SBW])
        sbm = sb("sbm", [P, SBW])
        dist = sb("dist", [P, 2, SEQ])
        lf = sb("lf", [FOX_HEADS, 4, T1])
        cum = sb("cum", [FOX_HEADS, T1])
        vtok = sb("vtok", [P, 3, 2 * FOX_W])
        win = sb("win", [P, 2, T1])
        win2 = sb("win2", [P, 2, T1])
        pd = sb("pd", [P, 2, SEQ])
        ssb = sb("ssb", [P, 2, T1])
        nmax = sb("nmax", [P, 16])
        rsum = sb("rsum", [P, 16])
        rinv = sb("rinv", [P, 16])
        prob = sb("prob", [P, 2, T1])
        probT = sb("probT", [P, 2, 3 * P])
        y = sb("y", [P, KC, SEQ])
        xtok = y[:, :, :].rearrange("p (t a) b -> p t (a b)", t=2)
        sba = sb("sba", [P, 3, SBW])
        sbs = sb("sbs", [P, SBW])
        sbl = sb("sbl", [P, SBW])
        sbr = sb("sbr", [P, SBW])
        sbp = sb("sbp", [P, SBW])
        zpad = sb("zpad", [P, CONV_C, CONV_T - 1 + SEQ])
        t8 = sb("t8", [P, KC, SEQ])
        cv = t8[:, 0:CONV_C, :]
        xmeta = t8[0:NMETA, 0:CONV_C, :].rearrange("p a b -> p (a b)")
        lam = sb("lam", [P, 4, KC])

        raw_loaded = [sem(f"raw_loaded{s}") for s in range(R)]
        hi_done, lo_done, slab_used = sem("hi_done"), sem("lo_done"), sem("slab_used")
        gemm_evac, acc_ready, prod_ready = sem("gemm_evac"), sem("acc_ready"), sem("prod_ready")
        x_loaded, par_loaded, small_loaded = sem("x_loaded"), sem("par_loaded"), sem("small_loaded")
        consts = sem("consts")
        par_T, par_ready = sem("par_T"), sem("par_ready")
        xT, h_ready = sem("xT"), sem("h_ready")
        sq_ready, stat_ready, std_ready = sem("sq_ready"), sem("stat_ready"), sem("std_ready")
        af_ready, ahi_ready, alo_ready = sem("af_ready"), sem("ahi_ready"), sem("alo_ready")
        hid_hi, hid_lo = sem("hid_hi"), sem("hid_lo")
        fl_ready, fl_x, fl_ln, cum_ready = sem("fl_ready"), sem("fl_x"), sem("fl_ln"), sem("cum_ready")
        vT, v_ready = sem("vT"), sem("v_ready")
        q_scaled = sem("q_scaled")
        s_ready, s_biased, m_ready, p_ready = sem("s_ready"), sem("s_biased"), sem("m_ready"), sem("p_ready")
        p_normed, pT, pT_copied, o_ready = sem("p_normed"), sem("pT"), sem("pT_copied"), sem("o_ready")
        o_copied = sem("o_copied")
        z_ready, z_ln, l_ready, r_ready = sem("z_ready"), sem("z_ln"), sem("l_ready"), sem("r_ready")
        r_masked, w_ready, sbo_ready, sbo_copied = sem("r_masked"), sem("w_ready"), sem("sbo_ready"), sem("sbo_copied")
        pool_d, pool_mixed = sem("pool_d"), sem("pool_mixed")
        hsq, hstat, hstd = sem("hsq"), sem("hstat"), sem("hstd")
        glu, conv = sem("glu"), sem("conv")
        ln_mean, ln_dev, ln_sq, ln_var = sem("ln_mean"), sem("ln_dev"), sem("ln_sq"), sem("ln_var")
        ln_std, ln_norm = sem("ln_std"), sem("ln_norm")
        lam_ln, lam_ready, lconv = sem("lam_ln"), sem("lam_ready"), sem("lconv")
        lru_sum, lru_gate, lru_exp, lru_m2 = sem("lru_sum"), sem("lru_gate"), sem("lru_exp"), sem("lru_m2")
        lru_root, lru_gelu, lru_ix = sem("lru_root"), sem("lru_gelu"), sem("lru_ix")
        dve_chain, act_chain, pool_chain = sem("dve_chain"), sem("act_chain"), sem("pool_chain")
        fin_ready, outT, out_copied, stored = sem("fin_ready"), sem("outT"), sem("out_copied"), sem("stored")

        FOX_U = 2 * FOX_HEADS
        MOBA_U = 2 * MOBA_HEADS
        FOX_N = (NMETA + P, NMETA + SEQ)
        FOX_TILES = ((P, NMETA), (P, P, NMETA))
        MOBA_N = (P, 2 * P)
        MOBA_TILES = ((P,), (P, P))
        CAT2_ORDER = (4, 5, 6, 7, 0, 1, 2, 3)
        flat = proj[:, :, :].rearrange("p c t -> p (c t)")
        lru_r = acc_bank
        lru_i = [gemm_bank[0], gemm_bank[1], stat_bank, aux_bank]
        sbo = [gemm_bank[0], gemm_bank[1], aux_bank]
        consts_done = 15

        block = ctx.enter_context(nc.Block())

        @block.sync
        def _(sp):
            def load(n, src, q=0):
                if n >= R:
                    sp.wait_ge(lo_done, n + R * q - R + 1)
                sp.dma_start(raw[:, n % R, :, :], src).then_inc(raw_loaded[n % R], 16)

            xt = A["x"][0].rearrange("(t p) d -> p t d", p=P)
            for t in range(2):
                sp.dma_start(xtok[:, t, :], xt[:, t, :]).then_inc(x_loaded, 16)
            for c in range(11):
                load(IN1 + c, cols(w_in, c * P))
            for c in range(9):
                load(IN1 + 11 + c, cols(w_in, SB0 + c * P))
            for c in range(KC):
                load(OUT1 + c, cols(w_out, c * P))

            def gate_up_down(f, n, q=0):
                load(n, cols(w_gate, f * P), q)
                load(n + 1, cols(w_up, f * P), q)
                load(n + 2, rows(w_down, (f - 1) * P), q)
            load(MLP1, cols(w_gate, 0))
            load(MLP1 + 1, cols(w_up, 0))
            gate_up_down(1, MLP1 + 2)
            with sp.Fori(0, (FF1 - 2) // 4) as it:
                for j in range(4):
                    gate_up_down(it * 4 + 2 + j, MLP1 + 5 + 3 * j, it * 3)
            load(MLP1 + 3 * FF1 - 1, rows(w_down, (FF1 - 1) * P))

            def squared_relu_loads(up, down, base):
                load(base, cols(up, 0))
                load(base + 1, cols(up, P))
                load(base + 2, rows(down, 0))
                with sp.Fori(0, (FF2 - 2) // 2) as it:
                    for j in range(2):
                        load(base + 3 + 2 * j, cols(up, (it * 2 + 2 + j) * P), it)
                        load(base + 4 + 2 * j, rows(down, (it * 2 + 1 + j) * P), it)
                load(base + 2 * FF2 - 1, rows(down, (FF2 - 1) * P))
            for c in range(20):
                load(IN2 + c, cols(A["ab_w_in_2"][0], c * P))
            for c in range(KC):
                load(OUT2 + c, cols(A["ab_w_out_2"][0], c * P))
            squared_relu_loads(A["w_up_2"][0], A["w_down_2"][0], MLP2)
            for c in range(16):
                load(IN3 + c, cols(A["c_w_in_2"][0], c * P))
            load(GATES, A["c_w_r_2"][0].rearrange("h i j -> i h j"))
            load(GATES + 1, A["c_w_i_2"][0].rearrange("h i j -> i h j"))
            for c in range(KC):
                load(OUT3 + c, cols(A["c_w_out_2"][0], c * P))
            squared_relu_loads(A["w_up_2"][1], A["w_down_2"][1], MLP3)

            ot = out[0].rearrange("(t p) d -> p t d", p=P)
            for i in range(4):
                sp.wait_ge(out_copied, i + 1)
                c = slice(512 * (i // 2), 512 * (i // 2) + 512)
                sp.dma_start(ot[:, i % 2, c], xtok[:, i % 2, c]).then_inc(stored, 16)
            sp.wait_ge(stored, 64)

        @block.gpsimd
        def _(pool):
            n = [0]

            def step(ins):
                n[0] += 1
                ins.then_inc(pool_chain, 1)
                pool.wait_ge(pool_chain, n[0])

            def select(buf, op, fill, base, pattern, cm):
                pool.affine_select(out=buf, in_=buf, compare_op=op, fill=fill, base=base,
                                   pattern=pattern, channel_multiplier=cm).then_inc(consts, 1)

            step(pool.memset(ident[:, :], 0.0))
            select(ident[:, :], ALU.not_equal, 1.0, 0, [[-1, P]], 1)
            pool.memset(ones[:, :], 1.0).then_inc(consts, 1)
            pool.memset(eps[:, :], EPS).then_inc(consts, 1)
            step(pool.memset(sel[:, :, :], 0.0))
            select(sel[:, :, :], ALU.not_equal, 1.0, 0, [[-1, FOX_HEADS], [0, T1]], 1)
            step(pool.memset(nsel[:, :, :], 0.0))
            select(nsel[:, :, :], ALU.not_equal, -1.0, 0, [[-1, FOX_HEADS], [0, P]], 1)
            step(pool.memset(block64[:, :], 0.0))
            step(pool.memset(block64[0:HD, 0:HD], 1.0))
            step(pool.memset(block64[HD:P, HD:P], 1.0))
            pool.memset(zero6[:, :], 0.0).then_inc(consts, 1)
            step(pool.memset(tri[:, :], 1.0))
            select(tri[:, :], ALU.is_ge, 0.0, 0, [[-1, P]], 1)
            step(pool.memset(fmask[:, :, :], 0.0))
            select(fmask[:, :, :], ALU.is_ge, -BIG, NMETA, [[P, 2], [-1, T1]], 1)
            step(pool.memset(sbneg[:, :], 0.0))
            step(pool.memset(sbm[:, :], -1.0))
            for i in range(3):
                for buf, fill in ((sbneg, -BIG), (sbm, 0.0)):
                    select(buf[:, SBC[i]:SBC[i] + SBN[i]], ALU.is_gt, fill, NMETA + SBQ[i] - P * i,
                           [[1, SBN[i]]], -1)
            step(pool.iota(dist[:, :, :], pattern=[[P, 2], [-1, SEQ]], base=0, channel_multiplier=1,
                           allow_small_or_imprecise_dtypes=True))
            step(pool.memset(zpad[:, :, 0:CONV_T - 1], 0.0))
            select(dist[:, :, :], ALU.is_ge, BIG, 0, [[P, 2], [-1, SEQ]], 1)

        @block.scalar
        def _(act):
            chain = [0]

            def link(ins):
                chain[0] += 1
                ins.then_inc(act_chain, 1)
                act.wait_ge(act_chain, chain[0])

            def as_rows(a):
                return a.rearrange("(k p) -> k p", p=P)

            def par_row(j, r, a):
                act.dma_start(par_rows[r:r + a.shape[0], j, :], a).then_inc(par_loaded, 16)

            act.dma_start(xmeta[:, :], A["meta_tokens"]).then_inc(x_loaded, 16)
            gains = (A["norm1"][0], A["norm2"][0], A["final_norm"], A["mix_norm_2"][0], A["mlp_norm_2"][0],
                     A["mix_norm_2"][1], A["mlp_norm_2"][1], A["final_norm_2"])
            for i, a in enumerate(gains):
                par_row(0, G_NORM[i], as_rows(a))
            for r, a in ((G_CONVB, A["c_conv_b_2"][0]), (G_LAM, A["c_lambda_2"][0]),
                         (G_PSCALE, A["pool_scale"][0]), (G_FOX, A["fox_out_gain"][0]),
                         (G_SB, A["sb_out_gain"][0]), (G_LNG, A["ab_ln_g_2"][0]), (G_LNB, A["ab_ln_b_2"][0])):
                par_row(0, r, as_rows(a))
            par_row(0, G_BR, A["c_b_r_2"][0])
            par_row(0, G_BI, A["c_b_i_2"][0])
            par_row(1, 0, A["ab_conv_w_2"][0].rearrange("w (k p) -> (w k) p", p=P))
            par_row(2, 0, A["c_conv_w_2"][0].rearrange("w (k p) -> (w k) p", p=P))
            act.dma_start(wfl[:, :, :], w_in.rearrange("(k p) n -> p k n", p=P)[:, :, FL0:SB0])\
               .then_inc(small_loaded, 16)
            act.dma_start(fbias[:, :], A["forget_bias"].rearrange("a n -> n a")).then_inc(small_loaded, 16)
            for g in range(4):
                act.dma_start(poolw[HD * (g % 2):HD * (g % 2) + HD, g // 2, :], A["pool_w"][0, g])\
                   .then_inc(small_loaded, 16)

            def split(n, q=0):
                act.wait_ge(raw_loaded[n % R], 16 * (n // R + 1 + q))
                if n >= R:
                    act.wait_ge(slab_used, n + R * q - R + 1)
                act.activation(whi[:, n % R, :, :], raw[:, n % R, :, :], ACT.Copy).then_inc(hi_done, 1)

            def split_ahead(n, q=0):
                if n + R * (q if type(q) is int else 0) + LOOKAHEAD < NSLABS:
                    split(n + LOOKAHEAD, q)

            def norm(i, lo=NMETA):
                for k in range(KC):
                    act.wait_ge(h_ready, KC * i + k + 1)
                    act.activation(sq[:, k, lo:], h[:, k, lo:], ACT.Square).then_inc(sq_ready, 1)
                act.wait_ge(stat_ready, i + 1)
                act.activation(std[:, lo:], stat_bank[:, lo:T1], ACT.Sqrt, bias=eps[:, 0:1],
                               scale=1.0 / DM).then_inc(std_ready, 1)

            def operand_hi(s, lo=NMETA, order=range(KC)):
                for i, k in enumerate(order):
                    act.wait_ge(af_ready, KC * s + i + 1)
                    act.activation(ahi[:, k, lo:], af[:, k, lo:], ACT.Copy).then_inc(ahi_ready, 1)

            def project(n0, chunks, lo=NMETA):
                with act.Fori(0, chunks // R) as it:
                    for j in range(R):
                        act.wait_ge(slab_used, it * R + n0 + j + 1)
                        act.activation(proj[:, it * R + j, lo:T1], gemm_bank[j % 2][:, lo:T1], ACT.Copy)\
                           .then_inc(gemm_evac, 1)
                        split_ahead(n0 + j, it)

            def residual_splits(n0):
                for j in range(KC):
                    split_ahead(n0 + j)

            def values(v0, groups):
                for g, (m, dst) in enumerate(groups):
                    act.wait_ge(vT, v0 + g + 1)
                    act.activation(dst, acc_bank[2 + g % 2][0:m, 0:dst.shape[1]], ACT.Copy).then_inc(v_ready, 1)

            def attention(units, u0, keys, tiles, pair_done):
                for u in range(units + 1):
                    if u < units:
                        act.wait_ge(m_ready, u0 + u + 1)
                        if u >= 2:
                            act.wait_ge(pT, u0 + u - 1)
                        n = keys[u % 2]
                        act.activation(prob[:, u % 2, 0:n], ssb[:, u % 2, 0:n], ACT.Exp, bias=nmax[:, u:u + 1],
                                       accum_out=rsum[:, u:u + 1]).then_inc(p_ready, 1)
                    if u >= 1:
                        v = u - 1
                        act.wait_ge(pT, u0 + v + 1)
                        if v >= 2:
                            act.wait_ge(o_ready, u0 + v - 1)
                        full = P * sum(m == P for m in tiles[v % 2])
                        src = acc_bank[2 + v % 2]
                        ins = act.activation(probT[:, v % 2, 0:full], src[:, 0:full], ACT.Copy)
                        if tiles[v % 2][-1] < P:
                            m = tiles[v % 2][-1]
                            ins = act.activation(probT[0:m, v % 2, full:full + P], src[0:m, full:full + P], ACT.Copy)
                        ins.then_inc(pT_copied, 1)
                        if v >= 4 and v % 4 == 0:
                            pair_done(v // 4 - 1)
                pair_done(units // 4 - 1)

            act.wait_ge(par_T, 1)
            act.activation(par[:, :], acc_bank[0][:, 0:PAR_N], ACT.Copy).then_inc(par_ready, 1)
            act.wait_ge(consts, 3)
            norm(N_NORM1, 0)
            for n in range(LOOKAHEAD):
                split(n)
            operand_hi(A_NORM1, 0)
            project(IN1, 20, 0)

            act.wait_ge(fl_x, 1)
            link(act.activation(lf[:, 1, :], lf[:, 0, :], ACT.Abs))
            link(act.activation(lf[:, 2, :], lf[:, 1, :], ACT.Exp, scale=-1.0))
            act.activation(lf[:, 3, :], lf[:, 2, :], ACT.Ln, bias=1.0).then_inc(fl_ln, 1)
            values(0, [((P, P, NMETA)[g // 2],
                        vtok[0:(P, P, NMETA)[g // 2], g // 2, (g % 2) * FOX_W:(g % 2 + 1) * FOX_W])
                       for g in range(6)])

            def fox_pair(pair):
                act.wait_ge(o_ready, 4 * pair + 4)
                act.activation(y[:, 2 + pair, :], gemm_bank[pair % 2][:, 0:SEQ], ACT.Copy).then_inc(o_copied, 1)
            attention(FOX_U, 0, FOX_N, FOX_TILES, fox_pair)

            for i in range(SB_HEADS + 1):
                if i < SB_HEADS:
                    act.wait_ge(z_ready, i + 1)
                    if i >= 1:
                        act.wait_ge(l_ready, i)
                    link(act.activation(sba[:, 0, :], acc_bank[i % 2][:, 0:SBW], ACT.Abs))
                    link(act.activation(sba[:, 1, :], sba[:, 0, :], ACT.Exp, scale=-1.0))
                    act.activation(sba[:, 2, :], sba[:, 1, :], ACT.Ln, bias=1.0).then_inc(z_ln, 1)
                if i >= 1:
                    act.wait_ge(r_masked, i)
                    if i >= 2:
                        act.wait_ge(sbo_ready, i - 1)
                    act.activation(sbp[:, :], sbr[:, :], ACT.Exp).then_inc(w_ready, 1)
            for pair in range(SB_HEADS // 2):
                act.wait_ge(sbo_ready, 2 * pair + 2)
                act.activation(y[:, 5 + pair, :], sbo[pair][:, 0:SEQ], ACT.Copy).then_inc(sbo_copied, 1)

            act.wait_ge(o_copied, 3)
            act.wait_ge(sbo_copied, 3)
            for j in range(6):
                act.activation(sq[:, j, NMETA:], y[:, 2 + j, :], ACT.Square).then_inc(hsq, 1)
            for j in range(3):
                act.wait_ge(hstat, 2 * j + 2)
                act.activation(sq[:, 2 * j:2 * j + 2, NMETA:],
                               acc_bank[j][:, :].rearrange("p (a b) -> p a b", a=2),
                               ACT.Sqrt, bias=eps[:, 0:1], scale=1.0 / HD).then_inc(hstd, 1)
            operand_hi(A_MIX1)
            residual_splits(OUT1)
            norm(N_NORM2)
            operand_hi(A_NORM2)

            def swiglu(f, n, q=0):
                act.wait_ge(slab_used, n + 1 + 12 * q)
                act.activation(hid[:, f % 2, :], gemm_bank[0][:, NMETA:T1], ACT.Silu).then_inc(gemm_evac, 1)
                split_ahead(n, 3 * q)
                act.wait_ge(gemm_evac, E_MLP1 + 2 * f + 2 + 8 * q)
                act.activation(hidhi[:, f % 2, :], hid2[:, f % 2, :], ACT.Copy).then_inc(hid_hi, 1)
                split_ahead(n + 1, 3 * q)
                if f >= 1:
                    split_ahead(n + 2, 3 * q)
            swiglu(0, MLP1)
            swiglu(1, MLP1 + 2)
            with act.Fori(0, (FF1 - 2) // 4) as it:
                for j in range(4):
                    swiglu(2 + j, MLP1 + 5 + 3 * j, it)
            split_ahead(MLP1 + 3 * FF1 - 1)

            norm(N_FINAL1)
            norm(N_MIX0)
            operand_hi(A_MIX0)
            project(IN2, 20)

            act.wait_ge(gemm_evac, E_IN2 + 20)
            act.activation(sq[:, 0:CONV_C, NMETA:], proj[:, CONV_C:2 * CONV_C, NMETA:], ACT.Sigmoid).then_inc(glu, 1)
            values(6, [(P, vtok[:, g, 0:512]) for g in range(2)])

            def moba_pair(pair):
                act.wait_ge(o_ready, FOX_U + 4 * pair + 4)
                act.activation(af[:, 4 + pair, NMETA:], gemm_bank[pair % 2][:, 0:SEQ], ACT.Copy).then_inc(af_ready, 1)
            attention(MOBA_U, FOX_U, MOBA_N, MOBA_TILES, moba_pair)

            for k in range(CONV_C):
                act.wait_ge(ln_dev, k + 1)
                act.activation(sq[:, k, NMETA:], cv[:, k, :], ACT.Square).then_inc(ln_sq, 1)
            act.wait_ge(ln_var, 1)
            act.activation(std[:, NMETA:], aux_bank[:, NMETA:T1], ACT.Sqrt, bias=eps[:, 0:1],
                           scale=1.0 / (CONV_C * P)).then_inc(ln_std, 1)
            for k in range(CONV_C):
                act.wait_ge(ln_norm, k + 1)
                act.activation(af[:, k, NMETA:], cv[:, k, :], ACT.Silu, scale=par[:, G_LNG + k:G_LNG + k + 1],
                               bias=par[:, G_LNB + k:G_LNB + k + 1]).then_inc(af_ready, 1)
            operand_hi(A_CAT2, order=CAT2_ORDER)
            residual_splits(OUT2)
            norm(N_MLP0)
            operand_hi(A_MLP0)

            def squared_relu(f, n, p0, q=0):
                act.wait_ge(slab_used, n + 1 + 4 * q)
                act.activation(hid[:, f % 2, :], gemm_bank[f % 2][:, NMETA:T1], ACT.Relu).then_inc(gemm_evac, 1)
                split_ahead(n, q)
                act.wait_ge(prod_ready, p0 + f + 1 + 2 * q)
                act.activation(hidhi[:, f % 2, :], hid2[:, f % 2, :], ACT.Copy).then_inc(hid_hi, 1)
                if f >= 1:
                    split_ahead(n + 1, q)

            def squared_relu_mlp(base, p0):
                squared_relu(0, base, p0)
                squared_relu(1, base + 1, p0)
                last = (FF2 - 2) // 2 - 1
                with act.Fori(0, last) as it:
                    for j in range(2):
                        squared_relu(2 + j, base + 3 + 2 * j, p0, it)
                for j in range(2):
                    squared_relu(2 + j, base + 3 + 2 * j, p0, last)
                split_ahead(base + 2 * FF2 - 1)
            squared_relu_mlp(MLP2, 0)
            norm(N_MIXC)
            operand_hi(A_MIXC)
            project(IN3, 16)

            link(act.activation(lam[:, 0, :], par[:, G_LAM:G_LAM + KC], ACT.Abs))
            link(act.activation(lam[:, 1, :], lam[:, 0, :], ACT.Exp, scale=-1.0))
            act.activation(lam[:, 2, :], lam[:, 1, :], ACT.Ln, bias=1.0).then_inc(lam_ln, 1)
            operand_hi(A_CONV)
            for g, (banks, b0) in enumerate(((lru_r, G_BR), (lru_i, G_BI))):
                for j in range(KC):
                    if j < KC - 2:
                        act.wait_ge(lru_sum, 3 * g + j // 2 + 1)
                    else:
                        act.wait_ge(slab_used, GATES + g + 1)
                    dst = sq[:, j, NMETA:] if g == 0 else y[:, j, :]
                    act.activation(dst, banks[j // 2][:, SEQ * (j % 2):SEQ * (j % 2) + SEQ], ACT.Sigmoid,
                                   bias=par[:, b0 + j:b0 + j + 1]).then_inc(lru_gate, 1)
                split_ahead(GATES + g)
            act.wait_ge(lam_ready, 1)
            act.wait_ge(lru_gate, KC)
            for j in range(KC):
                act.activation(proj[:, 8 + j, NMETA:], sq[:, j, NMETA:], ACT.Exp, scale=lam[:, 3, j:j + 1])\
                   .then_inc(lru_exp, 1)
                act.activation(t8[:, j, :], sq[:, j, NMETA:], ACT.Tanh, scale=lam[:, 3, j:j + 1]).then_inc(lru_exp, 1)
            for j in range(KC):
                act.wait_ge(lru_m2, j + 1)
                act.activation(sq[:, j, NMETA:], sq[:, j, NMETA:], ACT.Sqrt, scale=-1.0).then_inc(lru_root, 1)
            for j in range(KC):
                act.activation(proj[:, j, NMETA:], proj[:, j, NMETA:], ACT.Gelu_apprx_tanh).then_inc(lru_gelu, 1)
            operand_hi(A_LRU)
            residual_splits(OUT3)
            norm(N_MLPC)
            operand_hi(A_MLPC)
            squared_relu_mlp(MLP3, FF2)
            norm(N_FINAL2)
            for i in range(0, 4, 2):
                act.wait_ge(outT, i + 1)
                if i:
                    act.wait_ge(out_copied, i)
                act.activation(xtok[:, 0, 256 * i:256 * i + 512], acc_bank[i][:, :], ACT.Copy).then_inc(out_copied, 1)

        @block.vector
        def _(dve):
            chain = [0]

            def link(ins):
                chain[0] += 1
                ins.then_inc(dve_chain, 1)
                dve.wait_ge(dve_chain, chain[0])

            def split(n, q=0):
                dve.wait_ge(hi_done, n + 1 + R * q)
                dve.tensor_tensor(wlo[:, n % R, :, :], raw[:, n % R, :, :], whi[:, n % R, :, :].bitcast(F32),
                                  ALU.subtract).then_inc(lo_done, 1)

            def split_ahead(n, q=0):
                if n + R * (q if type(q) is int else 0) + LOOKAHEAD < NSLABS:
                    split(n + LOOKAHEAD, q)

            def operand_lo(s, i, k, lo=NMETA):
                dve.wait_ge(ahi_ready, KC * s + i + 1)
                dve.tensor_tensor(alo[:, k, lo:], af[:, k, lo:], ahi[:, k, lo:].bitcast(F32), ALU.subtract)\
                   .then_inc(alo_ready, 1)

            def norm_scale(i, lo=NMETA):
                dve.wait_ge(std_ready, i + 1)
                link(dve.reciprocal(rstd[:, lo:], std[:, lo:]))

            def norm(i, s, lo=NMETA):
                norm_scale(i, lo)
                for k in range(KC + 1):
                    if k < KC:
                        g = G_NORM[i] + k
                        dve.scalar_tensor_tensor(af[:, k, lo:], h[:, k, lo:], par[:, g:g + 1], rstd[:, lo:],
                                                 ALU.mult, ALU.mult).then_inc(af_ready, 1)
                    if k >= 1:
                        operand_lo(s, k - 1, k - 1, lo)

            def residual_add(n0):
                for j in range(KC):
                    dve.wait_ge(slab_used, n0 + j + 1)
                    dve.tensor_tensor(h[:, j, NMETA:], gemm_bank[j % 2][:, NMETA:T1], h[:, j, NMETA:], ALU.add)\
                       .then_inc(h_ready, 1)
                    split_ahead(n0 + j)

            def acc_add(m, n):
                for j in range(KC):
                    if j < KC - 2:
                        dve.wait_ge(acc_ready, 3 * m + j // 2 + 1)
                    else:
                        dve.wait_ge(slab_used, n + 1)
                    dve.tensor_tensor(h[:, j, NMETA:], acc_bank[j // 2][:, SEQ * (j % 2):SEQ * (j % 2) + SEQ],
                                      h[:, j, NMETA:], ALU.add).then_inc(h_ready, 1)

            def project_splits(n0, chunks):
                with dve.Fori(0, chunks // R) as it:
                    for j in range(R):
                        split_ahead(n0 + j, it)

            def attention(units, u0, keys, biased, filler):
                for u in range(units + 1):
                    if u < units:
                        n = keys[u % 2]
                        dve.wait_ge(s_ready, u0 + u + 1)
                        if u >= 2:
                            dve.wait_ge(p_ready, u0 + u - 1)
                        biased(u, ssb[:, u % 2, 0:n], acc_bank[u % 2][:, 0:n]).then_inc(s_biased, 1)
                        dve.wait_ge(s_biased, u0 + u + 1)
                        dve.tensor_reduce(nmax[:, u:u + 1], ssb[:, u % 2, 0:n], AX, ALU.max, negate=True)\
                           .then_inc(m_ready, 1)
                        filler(4)
                    if u >= 1:
                        v, n = u - 1, keys[(u - 1) % 2]
                        dve.wait_ge(p_ready, u0 + v + 1)
                        link(dve.reciprocal(rinv[:, v:v + 1], rsum[:, v:v + 1]))
                        dve.tensor_scalar(prob[:, v % 2, 0:n], prob[:, v % 2, 0:n], rinv[:, v:v + 1], None, ALU.mult)\
                           .then_inc(p_normed, 1)
                        filler(4)

            for k in range(KC):
                dve.wait_ge(xT, k + 1)
                dve.tensor_copy(h[:, k, :], gemm_bank[k % 2][:, 0:T1]).then_inc(h_ready, 1)
            dve.wait_ge(par_ready, 1)
            norm_scale(N_NORM1, 0)
            for n in range(LOOKAHEAD):
                split(n)
            for k in range(KC + 1):
                if k < KC:
                    dve.scalar_tensor_tensor(af[:, k, :], h[:, k, :], par[:, k:k + 1], rstd[:, :],
                                             ALU.mult, ALU.mult).then_inc(af_ready, 1)
                if k >= 1:
                    operand_lo(A_NORM1, k - 1, k - 1, 0)
            project_splits(IN1, 20)

            dve.wait_ge(small_loaded, 96)
            dve.wait_ge(fl_ready, 1)
            dve.tensor_scalar(lf[:, 0, :], aux_bank[0:FOX_HEADS, 0:T1], fbias[:, 0:1], None, ALU.add).then_inc(fl_x, 1)
            dve.wait_ge(gemm_evac, E_IN1 + 20)
            for c in (2, 11):
                dve.tensor_scalar(proj[:, c:c + 3, NMETA:], proj[:, c:c + 3, NMETA:], QSCALE, None, ALU.mult)\
                   .then_inc(q_scaled, 1)
            dve.wait_ge(fl_ln, 1)
            link(dve.scalar_tensor_tensor(lf[:, 1, :], lf[:, 0, :], 0.0, lf[:, 3, :], ALU.min, ALU.subtract))
            dve.wait_ge(consts, consts_done)
            dve.tensor_tensor_scan(cum[:, :], lf[:, 1, :], zero6[:, :], 0.0, ALU.add, ALU.add).then_inc(cum_ready, 1)

            u_ = proj[:, 0:2, :]
            link(dve.tensor_tensor(win[:, :, 1:], u_[:, :, 1:], u_[:, :, 0:T1 - 1], ALU.add))
            link(dve.tensor_tensor(win2[:, :, 3:], win[:, :, 3:], win[:, :, 1:T1 - 2], ALU.add))

            def window_mean(p0, c, buf, w):
                pr = slice(p0, p0 + HD)
                return dve.scalar_tensor_tensor(pd[pr, c, :], buf[pr, c, NMETA:], 1.0 / w, u_[pr, c, NMETA:],
                                                ALU.mult, ALU.subtract)
            window_mean(0, 0, win, 2)
            window_mean(HD, 0, win2, 4)
            link(dve.tensor_tensor(win[:, 1, 7:], win2[:, 1, 7:], win2[:, 1, 3:T1 - 4], ALU.add))
            window_mean(0, 1, win, 8)
            link(dve.tensor_tensor(win2[HD:P, 1, 15:], win[HD:P, 1, 15:], win[HD:P, 1, 7:T1 - 8], ALU.add))
            window_mean(HD, 1, win2, 16).then_inc(pool_d, 1)

            def fox_bias(u, dst, src):
                return dve.tensor_tensor(dst, src, fmask[:, u % 2, 0:FOX_N[u % 2]], ALU.add)
            attention(FOX_U, 0, FOX_N, fox_bias, lambda n: None)

            for i in range(SB_HEADS + 1):
                if i < SB_HEADS:
                    dve.wait_ge(z_ln, i + 1)
                    link(dve.scalar_tensor_tensor(sbs[:, :], acc_bank[i % 2][:, 0:SBW], 0.0, sba[:, 2, :],
                                                  ALU.max, ALU.add))
                    if i >= 1:
                        dve.wait_ge(r_ready, i)
                    dve.tensor_tensor(sbl[:, :], sbs[:, :], sbm[:, :], ALU.mult).then_inc(l_ready, 1)
                if i >= 1:
                    dve.wait_ge(r_ready, i)
                    if i >= 2:
                        dve.wait_ge(w_ready, i - 1)
                    dve.tensor_tensor(sbr[:, :], acc_bank[(i - 1) % 2][:, 0:SBW], sbneg[:, :], ALU.add)\
                       .then_inc(r_masked, 1)

            dve.wait_ge(pool_mixed, 1)
            for c in range(2):
                dve.tensor_scalar(af[:, c, NMETA:], stat_bank[:, SEQ * c:SEQ * c + SEQ],
                                  par[:, G_PSCALE + c:G_PSCALE + c + 1], None, ALU.mult).then_inc(af_ready, 1)
            for c in range(2):
                operand_lo(A_MIX1, c, c)
            for j in range(3):
                dve.wait_ge(hstd, j + 1)
                link(dve.reciprocal(sq[:, 2 * j:2 * j + 2, NMETA:], sq[:, 2 * j:2 * j + 2, NMETA:]))
                for k in (2 * j, 2 * j + 1):
                    dve.scalar_tensor_tensor(af[:, 2 + k, NMETA:], y[:, 2 + k, :], par[:, G_FOX + k:G_FOX + k + 1],
                                             sq[:, k, NMETA:], ALU.mult, ALU.mult).then_inc(af_ready, 1)
                for k in (2 * j, 2 * j + 1):
                    operand_lo(A_MIX1, 2 + k, 2 + k)
            residual_add(OUT1)
            norm(N_NORM2, A_NORM2)

            def swiglu(f, n, q=0):
                split_ahead(n, 3 * q)
                dve.wait_ge(gemm_evac, E_MLP1 + 2 * f + 1 + 8 * q)
                dve.wait_ge(slab_used, n + 2 + 12 * q)
                dve.tensor_tensor(hid2[:, f % 2, :], gemm_bank[1][:, NMETA:T1], hid[:, f % 2, :], ALU.mult)\
                   .then_inc(gemm_evac, 1)
                dve.wait_ge(hid_hi, f + 1 + 4 * q)
                dve.tensor_tensor(hidlo[:, f % 2, :], hid2[:, f % 2, :], hidhi[:, f % 2, :].bitcast(F32),
                                  ALU.subtract).then_inc(hid_lo, 1)
                split_ahead(n + 1, 3 * q)
                if f >= 1:
                    split_ahead(n + 2, 3 * q)
            swiglu(0, MLP1)
            swiglu(1, MLP1 + 2)
            with dve.Fori(0, (FF1 - 2) // 4) as it:
                for j in range(4):
                    swiglu(2 + j, MLP1 + 5 + 3 * j, it)
            split_ahead(MLP1 + 3 * FF1 - 1)
            acc_add(0, MLP1 + 3 * FF1 - 1)

            norm_scale(N_FINAL1)
            for k in range(KC):
                g = G_NORM[N_FINAL1] + k
                dve.scalar_tensor_tensor(h[:, k, NMETA:], h[:, k, NMETA:], par[:, g:g + 1], rstd[:, NMETA:],
                                         ALU.mult, ALU.mult).then_inc(h_ready, 1)
            norm(N_MIX0, A_MIX0)
            project_splits(IN2, 20)

            dve.wait_ge(gemm_evac, E_IN2 + 20)
            dve.tensor_scalar(proj[:, 8:12, NMETA:], proj[:, 8:12, NMETA:], QSCALE, None, ALU.mult).then_inc(q_scaled, 1)
            dve.wait_ge(glu, 1)
            link(dve.tensor_tensor(zpad[:, :, CONV_T - 1:], proj[:, 0:CONV_C, NMETA:], sq[:, 0:CONV_C, NMETA:], ALU.mult))
            taps = [(t, k) for t in range(CONV_T) for k in range(CONV_C)]
            at = [0]

            def conv_taps(n):
                for _ in range(n):
                    if at[0] == len(taps):
                        return
                    t, k = taps[at[0]]
                    w, src = par[:, G_CONVW + CONV_C * t + k:G_CONVW + CONV_C * t + k + 1], zpad[:, k, t:t + SEQ]
                    if t == 0:
                        ins = dve.tensor_scalar(cv[:, k, :], src, w, None, ALU.mult)
                    else:
                        dve.wait_ge(conv, at[0] + 1 - CONV_C)
                        ins = dve.scalar_tensor_tensor(cv[:, k, :], src, w, cv[:, k, :], ALU.mult, ALU.add)
                    ins.then_inc(conv, 1)
                    at[0] += 1

            def alibi_bias(u, dst, src):
                slope = 2.0 ** (-8.0 * (u // 2 + 1) / MOBA_HEADS)
                return dve.scalar_tensor_tensor(dst, dist[:, u % 2, 0:MOBA_N[u % 2]], -slope, src, ALU.mult, ALU.add)
            attention(MOBA_U, FOX_U, MOBA_N, alibi_bias, conv_taps)
            conv_taps(len(taps))

            dve.wait_ge(ln_mean, 1)
            for k in range(CONV_C):
                dve.scalar_tensor_tensor(cv[:, k, :], stat_bank[:, NMETA:T1], -1.0 / (CONV_C * P), cv[:, k, :],
                                         ALU.mult, ALU.add).then_inc(ln_dev, 1)
            dve.wait_ge(ln_std, 1)
            link(dve.reciprocal(rstd[:, NMETA:], std[:, NMETA:]))
            for k in range(CONV_C):
                dve.tensor_tensor(cv[:, k, :], cv[:, k, :], rstd[:, NMETA:], ALU.mult).then_inc(ln_norm, 1)
            for i, k in enumerate(CAT2_ORDER):
                operand_lo(A_CAT2, i, k)
            residual_add(OUT2)
            norm(N_MLP0, A_MLP0)

            def squared_relu(f, n, e0, m0, q=0):
                split_ahead(n, q)
                dve.wait_ge(gemm_evac, e0 + f + 1 + 2 * q)
                dve.tensor_tensor(hid2[:, f % 2, :], hid[:, f % 2, :], hid[:, f % 2, :], ALU.mult)\
                   .then_inc(prod_ready, 1)
                dve.wait_ge(hid_hi, m0 + f + 1 + 2 * q)
                dve.tensor_tensor(hidlo[:, f % 2, :], hid2[:, f % 2, :], hidhi[:, f % 2, :].bitcast(F32),
                                  ALU.subtract).then_inc(hid_lo, 1)
                if f >= 1:
                    split_ahead(n + 1, q)

            def squared_relu_mlp(base, e0, m0):
                squared_relu(0, base, e0, m0)
                squared_relu(1, base + 1, e0, m0)
                last = (FF2 - 2) // 2 - 1
                with dve.Fori(0, last) as it:
                    for j in range(2):
                        squared_relu(2 + j, base + 3 + 2 * j, e0, m0, it)
                for j in range(2):
                    squared_relu(2 + j, base + 3 + 2 * j, e0, m0, last)
                split_ahead(base + 2 * FF2 - 1)
            squared_relu_mlp(MLP2, E_MLP2, FF1)
            acc_add(1, MLP2 + 2 * FF2 - 1)
            norm(N_MIXC, A_MIXC)
            project_splits(IN3, 16)

            dve.wait_ge(lam_ln, 1)
            link(dve.tensor_scalar(lam[:, 0, :], par[:, G_LAM:G_LAM + KC], -1.0, 0.0, ALU.mult, ALU.max))
            link(dve.tensor_tensor(lam[:, 1, :], lam[:, 0, :], lam[:, 2, :], ALU.add))
            dve.tensor_scalar(lam[:, 3, :], lam[:, 1, :], -LRU_C, None, ALU.mult).then_inc(lam_ready, 1)
            dve.wait_ge(gemm_evac, E_IN3 + 16)
            link(dve.memset(proj[:, 8:16, NMETA - LRU_T + 1:NMETA], 0.0))
            for i, t in enumerate((LRU_T - 1, 0, 1, 2)):
                for k in range(KC):
                    w = par[:, G_CCONVW + KC * t + k:G_CCONVW + KC * t + k + 1]
                    src = proj[:, 8 + k, NMETA - LRU_T + 1 + t:NMETA - LRU_T + 1 + t + SEQ]
                    if i == 0:
                        ins = dve.tensor_scalar(af[:, k, NMETA:], src, w, par[:, G_CONVB + k:G_CONVB + k + 1],
                                                ALU.mult, ALU.add)
                    else:
                        dve.wait_ge(lconv, KC * (i - 1) + k + 1)
                        ins = dve.scalar_tensor_tensor(af[:, k, NMETA:], src, w, af[:, k, NMETA:], ALU.mult, ALU.add)
                    ins.then_inc(lconv if i < LRU_T - 1 else af_ready, 1)
            for k in range(KC):
                operand_lo(A_CONV, k, k)
            split_ahead(GATES)
            split_ahead(GATES + 1)
            for j in range(KC):
                dve.wait_ge(lru_exp, 2 * j + 2)
                link(dve.tensor_tensor(sq[:, j, NMETA:], proj[:, 8 + j, NMETA:], proj[:, 8 + j, NMETA:], ALU.mult))
                dve.scalar_tensor_tensor(sq[:, j, NMETA:], sq[:, j, NMETA:], 1.0, t8[:, j, :], ALU.add, ALU.mult)\
                   .then_inc(lru_m2, 1)
            for j in range(KC):
                dve.wait_ge(lru_gate, KC + j + 1)
                dve.tensor_tensor(y[:, j, :], y[:, j, :], af[:, j, NMETA:], ALU.mult).then_inc(lru_ix, 1)
            for j in range(KC):
                dve.wait_ge(lru_root, j + 1)
                dve.wait_ge(lru_ix, j + 1)
                link(dve.tensor_tensor(y[:, j, :], y[:, j, :], sq[:, j, NMETA:], ALU.mult))
                link(dve.tensor_tensor_scan(t8[:, j, :], proj[:, 8 + j, NMETA:], y[:, j, :], 0.0, ALU.mult, ALU.add))
                dve.wait_ge(lru_gelu, j + 1)
                dve.tensor_tensor(af[:, j, NMETA:], t8[:, j, :], proj[:, j, NMETA:], ALU.mult).then_inc(af_ready, 1)
                if j >= 1:
                    operand_lo(A_LRU, j - 1, j - 1)
            operand_lo(A_LRU, KC - 1, KC - 1)
            residual_add(OUT3)
            norm(N_MLPC, A_MLPC)
            squared_relu_mlp(MLP3, E_MLP3, FF1 + FF2)
            acc_add(2, MLP3 + 2 * FF2 - 1)
            norm_scale(N_FINAL2)
            for k in range(KC):
                g = G_NORM[N_FINAL2] + k
                dve.scalar_tensor_tensor(af[:, k, NMETA:], h[:, k, NMETA:], par[:, g:g + 1], rstd[:, NMETA:],
                                         ALU.mult, ALU.mult).then_inc(fin_ready, 1)
            for i in range(1, 4, 2):
                dve.wait_ge(outT, i + 1)
                dve.wait_ge(out_copied, i)
                dve.tensor_copy(xtok[:, 1, 256 * (i - 1):256 * (i - 1) + 512], acc_bank[i][:, :]).then_inc(out_copied, 1)

        @block.tensor
        def _(pe):
            def three(dst, n, j, xh, xl, start=False, stop=False):
                hi, lo = whi[:, n % R, j, :], wlo[:, n % R, j, :]
                pe.matmul(dst, hi, xh, start=start, stop=False, skip_group_check=True)
                pe.matmul(dst, hi, xl, start=False, stop=False, skip_group_check=True)
                return pe.matmul(dst, lo, xh, start=False, stop=stop, skip_group_check=True)

            def slab_ready(n, q=0):
                pe.wait_ge(lo_done, n + 1 + R * q)

            def chunk(n, b, q=0, s=None, lo=NMETA, order=range(KC)):
                slab_ready(n, q)
                for i, k in enumerate(order):
                    if s is not None:
                        pe.wait_ge(alo_ready, KC * s + i + 1)
                    ins = three(gemm_bank[b][:, lo:T1], n, k, ahi[:, k, lo:], alo[:, k, lo:], i == 0, i == KC - 1)
                ins.then_inc(slab_used, 1)

            def project(n0, e0, s, chunks, lo=NMETA, after_first=None):
                for j in range(R):
                    if j >= 2:
                        pe.wait_ge(gemm_evac, e0 + j - 1)
                    chunk(n0 + j, j % 2, s=s if j == 0 else None, lo=lo)
                if after_first:
                    after_first()
                with pe.Fori(1, chunks // R) as it:
                    for j in range(R):
                        pe.wait_ge(gemm_evac, it * R + e0 + j - 1)
                        chunk(n0 + j, j % 2, q=it, lo=lo)

            def residual(n0, norm_i, s, order=range(KC)):
                for j in range(KC):
                    if j >= 2:
                        pe.wait_ge(h_ready, KC * norm_i + j - 1)
                    chunk(n0 + j, j % 2, s=s if j == 0 else None, order=order)

            def stats(i, lo=NMETA):
                for k in range(KC):
                    pe.wait_ge(sq_ready, KC * i + k + 1)
                    ins = pe.matmul(stat_bank[:, lo:T1], ones[:, :], sq[:, k, lo:], start=(k == 0), stop=(k == KC - 1))
                ins.then_inc(stat_ready, 1)

            def down(f, n, m, q=0, first=False, last=False):
                pe.wait_ge(hid_lo, m + 1)
                slab_ready(n, q)
                for j in range(KC):
                    ins = three(acc_bank[j // 2][:, SEQ * (j % 2):SEQ * (j % 2) + SEQ], n, j,
                                hidhi[:, f % 2, :], hidlo[:, f % 2, :], start=first and j % 2 == 0, stop=last)
                    if last and j % 2 and j < KC - 1:
                        ins.then_inc(acc_ready, 1)
                ins.then_inc(slab_used, 1)

            def attention(units, u0, qc, kc, q0, keys, tiles, extra, pair_free):
                for u in range(units + 2):
                    if u < units:
                        hd, t = u // 2, u % 2
                        b = HD * (hd % 2)
                        if u >= 2:
                            pe.wait_ge(s_biased, u0 + u - 1)
                        n, dst = keys[t], acc_bank[t]
                        ins = pe.matmul(dst[:, 0:n], proj[b:b + HD, qc + hd // 2, NMETA + P * t:NMETA + P * t + P],
                                        proj[b:b + HD, kc + hd // 2, q0:q0 + n], start=True, stop=not extra)
                        if extra:
                            ins = extra(hd, t, dst[:, 0:n], n)
                        ins.then_inc(s_ready, 1)
                    if 1 <= u <= units:
                        v = u - 1
                        pe.wait_ge(p_normed, u0 + v + 1)
                        if v >= 2:
                            pe.wait_ge(pT_copied, u0 + v - 1)
                        c = 0
                        for m in tiles[v % 2]:
                            ins = pe.transpose(acc_bank[2 + v % 2][0:m, c:c + P], prob[:, v % 2, c:c + m], ident[:, :])
                            c += P
                        ins.then_inc(pT, 1)
                    if u >= 2:
                        v = u - 2
                        hd, t, pair = v // 2, v % 2, v // 4
                        b = HD * (hd % 2)
                        pe.wait_ge(pT_copied, u0 + v + 1)
                        if v % 4 == 0:
                            pair_free(pair)
                        for j, m in enumerate(tiles[t]):
                            ins = pe.matmul(gemm_bank[pair % 2][b:b + HD, P * t:P * t + P],
                                            vtok[0:m, j, HD * hd:HD * hd + HD], probT[0:m, t, P * j:P * j + P],
                                            start=(j == 0), stop=(j == len(tiles[t]) - 1))
                        ins.then_inc(o_ready, 1)

            pe.wait_ge(consts, 2)
            pe.wait_ge(x_loaded, 48)
            for k in range(KC):
                if k >= 2:
                    pe.wait_ge(h_ready, k - 1)
                ks = slice(P * k, P * k + P)
                pe.transpose(gemm_bank[k % 2][:, 0:NMETA], xmeta[:, ks], ident[0:NMETA, 0:NMETA])
                pe.transpose(gemm_bank[k % 2][:, NMETA:NMETA + P], xtok[:, 0, ks], ident[:, :])
                pe.transpose(gemm_bank[k % 2][:, NMETA + P:T1], xtok[:, 1, ks], ident[:, :]).then_inc(xT, 1)
            pe.wait_ge(par_loaded, 16 * 19)
            c = 0
            for j, r in enumerate((PAR_A, CONV_T * CONV_C, LRU_T * KC)):
                ins = pe.transpose(acc_bank[0][:, c:c + r], par_rows[0:r, j, :], ident[0:r, 0:r])
                c += r
            ins.then_inc(par_T, 1)
            stats(N_NORM1, 0)

            def forget_gates():
                pe.wait_ge(small_loaded, 96)
                for k in range(KC):
                    ins = pe.matmul(aux_bank[0:FOX_HEADS, 0:T1], wfl[:, k, :], af[:, k, :], start=(k == 0), stop=(k == KC - 1))
                ins.then_inc(fl_ready, 1)
            project(IN1, E_IN1, A_NORM1, 20, 0, forget_gates)

            pe.wait_ge(gemm_evac, E_IN1 + 20)
            for g in range(6):
                if g >= 2:
                    pe.wait_ge(v_ready, g - 1)
                tt, m = g // 2, (P, P, NMETA)[g // 2]
                for j in range(3):
                    ins = pe.transpose(acc_bank[2 + g % 2][0:m, P * j:P * j + P],
                                       proj[:, (8, 17)[g % 2] + j, P * tt:P * tt + m], ident[:, :])
                ins.then_inc(vT, 1)
            pe.wait_ge(consts, consts_done)
            pe.wait_ge(pool_d, 1)
            for g in range(4):
                b, c = HD * (g % 2), g // 2
                ins = pe.matmul(stat_bank[b:b + HD, SEQ * c:SEQ * c + SEQ], poolw[b:b + HD, c, :], pd[b:b + HD, c, :],
                                start=True, stop=True)
            ins.then_inc(pool_mixed, 1)

            pe.wait_ge(q_scaled, 2)
            pe.wait_ge(cum_ready, 1)
            pe.wait_ge(v_ready, 6)

            def forgetting(hd, t, dst, n):
                pe.matmul(dst, cum[:, NMETA + P * t:NMETA + P * t + P], sel[:, hd, 0:n], start=False, stop=False)
                return pe.matmul(dst, nsel[:, hd, :], cum[:, 0:n], start=False, stop=True)

            def fox_bank(pair):
                if pair >= 2:
                    pe.wait_ge(o_copied, pair - 1)
            attention(FOX_U, 0, 2, 5, 0, FOX_N, FOX_TILES, forgetting, fox_bank)

            pe.wait_ge(s_biased, FOX_U)
            pe.wait_ge(o_copied, 3)

            def sb_scores(i):
                b, ch = HD * (i % 2), i // 2
                if i >= 2:
                    pe.wait_ge(r_masked, i - 1)
                for j in range(3):
                    k0 = T1 * (14 + ch) + P * j
                    ins = pe.matmul(acc_bank[i % 2][:, SBC[j]:SBC[j] + SBN[j]], flat[b:b + HD, k0:k0 + P],
                                    proj[b:b + HD, 11 + ch, NMETA + SBQ[j]:T1], start=(j == 0), stop=False,
                                    skip_group_check=True)
                ins.then_inc(z_ready, 1)

            def sb_sums(i):
                pe.wait_ge(l_ready, i + 1)
                dst = acc_bank[i % 2]
                for a in range(3):
                    for j in range(a, 3):
                        m = P if j < 2 else NMETA
                        w = SBN[j]
                        c = SBC[a] + SBQ[j] - SBQ[a]
                        ins = pe.matmul(dst[:, c:c + w], (tri if a == j else ones)[0:m, :],
                                        sbl[0:m, SBC[j]:SBC[j] + w], start=False, stop=False, skip_group_check=True)
                ins.then_inc(r_ready, 1)

            def sb_values(i):
                pe.wait_ge(w_ready, i + 1)
                b = HD * (i % 2)
                for j in range(3):
                    m = P if j < 2 else NMETA
                    ins = pe.matmul(sbo[i // 2][b:b + HD, SBQ[j]:SEQ], vtok[0:m, j, FOX_W + HD * i:FOX_W + HD * i + HD],
                                    sbp[0:m, SBC[j]:SBC[j] + SBN[j]], start=(j == 0), stop=(j == 2),
                                    skip_group_check=True)
                ins.then_inc(sbo_ready, 1)
            sb_scores(0)
            for i in range(SB_HEADS + 1):
                if i + 1 < SB_HEADS:
                    sb_scores(i + 1)
                if i < SB_HEADS:
                    sb_sums(i)
                if i >= 1:
                    sb_values(i - 1)
            for j in range(6):
                pe.wait_ge(hsq, j + 1)
                pe.matmul(acc_bank[j // 2][:, SEQ * (j % 2):SEQ * (j % 2) + SEQ], block64[:, :], sq[:, j, NMETA:],
                          start=True, stop=True).then_inc(hstat, 1)
            residual(OUT1, N_NORM2, A_MIX1)
            stats(N_NORM2)

            def gate_up(f, n, q=0, s=None):
                if f >= 1:
                    pe.wait_ge(gemm_evac, E_MLP1 + 2 * f - 1 + 8 * q)
                chunk(n, 0, q=3 * q, s=s)
                if f >= 1:
                    pe.wait_ge(gemm_evac, E_MLP1 + 2 * f + 8 * q)
                chunk(n + 1, 1, q=3 * q)
            gate_up(0, MLP1, s=A_NORM2)
            gate_up(1, MLP1 + 2)
            down(0, MLP1 + 4, 0, first=True)
            with pe.Fori(0, (FF1 - 2) // 4) as it:
                for j in range(4):
                    gate_up(2 + j, MLP1 + 5 + 3 * j, it)
                    down(1 + j, MLP1 + 7 + 3 * j, it * 4 + 1 + j, q=it * 3)
            down(FF1 - 1, MLP1 + 3 * FF1 - 1, FF1 - 1, last=True)
            stats(N_FINAL1)
            stats(N_MIX0)

            project(IN2, E_IN2, A_MIX0, 20)
            pe.wait_ge(gemm_evac, E_IN2 + 20)
            for g in range(2):
                for j in range(4):
                    ins = pe.transpose(acc_bank[2 + g][:, P * j:P * j + P], proj[:, 16 + j, NMETA + P * g:NMETA + P * g + P],
                                       ident[:, :])
                ins.then_inc(vT, 1)
            pe.wait_ge(q_scaled, 3)
            pe.wait_ge(v_ready, 8)

            def moba_bank(pair):
                if pair >= 2:
                    pe.wait_ge(af_ready, KC * A_CAT2 + pair - 1)
            attention(MOBA_U, FOX_U, 8, 12, NMETA, MOBA_N, MOBA_TILES, None, moba_bank)
            pe.wait_ge(conv, CONV_T * CONV_C)
            for k in range(CONV_C):
                ins = pe.matmul(stat_bank[:, NMETA:T1], ones[:, :], cv[:, k, :], start=(k == 0), stop=(k == CONV_C - 1))
            ins.then_inc(ln_mean, 1)
            for k in range(CONV_C):
                pe.wait_ge(ln_sq, k + 1)
                ins = pe.matmul(aux_bank[:, NMETA:T1], ones[:, :], sq[:, k, NMETA:], start=(k == 0), stop=(k == CONV_C - 1))
            ins.then_inc(ln_var, 1)
            residual(OUT2, N_MLP0, A_CAT2, CAT2_ORDER)
            stats(N_MLP0)

            def squared_relu_mlp(base, e0, m0, s):
                chunk(base, 0, s=s)
                chunk(base + 1, 1)
                down(0, base + 2, m0, first=True)
                with pe.Fori(0, (FF2 - 2) // 2) as it:
                    for j in range(2):
                        pe.wait_ge(gemm_evac, it * 2 + e0 + j + 1)
                        chunk(base + 3 + 2 * j, j, q=it)
                        down(1 + j, base + 4 + 2 * j, it * 2 + m0 + 1 + j, q=it)
                down(FF2 - 1, base + 2 * FF2 - 1, m0 + FF2 - 1, last=True)
            squared_relu_mlp(MLP2, E_MLP2, FF1, A_MLP0)
            stats(N_MIXC)

            project(IN3, E_IN3, A_MIXC, 16)
            for g, banks in enumerate((lru_r, lru_i)):
                slab_ready(GATES + g)
                for j in range(KC):
                    pe.wait_ge(alo_ready, KC * A_CONV + j + 1)
                    ins = three(banks[j // 2][:, SEQ * (j % 2):SEQ * (j % 2) + SEQ], GATES + g, j,
                                ahi[:, j, NMETA:], alo[:, j, NMETA:], True, True)
                    if j % 2 and j < KC - 1:
                        ins.then_inc(lru_sum, 1)
                ins.then_inc(slab_used, 1)
            residual(OUT3, N_MLPC, A_LRU)
            stats(N_MLPC)
            squared_relu_mlp(MLP3, E_MLP3, FF1 + FF2, A_MLPC)
            stats(N_FINAL2)

            for i in range(4):
                for j in range(4):
                    k = 4 * (i // 2) + j
                    pe.wait_ge(fin_ready, k + 1)
                    t0 = NMETA + P * (i % 2)
                    ins = pe.transpose(acc_bank[i][:, P * j:P * j + P], af[:, k, t0:t0 + P], ident[:, :])
                ins.then_inc(outT, 1)


_OUT = ((1, SEQ, DM), "float32")


def kernel(**inputs):
    import numpy as _np
    import concourse.bacc as _bacc
    from concourse.bass_utils import run_bass_kernel_spmd as _run

    nc = _bacc.Bacc("TRN2", target_bir_lowering=False, num_devices=1)
    arrays, args = {}, {}
    for name, value in inputs.items():
        a = _np.ascontiguousarray(value)
        arrays[f"in_{name}"] = a
        args[name] = nc.dram_tensor(f"in_{name}", a.shape, mybir.dt.from_np(a.dtype), kind="ExternalInput").ap()
    out = nc.dram_tensor("out", _OUT[0], F32, kind="ExternalOutput").ap()
    build(nc, args, out)
    r = _run(nc, [arrays], core_ids=[0])
    return r.results[0]["out"]
```

```python
from contextlib import ExitStack

import concourse.bass as bass
from concourse import mybir

F32 = mybir.dt.float32
F32R = mybir.dt.float32r
ALU = mybir.AluOpType
ACT = mybir.ActivationFunctionType
AX = mybir.AxisListType.X

P = 128
DM = 1024
KC = DM // P
SEQ = 256
NMETA = 16
T1 = NMETA + SEQ
EPS = 1e-6
BIG = 1.0e30

FOX_HEADS = SB_HEADS = 6
HD = 64
QSCALE = HD ** -0.5
POOL_W = 256
FOX_W = FOX_HEADS * HD
MOBA_HEADS = 8
CONV_T = 31
CONV_C = 4
CONV_D = 2
LRU_T = 4
LRU_C = 8.0

FF1 = 2816 // P
FF2 = 4096 // P

R = 4
LOOKAHEAD = R - 1

IN1 = 0
OUT1 = IN1 + 21
MLP1 = OUT1 + KC
IN2 = MLP1 + 3 * FF1
OUT2 = IN2 + 20
MLP2 = OUT2 + KC
IN3 = MLP2 + 2 * FF2
OUT3 = IN3 + 16
MLP3 = OUT3 + KC
NSLABS = MLP3 + 2 * FF2
QF, KF, VF, PU, QS, KS, VS = 0, 3, 6, 9, 11, 14, 17
FOX_READY = 10
OUT2_ORDER = (4, 5, 6, 7, 0, 1, 2, 3)
IN3_ORDER = tuple(range(8, 16)) + (0, 1, "r", 2, 3, "i", 4, 5, 6, 7)

E_IN1 = 0
E_MLP1 = E_IN1 + 21
E_IN2 = E_MLP1 + 2 * FF1
E_MLP2 = E_IN2 + 20
E_IN3 = E_MLP2 + FF2
E_MLP3 = E_IN3 + 16

(ACC_OUT1, ACC_MLP1, ACC_OUT2, ACC_MLP2, ACC_OUT3, ACC_MLP3) = range(6)
(A_NORM1, A_MIX1, A_NORM2, A_MIX0, A_CAT2, A_MLP0, A_MIXC, A_LRU, A_MLPC) = range(9)
(F_MIX1, F_CAT2, F_CONV, F_LRU) = range(4)
(N_NORM1, N_NORM2, N_MIX0, N_MLP0, N_MIXC, N_MLPC, N_FINAL) = range(7)
SQ0 = (0, 8, 16, 32, 40, 48, 56)
ST0 = (0, 1, 2, 4, 5, 6, 7)

PAR = (("norm1", KC), ("norm2", KC), ("final_norm", KC), ("mix_norm_2", 2 * KC), ("mlp_norm_2", 2 * KC),
       ("final_norm_2", KC), ("c_conv_b_2", KC), ("c_b_r_2", KC), ("c_b_i_2", KC), ("c_lambda_2", KC),
       ("pool_scale", 2), ("fox_out_gain", 3), ("sb_out_gain", 3), ("ab_ln_g_2", CONV_C), ("ab_ln_b_2", CONV_C),
       ("ab_conv_w_2", CONV_T * CONV_C), ("c_conv_w_2", LRU_T * KC))
COL = {name: sum(n for _, n in PAR[:i]) for i, (name, _) in enumerate(PAR)}
PAR_N = sum(n for _, n in PAR)
G_PROD = PAR_N
GAIN = {N_NORM1: COL["norm1"], N_NORM2: COL["norm2"], N_MIX0: G_PROD, N_MLP0: COL["mlp_norm_2"],
        N_MIXC: COL["mix_norm_2"] + KC, N_MLPC: COL["mlp_norm_2"] + KC, N_FINAL: COL["final_norm_2"]}

SBQ = (0, 112, 240)
SBC = (0, 256, 400)
SBN = (256, 144, 16)
SBW = 416

FOX_U = 2 * FOX_HEADS
MOBA_U = 2 * MOBA_HEADS
FOX_N = (NMETA + P, NMETA + SEQ)
FOX_TILES = ((P, NMETA), (P, P, NMETA))
MOBA_N = (P, 2 * P)
MOBA_TILES = ((P,), (P, P))


def build(nc, slabs, xT, par_in, fbias_in, poolw_in, gatew_in, out):
    with ExitStack() as ctx:
        def sb(name, shape, dt=F32):
            return ctx.enter_context(nc.sbuf_tensor(name, shape, dt))

        def sem(name):
            return ctx.enter_context(nc.semaphore(name))

        bank = [ctx.enter_context(nc.psum_tensor(f"bank{i}", [P, 512], F32)) for i in range(8)]
        gemm_bank = bank[0:2]
        acc_bank = bank[2:6]
        stat_bank = bank[6]
        aux_bank = bank[7]

        raw = sb("raw", [P, R, KC, P])
        whi = sb("whi", [P, R, KC, P], F32R)
        wlo = sb("wlo", [P, R, KC, P], F32R)
        h = sb("h", [P, KC, T1])
        af = sb("af", [P, KC, SEQ])
        ahi = sb("ahi", [P, KC, T1], F32R)
        alo = sb("alo", [P, KC, T1], F32R)
        sq = sb("sq", [P, KC, T1])
        std = sb("std", [P, T1])
        rstd = sb("rstd", [P, T1])
        r1 = sb("r1", [P, SEQ])
        proj = sb("proj", [P, 20, T1])
        hid = sb("hid", [P, 2, SEQ])
        hid2 = sb("hid2", [P, 2, SEQ])
        hidhi = sb("hidhi", [P, 2, SEQ], F32R)
        hidlo = sb("hidlo", [P, 2, SEQ], F32R)
        par = sb("par", [P, PAR_N + KC])
        fbias = sb("fbias", [FOX_HEADS, 1])
        poolw = sb("poolw", [P, 2, HD])
        ident = sb("ident", [P, P])
        ones = sb("ones", [P, P])
        block64 = sb("block64", [P, P])
        tri = sb("tri", [P, P])
        eps = sb("eps", [P, 1])
        zero6 = sb("zero6", [FOX_HEADS, T1])
        sel = sb("sel", [FOX_HEADS, FOX_HEADS, T1])
        nsel = sb("nsel", [FOX_HEADS, FOX_HEADS, P])
        fmask = sb("fmask", [P, 2, T1])
        sbneg = sb("sbneg", [P, SBW])
        sbm = sb("sbm", [P, SBW])
        dist = sb("dist", [P, 2, SEQ])
        lf = sb("lf", [FOX_HEADS, 5, T1])
        cum = sb("cum", [FOX_HEADS, T1])
        vtok = sb("vtok", [P, 3, 2 * FOX_W])
        win = sb("win", [P, 2, T1])
        win2 = sb("win2", [P, 2, T1])
        pd = sb("pd", [P, 2, SEQ])
        ssb = sb("ssb", [P, 2, T1])
        nmax = sb("nmax", [P, 16])
        rsum = sb("rsum", [P, 16])
        rinv = sb("rinv", [P, 16])
        prob = sb("prob", [P, 2, T1])
        hidg = ssb[:, :, 0:SEQ]
        hidu = prob[:, :, 0:SEQ]
        probT = sb("probT", [P, 2, 3 * P])
        y = sb("y", [P, KC, SEQ])
        sba = sb("sba", [P, 3, SBW])
        sbs = sb("sbs", [P, SBW])
        sbl = sb("sbl", [P, SBW])
        sbr = sb("sbr", [P, SBW])
        sbp = sb("sbp", [P, SBW])
        zpad = sb("zpad", [P, CONV_C, CONV_T - 1 + SEQ])
        t8 = sb("t8", [P, KC, SEQ])
        cv = t8[:, 0:CONV_C, :]
        cpr = t8[:, CONV_C:KC, :]
        lam = sb("lam", [P, 4, KC])

        raw_loaded = [sem(f"raw_loaded{s}") for s in range(R)]
        hi_done, lo_done, slab_used = sem("hi_done"), sem("lo_done"), sem("slab_used")
        gemm_evac, acc_ready, prod_ready = sem("gemm_evac"), sem("acc_ready"), sem("prod_ready")
        x_loaded = [sem(f"x_loaded{i}") for i in range(KC // 2)]
        par_loaded, small_loaded = sem("par_loaded"), sem("small_loaded")
        consts, gprod = sem("consts"), sem("gprod")
        h_ready, h_final = sem("h_ready"), sem("h_final")
        sq_ready, sum_ready, stat_ready, std_ready = sem("sq_ready"), sem("sum_ready"), sem("stat_ready"), sem("std_ready")
        var2_ready = sem("var2_ready")
        af_ready, ahi_ready, alo_ready = sem("af_ready"), sem("ahi_ready"), sem("alo_ready")
        act_hid, hid_hi, hid_lo = sem("act_hid"), sem("hid_hi"), sem("hid_lo")
        fl_x, fl_ln, cum_ready = sem("fl_x"), sem("fl_ln"), sem("cum_ready")
        vT, v_ready = sem("vT"), sem("v_ready")
        s_ready, s_biased, m_ready, p_ready = sem("s_ready"), sem("s_biased"), sem("m_ready"), sem("p_ready")
        p_normed, pT, pT_copied, o_ready = sem("p_normed"), sem("pT"), sem("pT_copied"), sem("o_ready")
        o_copied = sem("o_copied")
        z_ready, z_ln, l_ready, r_ready = sem("z_ready"), sem("z_ln"), sem("l_ready"), sem("r_ready")
        r_masked, w_ready, sbo_ready, sbo_copied = sem("r_masked"), sem("w_ready"), sem("sbo_ready"), sem("sbo_copied")
        pool_d, pool_mixed = sem("pool_d"), sem("pool_mixed")
        hsq, hstat, hstd = sem("hsq"), sem("hstat"), sem("hstd")
        glu, z_pad, conv, cprod, pconv = sem("glu"), sem("z_pad"), sem("conv"), sem("cprod"), sem("pconv")
        ln_mean, ln_dev, ln_sq, ln_var = sem("ln_mean"), sem("ln_dev"), sem("ln_sq"), sem("ln_var")
        ln_std, ln_norm = sem("ln_std"), sem("ln_norm")
        gatew_loaded = sem("gatew_loaded")
        lam_ln, lam_ready, tap0 = sem("lam_ln"), sem("lam_ready"), sem("tap0")
        lru_sum, lru_gate, lru_exp, lru_aa, lru_m2 = sem("lru_sum"), sem("lru_gate"), sem("lru_exp"), sem("lru_aa"), sem("lru_m2")
        lru_root, lru_gelu, lru_ix, pad0 = sem("lru_root"), sem("lru_gelu"), sem("lru_ix"), sem("pad0")
        dve_chain, act_chain, pool_chain = sem("dve_chain"), sem("act_chain"), sem("pool_chain")
        fin_ready, stored = sem("fin_ready"), sem("stored")

        gatew = vtok[:, :, :].rearrange("p a b -> p (a b)")[:, 0:2 * DM].rearrange("p (g c t) -> p g c t", g=2, c=KC)
        flat = proj[:, :, :].rearrange("p c t -> p (c t)")
        hsum = (gemm_bank[1], stat_bank)
        consts_done = 16

        def half(b, j):
            return b[:, SEQ * (j % 2):SEQ * (j % 2) + SEQ]

        block = ctx.enter_context(nc.Block())

        @block.sync
        def _(sp):
            for c in range(0, KC, 2):
                sp.dma_start(h[:, c:c + 2, :], xT[:, c:c + 2, :]).then_inc(x_loaded[c // 2], 16)
            for s in range(R):
                sp.dma_start(raw[:, s, :, :], slabs[s]).then_inc(raw_loaded[s], 16)
            with sp.Fori(1, NSLABS // R) as it:
                for s in range(R):
                    sp.wait_ge(lo_done, it * R + (s + 1 - R))
                    sp.dma_start(raw[:, s, :, :], slabs[it * R + s]).then_inc(raw_loaded[s], 16)
            for n in range(NSLABS // R * R, NSLABS):
                sp.wait_ge(lo_done, n + 1 - R)
                sp.dma_start(raw[:, n % R, :, :], slabs[n]).then_inc(raw_loaded[n % R], 16)
            for c in range(0, KC, 2):
                sp.wait_ge(fin_ready, c + 2)
                sp.dma_start(out[:, c:c + 2, :], y[:, c:c + 2, :]).then_inc(stored, 16)
            sp.wait_ge(stored, 16 * KC // 2)

        @block.gpsimd
        def _(pool):
            n = [0]

            def step(ins):
                n[0] += 1
                ins.then_inc(pool_chain, 1)
                pool.wait_ge(pool_chain, n[0])

            def select(buf, op, fill, base, pattern, cm):
                pool.affine_select(out=buf, in_=buf, compare_op=op, fill=fill, base=base,
                                   pattern=pattern, channel_multiplier=cm).then_inc(consts, 1)

            def pair_sums(i, buf, s0, lo=NMETA):
                for j in range(KC // 2):
                    pool.wait_ge(sq_ready, s0 + 2 * j + 2)
                    a, b = buf[:, 2 * j, lo:], buf[:, 2 * j + 1, lo:]
                    pool.tensor_tensor(a, a, b, ALU.add).then_inc(sum_ready, 1)

            pool.memset(ones[:, :], 1.0).then_inc(consts, 1)
            pool.memset(eps[:, :], EPS).then_inc(consts, 1)
            pair_sums(N_NORM1, sq, SQ0[N_NORM1], 0)
            step(pool.memset(ident[:, :], 0.0))
            select(ident[:, :], ALU.not_equal, 1.0, 0, [[-1, P]], 1)
            step(pool.memset(sel[:, :, :], 0.0))
            select(sel[:, :, :], ALU.not_equal, 1.0, 0, [[-1, FOX_HEADS], [0, T1]], 1)
            step(pool.memset(nsel[:, :, :], 0.0))
            select(nsel[:, :, :], ALU.not_equal, -1.0, 0, [[-1, FOX_HEADS], [0, P]], 1)
            step(pool.memset(block64[:, :], 0.0))
            step(pool.memset(block64[0:HD, 0:HD], 1.0))
            step(pool.memset(block64[HD:P, HD:P], 1.0))
            pool.memset(zero6[:, :], 0.0).then_inc(consts, 1)
            step(pool.memset(tri[:, :], 1.0))
            select(tri[:, :], ALU.is_ge, 0.0, 0, [[-1, P]], 1)
            step(pool.memset(fmask[:, :, :], 0.0))
            select(fmask[:, :, :], ALU.is_ge, -BIG, NMETA, [[P, 2], [-1, T1]], 1)
            step(pool.memset(sbneg[:, :], 0.0))
            step(pool.memset(sbm[:, :], -1.0))
            for i in range(3):
                for buf, fill in ((sbneg, -BIG), (sbm, 0.0)):
                    select(buf[:, SBC[i]:SBC[i] + SBN[i]], ALU.is_gt, fill, NMETA + SBQ[i] - P * i,
                           [[1, SBN[i]]], -1)
            step(pool.iota(dist[:, :, :], pattern=[[P, 2], [-1, SEQ]], base=0, channel_multiplier=1,
                           allow_small_or_imprecise_dtypes=True))
            select(dist[:, :, :], ALU.is_ge, BIG, 0, [[P, 2], [-1, SEQ]], 1)
            pool.memset(zpad[:, :, 0:CONV_T - 1], 0.0).then_inc(consts, 1)
            pool.wait_ge(gemm_evac, E_IN1 + 1 + PU + 2)
            u_ = proj[:, PU:PU + 2, :]
            step(pool.tensor_tensor(win[:, :, 1:], u_[:, :, 1:], u_[:, :, 0:T1 - 1], ALU.add))
            step(pool.tensor_tensor(win2[:, :, 3:], win[:, :, 3:], win[:, :, 1:T1 - 2], ALU.add))
            step(pool.tensor_tensor(win[:, 1, 7:], win2[:, 1, 7:], win2[:, 1, 3:T1 - 4], ALU.add))
            pool.tensor_tensor(win2[:, 1, 15:], win[:, 1, 15:], win[:, 1, 7:T1 - 8], ALU.add).then_inc(pool_d, 1)

            pair_sums(N_NORM2, sq, SQ0[N_NORM2])
            pair_sums(N_MIX0, sq, SQ0[N_MIX0])
            pair_sums(N_MIX0, t8[:, :, :], SQ0[N_MIX0] + KC, 0)
            for k in range(CONV_C):
                pool.wait_ge(glu, k + 1)
                pool.tensor_tensor(zpad[:, k, CONV_T - 1:], proj[:, k, NMETA:], sq[:, k, NMETA:], ALU.mult).then_inc(z_pad, 1)
            m = CONV_C - CONV_D
            for i in range(m, m * CONV_T):
                k = CONV_D + i % m
                pool.wait_ge(cprod, i + 1)
                if i >= 2 * m:
                    pool.wait_ge(pconv, i + 1 - 2 * m)
                pool.tensor_tensor(cv[:, k, :], cv[:, k, :], cpr[:, i % 4, :], ALU.add).then_inc(pconv, 1)
            pool.wait_ge(o_ready, FOX_U + MOBA_U)
            for g in range(2):
                pool.dma_start(gatew[:, g, :, :], gatew_in[g]).then_inc(gatew_loaded, 16)
            pair_sums(N_MLP0, sq, SQ0[N_MLP0])
            pair_sums(N_MIXC, sq, SQ0[N_MIXC])
            for j in range(KC):
                pool.wait_ge(lru_exp, 2 * j + 2)
                pool.tensor_tensor(sq[:, j, NMETA:], proj[:, 8 + j, NMETA:], proj[:, 8 + j, NMETA:], ALU.mult).then_inc(lru_aa, 1)
            for j in range(KC):
                pool.wait_ge(lru_gate, KC + j + 1)
                pool.tensor_tensor(y[:, j, :], y[:, j, :], af[:, j, :], ALU.mult).then_inc(lru_ix, 1)
            pair_sums(N_MLPC, sq, SQ0[N_MLPC])
            pair_sums(N_FINAL, sq, SQ0[N_FINAL])

        @block.scalar
        def _(act):
            chain = [0]

            def link(ins):
                chain[0] += 1
                ins.then_inc(act_chain, 1)
                act.wait_ge(act_chain, chain[0])

            act.dma_start(par[:, 0:PAR_N], par_in).then_inc(par_loaded, 16)
            act.dma_start(fbias[:, :], fbias_in).then_inc(small_loaded, 16)
            act.dma_start(poolw[:, :, :], poolw_in).then_inc(small_loaded, 16)

            def split(n, q=0):
                act.wait_ge(raw_loaded[n % R], 16 * (n // R + 1 + q))
                if n >= R:
                    act.wait_ge(slab_used, n + R * q - R + 1)
                act.activation(whi[:, n % R, :, :], raw[:, n % R, :, :], ACT.Copy).then_inc(hi_done, 1)

            def split_ahead(n, q=0):
                if n + R * (q if type(q) is int else 0) + LOOKAHEAD < NSLABS:
                    split(n + LOOKAHEAD, q)

            def residual_hi(i, lo=NMETA):
                for k in range(KC):
                    if i == N_NORM1:
                        act.wait_ge(x_loaded[k // 2], 16)
                    else:
                        act.wait_ge(h_ready, KC * (i - 1) + k + 1)
                    if i < N_FINAL:
                        g = GAIN[i] + k
                        act.activation(ahi[:, k, lo:], h[:, k, lo:], ACT.Copy, scale=par[:, g:g + 1]).then_inc(ahi_ready, 1)
                    act.activation(sq[:, k, lo:], h[:, k, lo:], ACT.Square).then_inc(sq_ready, 1)

            def root(i, src, lo=NMETA):
                act.wait_ge(stat_ready, i + 1)
                act.activation(std[:, lo:], src, ACT.Sqrt, bias=eps[:, 0:1], scale=1.0 / DM).then_inc(std_ready, 1)

            def operand_hi(s, f, k):
                act.wait_ge(af_ready, KC * f + k + 1)
                act.activation(ahi[:, k, NMETA:], af[:, k, :], ACT.Copy).then_inc(ahi_ready, 1)

            def values(g, m, dst, src):
                act.wait_ge(vT, g + 1)
                act.activation(dst, src[0:m, 0:dst.shape[1]], ACT.Copy).then_inc(v_ready, 1)

            def softmax_step(u, units, u0, keys, tiles, t_banks):
                if u < units:
                    act.wait_ge(m_ready, u0 + u + 1)
                    if u >= 2:
                        act.wait_ge(pT, u0 + u - 1)
                    n = keys[u % 2]
                    act.activation(prob[:, u % 2, 0:n], ssb[:, u % 2, 0:n], ACT.Exp, bias=nmax[:, u:u + 1],
                                   accum_out=rsum[:, u:u + 1]).then_inc(p_ready, 1)
                if 1 <= u <= units:
                    v = u - 1
                    act.wait_ge(pT, u0 + v + 1)
                    if v >= 2:
                        act.wait_ge(o_ready, u0 + v - 1)
                    full = P * sum(m == P for m in tiles[v % 2])
                    src = t_banks[v % len(t_banks)]
                    ins = act.activation(probT[:, v % 2, 0:full], src[:, 0:full], ACT.Copy)
                    if tiles[v % 2][-1] < P:
                        m = tiles[v % 2][-1]
                        ins = act.activation(probT[0:m, v % 2, full:full + P], src[0:m, full:full + P], ACT.Copy)
                    ins.then_inc(pT_copied, 1)

            act.wait_ge(par_loaded, 16)
            residual_hi(N_NORM1, 0)
            for n in range(LOOKAHEAD):
                split(n)
            act.wait_ge(consts, 2)
            root(N_NORM1, stat_bank[:, 0:T1], 0)
            for n in range(IN1, IN1 + FOX_READY):
                split_ahead(n)
                if n == IN1 + 2:
                    act.wait_ge(fl_x, 1)
                    link(act.activation(lf[:, 1, :], lf[:, 0, :], ACT.Abs))
                    link(act.activation(lf[:, 2, :], lf[:, 1, :], ACT.Exp, scale=-1.0))
                    act.activation(lf[:, 3, :], lf[:, 2, :], ACT.Ln, bias=1.0).then_inc(fl_ln, 1)
            split_ahead(IN1 + FOX_READY)
            for g in range(3):
                m = (P, P, NMETA)[g]
                values(g, m, vtok[0:m, g, 0:FOX_W], acc_bank[2 + g % 2])

            for u in range(FOX_U + 2):
                softmax_step(u, FOX_U, 0, FOX_N, FOX_TILES, acc_bank[2:4])
                if u < 10:
                    split_ahead(IN1 + FOX_READY + 1 + u)
                if u >= 5 and u % 4 == 1:
                    pair = u // 4 - 1
                    act.wait_ge(o_ready, 4 * pair + 4)
                    act.activation(y[:, 2 + pair, :], (stat_bank, aux_bank)[pair % 2][:, 0:SEQ], ACT.Copy).then_inc(o_copied, 1)
                    act.wait_ge(o_copied, pair + 1)
                    act.activation(sq[:, pair, NMETA:], y[:, 2 + pair, :], ACT.Square).then_inc(hsq, 1)
            for g in range(3, 6):
                m = (P, P, NMETA)[g - 3]
                values(g, m, vtok[0:m, g - 3, FOX_W:2 * FOX_W], acc_bank[2 + g % 2])
            act.wait_ge(hstat, 3)
            act.activation(sq[:, 0:2, NMETA:], acc_bank[0][:, :].rearrange("p (a b) -> p a b", a=2),
                           ACT.Sqrt, bias=eps[:, 0:1], scale=1.0 / HD).then_inc(hstd, 1)
            act.activation(sq[:, 2, NMETA:], acc_bank[1][:, 0:SEQ], ACT.Sqrt, bias=eps[:, 0:1], scale=1.0 / HD).then_inc(hstd, 1)

            zb = (stat_bank, aux_bank)
            for i in range(SB_HEADS + 2):
                if i < SB_HEADS:
                    act.wait_ge(z_ready, i + 1)
                    if i >= 1:
                        act.wait_ge(l_ready, i)
                    link(act.activation(sba[:, 0, :], zb[i % 2][:, 0:SBW], ACT.Abs))
                    link(act.activation(sba[:, 1, :], sba[:, 0, :], ACT.Exp, scale=-1.0))
                    act.activation(sba[:, 2, :], sba[:, 1, :], ACT.Ln, bias=1.0).then_inc(z_ln, 1)
                if i < 5:
                    operand_hi(A_MIX1, F_MIX1, i)
                    if i:
                        split_ahead(OUT1 + i - 1)
                if i >= 3 and i % 2:
                    pair = (i - 3) // 2
                    act.wait_ge(sbo_ready, 2 * pair + 2)
                    act.activation(y[:, 5 + pair, :], gemm_bank[0][:, 0:SEQ], ACT.Copy).then_inc(sbo_copied, 1)
                    act.wait_ge(sbo_copied, pair + 1)
                    act.activation(sq[:, 3 + pair, NMETA:], y[:, 5 + pair, :], ACT.Square).then_inc(hsq, 1)
                if 1 <= i <= SB_HEADS:
                    act.wait_ge(r_masked, i)
                    if i >= 2:
                        act.wait_ge(sbo_ready, i - 1)
                    act.activation(sbp[:, :], sbr[:, :], ACT.Exp).then_inc(w_ready, 1)
            split_ahead(OUT1 + 4)
            act.wait_ge(hstat, 6)
            act.activation(sq[:, 3:5, NMETA:], hsum[0][:, :].rearrange("p (a b) -> p a b", a=2),
                           ACT.Sqrt, bias=eps[:, 0:1], scale=1.0 / HD).then_inc(hstd, 1)
            act.activation(sq[:, 5, NMETA:], hsum[1][:, 0:SEQ], ACT.Sqrt, bias=eps[:, 0:1], scale=1.0 / HD).then_inc(hstd, 1)
            for i in range(5, KC):
                operand_hi(A_MIX1, F_MIX1, i)
            for n in range(OUT1 + 5, MLP1):
                split_ahead(n)
            residual_hi(N_NORM2)
            root(N_NORM2, stat_bank[:, 0:SEQ])

            def swiglu(f, n, q=0):
                split_ahead(n, 3 * q)
                act.wait_ge(gemm_evac, E_MLP1 + 2 * f + 1 + 8 * q)
                act.activation(hid[:, f % 2, :], hidg[:, f % 2, :], ACT.Silu).then_inc(act_hid, 1)
                act.wait_ge(prod_ready, f + 1 + 4 * q)
                act.activation(hidhi[:, f % 2, :], hid2[:, f % 2, :], ACT.Copy).then_inc(hid_hi, 1)
                split_ahead(n + 1, 3 * q)
                if f >= 1:
                    split_ahead(n + 2, 3 * q)
            swiglu(0, MLP1)
            swiglu(1, MLP1 + 2)
            with act.Fori(0, (FF1 - 2) // 4) as it:
                for j in range(4):
                    swiglu(2 + j, MLP1 + 5 + 3 * j, it)
            split_ahead(MLP1 + 3 * FF1 - 1)

            act.wait_ge(gprod, 1)
            residual_hi(N_MIX0)
            for k in range(KC):
                g = COL["final_norm"] + k
                act.activation(t8[:, k, :], h[:, k, NMETA:], ACT.Square, scale=par[:, g:g + 1]).then_inc(sq_ready, 1)
            act.wait_ge(stat_ready, N_MIX0 + 1)
            act.activation(std[:, NMETA:], half(stat_bank, 0), ACT.Sqrt, bias=eps[:, 0:1], scale=1.0 / DM).then_inc(std_ready, 1)
            act.wait_ge(var2_ready, 1)
            act.activation(std[:, NMETA:], std[:, NMETA:], ACT.Sqrt, bias=eps[:, 0:1], scale=1.0 / DM).then_inc(std_ready, 1)

            m = CONV_C - CONV_D
            done = [0]

            def conv_products(count):
                for _ in range(count):
                    i = done[0]
                    if i == m * CONV_T:
                        return
                    t, k = i // m, CONV_D + i % m
                    act.wait_ge(z_pad, k + 1)
                    if i >= m + 4:
                        act.wait_ge(pconv, i - 4 - m + 1)
                    dst = cv[:, k, :] if t == 0 else cpr[:, i % 4, :]
                    w = COL["ab_conv_w_2"] + CONV_C * t + k
                    act.activation(dst, zpad[:, k, t:t + SEQ], ACT.Copy, scale=par[:, w:w + 1]).then_inc(cprod, 1)
                    done[0] += 1

            for c in range(20):
                split_ahead(IN2 + c)
                if 4 <= c < 8:
                    k = c - 4
                    act.wait_ge(gemm_evac, E_IN2 + c + 1)
                    act.activation(sq[:, k, NMETA:], proj[:, c, NMETA:], ACT.Sigmoid).then_inc(glu, 1)
                if c >= 9:
                    conv_products(2)
            for g in range(2):
                values(6 + g, P, vtok[:, g, 0:512], (stat_bank, aux_bank)[g])
            for u in range(MOBA_U + 2):
                softmax_step(u, MOBA_U, FOX_U, MOBA_N, MOBA_TILES, [stat_bank])
                conv_products(2)
                if u >= 5 and u % 4 == 1:
                    pair = u // 4 - 1
                    act.wait_ge(o_ready, FOX_U + 4 * pair + 4)
                    act.activation(af[:, pair, :], aux_bank[:, 0:SEQ], ACT.Copy).then_inc(af_ready, 1)
                    operand_hi(A_CAT2, F_CAT2, pair)
                    if pair:
                        split_ahead(OUT2 + pair - 1)
            conv_products(m * CONV_T)
            for k in range(CONV_C):
                act.wait_ge(ln_dev, k + 1)
                act.activation(sq[:, k, NMETA:], cv[:, k, :], ACT.Square).then_inc(ln_sq, 1)
            split_ahead(OUT2 + 3)
            act.wait_ge(ln_var, 1)
            act.activation(std[:, NMETA:], gemm_bank[1][:, 0:SEQ], ACT.Sqrt, bias=eps[:, 0:1],
                           scale=1.0 / (CONV_C * P)).then_inc(ln_std, 1)
            for k in range(CONV_C):
                g, b = COL["ab_ln_g_2"] + k, COL["ab_ln_b_2"] + k
                act.wait_ge(ln_norm, k + 1)
                act.activation(af[:, 4 + k, :], cv[:, k, :], ACT.Silu, scale=par[:, g:g + 1], bias=par[:, b:b + 1]).then_inc(af_ready, 1)
                operand_hi(A_CAT2, F_CAT2, 4 + k)
            for n in range(OUT2 + 4, MLP2):
                split_ahead(n)
            residual_hi(N_MLP0)
            root(N_MLP0, stat_bank[:, 0:SEQ])

            def squared_relu(f, n, e0, q=0):
                split_ahead(n, q)
                act.wait_ge(gemm_evac, e0 + f + 1 + 2 * q)
                act.activation(hidhi[:, f % 2, :], hid[:, f % 2, :], ACT.Square).then_inc(hid_hi, 1)
                if f >= 1:
                    split_ahead(n + 1, q)

            def squared_relu_mlp(base, e0):
                squared_relu(0, base, e0)
                squared_relu(1, base + 1, e0)
                last = (FF2 - 2) // 2 - 1
                with act.Fori(0, last) as it:
                    for j in range(2):
                        squared_relu(2 + j, base + 3 + 2 * j, e0, it)
                for j in range(2):
                    squared_relu(2 + j, base + 3 + 2 * j, e0, last)
                split_ahead(base + 2 * FF2 - 1)
            squared_relu_mlp(MLP2, E_MLP2)
            residual_hi(N_MIXC)
            root(N_MIXC, stat_bank[:, 0:SEQ])

            link(act.activation(lam[:, 0, :], par[:, COL["c_lambda_2"]:COL["c_lambda_2"] + KC], ACT.Abs))
            link(act.activation(lam[:, 1, :], lam[:, 0, :], ACT.Exp, scale=-1.0))
            act.activation(lam[:, 2, :], lam[:, 1, :], ACT.Ln, bias=1.0).then_inc(lam_ln, 1)

            def gates(g, col, dst):
                for j in range(KC):
                    act.wait_ge(lru_sum, 4 * g + j // 2 + 1)
                    act.activation(dst(j), half(acc_bank[j // 2], j), ACT.Sigmoid, bias=par[:, col + j:col + j + 1])\
                       .then_inc(lru_gate, 1)

            def decays(js):
                for j in js:
                    act.activation(proj[:, 8 + j, NMETA:], sq[:, j, NMETA:], ACT.Exp, scale=lam[:, 3, j:j + 1]).then_inc(lru_exp, 1)
                    act.activation(t8[:, j, :], sq[:, j, NMETA:], ACT.Tanh, scale=lam[:, 3, j:j + 1]).then_inc(lru_exp, 1)

            chunks = 0
            for i, c in enumerate(IN3_ORDER):
                if i < KC:
                    w, b = COL["c_conv_w_2"] + KC * (LRU_T - 1) + i, COL["c_conv_b_2"] + i
                    act.wait_ge(gemm_evac, E_IN3 + i + 1)
                    act.activation(af[:, i, :], proj[:, 8 + i, NMETA:], ACT.Identity, scale=par[:, w:w + 1],
                                   bias=par[:, b:b + 1]).then_inc(tap0, 1)
                if type(c) is int:
                    split_ahead(IN3 + chunks)
                    chunks += 1
                if c == "r":
                    gates(0, COL["c_b_r_2"], lambda j: sq[:, j, NMETA:])
                    act.wait_ge(lam_ready, 1)
                    act.wait_ge(lru_gate, KC)
                if c == 2:
                    decays(range(0, 4))
                if c == 3:
                    decays(range(4, KC))
                if c == "i":
                    gates(1, COL["c_b_i_2"], lambda j: y[:, j, :])
                if c == 6:
                    for j in range(KC):
                        act.wait_ge(lru_m2, j + 1)
                        act.activation(sq[:, j, NMETA:], sq[:, j, NMETA:], ACT.Sqrt, scale=-1.0).then_inc(lru_root, 1)
            act.wait_ge(gemm_evac, E_IN3 + 16)
            for j in range(KC):
                act.activation(proj[:, j, NMETA:], proj[:, j, NMETA:], ACT.Gelu_apprx_tanh).then_inc(lru_gelu, 1)
            for j in range(KC):
                operand_hi(A_LRU, F_LRU, j)
                if j >= 1:
                    split_ahead(OUT3 + j - 1)
            split_ahead(MLP3 - 1)
            residual_hi(N_MLPC)
            root(N_MLPC, stat_bank[:, 0:SEQ])
            squared_relu_mlp(MLP3, E_MLP3)
            residual_hi(N_FINAL)
            root(N_FINAL, stat_bank[:, 0:SEQ])

        @block.vector
        def _(dve):
            chain = [0]

            def link(ins):
                chain[0] += 1
                ins.then_inc(dve_chain, 1)
                dve.wait_ge(dve_chain, chain[0])

            def split(n, q=0):
                dve.wait_ge(hi_done, n + 1 + R * q)
                dve.tensor_tensor(wlo[:, n % R, :, :], raw[:, n % R, :, :], whi[:, n % R, :, :].bitcast(F32),
                                  ALU.subtract).then_inc(lo_done, 1)

            def split_ahead(n, q=0):
                if n + R * (q if type(q) is int else 0) + LOOKAHEAD < NSLABS:
                    split(n + LOOKAHEAD, q)

            def operand_lo(s, k):
                dve.wait_ge(ahi_ready, KC * s + k + 1)
                dve.tensor_tensor(alo[:, k, NMETA:], af[:, k, :], ahi[:, k, NMETA:].bitcast(F32), ALU.subtract)\
                   .then_inc(alo_ready, 1)

            def residual_lo(i, s, k, lo=NMETA):
                g = GAIN[i] + k
                dve.wait_ge(ahi_ready, KC * s + k + 1)
                dve.scalar_tensor_tensor(alo[:, k, lo:], h[:, k, lo:], par[:, g:g + 1], ahi[:, k, lo:].bitcast(F32),
                                         ALU.mult, ALU.subtract).then_inc(alo_ready, 1)

            def rstd_ready(i, lo=NMETA):
                dve.wait_ge(std_ready, ST0[i] + 1)
                link(dve.reciprocal(rstd[:, lo:], std[:, lo:]))

            def acc_add(m, n, i, s):
                for j in range(KC + 1):
                    if j < KC:
                        if j < KC - 2:
                            dve.wait_ge(acc_ready, 3 * m + j // 2 + 1)
                        else:
                            dve.wait_ge(slab_used, n + 1)
                        dve.tensor_tensor(h[:, j, NMETA:], half(acc_bank[j // 2], j), h[:, j, NMETA:], ALU.add)\
                           .then_inc(h_ready, 1)
                    if j >= 1 and s is not None:
                        residual_lo(i, s, j - 1)

            def take(n, b, d, scale=1.0, lo=NMETA):
                dve.wait_ge(slab_used, n + 1)
                dve.scalar_tensor_tensor(proj[:, d, lo:], gemm_bank[b][:, lo:T1], scale, rstd[:, lo:],
                                         ALU.mult, ALU.mult).then_inc(gemm_evac, 1)
                split_ahead(n)

            def softmax_step(u, units, u0, keys, biased):
                if u < units:
                    n = keys[u % 2]
                    dve.wait_ge(s_ready, u0 + u + 1)
                    if u >= 2:
                        dve.wait_ge(p_ready, u0 + u - 1)
                    biased(u, ssb[:, u % 2, 0:n]).then_inc(s_biased, 1)
                    dve.wait_ge(s_biased, u0 + u + 1)
                    dve.tensor_reduce(nmax[:, u:u + 1], ssb[:, u % 2, 0:n], AX, ALU.max, negate=True)\
                       .then_inc(m_ready, 1)
                if 1 <= u <= units:
                    v, n = u - 1, keys[(u - 1) % 2]
                    dve.wait_ge(p_ready, u0 + v + 1)
                    link(dve.reciprocal(rinv[:, v:v + 1], rsum[:, v:v + 1]))
                    dve.tensor_scalar(prob[:, v % 2, 0:n], prob[:, v % 2, 0:n], rinv[:, v:v + 1], None, ALU.mult)\
                       .then_inc(p_normed, 1)

            dve.wait_ge(par_loaded, 16)
            g0, g1 = COL["final_norm"], COL["mix_norm_2"]
            dve.tensor_tensor(par[:, G_PROD:G_PROD + KC], par[:, g0:g0 + KC], par[:, g1:g1 + KC], ALU.mult).then_inc(gprod, 1)
            for k in range(KC):
                residual_lo(N_NORM1, A_NORM1, k, 0)
            for n in range(LOOKAHEAD):
                split(n)
            rstd_ready(N_NORM1, 0)
            dve.wait_ge(small_loaded, 32)
            dve.wait_ge(slab_used, IN1 + 1)
            dve.tensor_tensor(lf[:, 4, :], gemm_bank[0][0:FOX_HEADS, 0:T1], rstd[0:FOX_HEADS, :], ALU.mult).then_inc(gemm_evac, 1)
            dve.wait_ge(gemm_evac, E_IN1 + 1)
            dve.tensor_scalar(lf[:, 0, :], lf[:, 4, :], fbias[:, 0:1], None, ALU.add).then_inc(fl_x, 1)
            split_ahead(IN1)
            for n in range(IN1 + 1, IN1 + FOX_READY + 1):
                take(n, (n - IN1) % 2, n - IN1 - 1, QSCALE if n - IN1 - 1 < KF else 1.0, 0)
                if n == IN1 + 6:
                    dve.wait_ge(fl_ln, 1)
                    link(dve.scalar_tensor_tensor(lf[:, 1, :], lf[:, 0, :], 0.0, lf[:, 3, :], ALU.min, ALU.subtract))
                    dve.wait_ge(consts, consts_done)
                    dve.tensor_tensor_scan(cum[:, :], lf[:, 1, :], zero6[:, :], 0.0, ALU.add, ALU.add).then_inc(cum_ready, 1)

            def fox_bias(u, dst):
                n = FOX_N[u % 2]
                return dve.tensor_tensor(dst, acc_bank[u % 2][:, 0:n], fmask[:, u % 2, 0:n], ALU.add)
            for u in range(FOX_U + 1):
                softmax_step(u, FOX_U, 0, FOX_N, fox_bias)
                n = IN1 + FOX_READY + 1 + u
                if n < OUT1:
                    d = n - IN1 - 1
                    take(n, (n - IN1) % 2, d, QSCALE if QS <= d < KS else 1.0, 0)
                if u == 6:
                    dve.wait_ge(pool_d, 1)
                    for w, buf, p0, c in ((2, win, 0, 0), (4, win2, HD, 0), (8, win, 0, 1), (16, win2, HD, 1)):
                        ins = dve.scalar_tensor_tensor(pd[p0:p0 + HD, c, :], buf[p0:p0 + HD, c, NMETA:], 1.0 / w,
                                                       proj[p0:p0 + HD, PU + c, NMETA:], ALU.mult, ALU.subtract)
                    ins.then_inc(pool_d, 1)

            dve.wait_ge(pool_mixed, 1)
            for c in range(2):
                g = COL["pool_scale"] + c
                dve.tensor_scalar(af[:, c, :], half(gemm_bank[1], c), par[:, g:g + 1], None, ALU.mult).then_inc(af_ready, 1)

            def head_norms(k, gcol):
                dve.scalar_tensor_tensor(af[:, 2 + k, :], y[:, 2 + k, :], par[:, gcol + k:gcol + k + 1],
                                         sq[:, k, NMETA:], ALU.mult, ALU.mult).then_inc(af_ready, 1)
            dve.wait_ge(hstd, 2)
            link(dve.reciprocal(sq[:, 0:3, NMETA:], sq[:, 0:3, NMETA:]))
            for k in range(3):
                head_norms(k, COL["fox_out_gain"])

            zb = (stat_bank, aux_bank)
            for i in range(SB_HEADS + 1):
                if i < SB_HEADS:
                    dve.wait_ge(z_ln, i + 1)
                    link(dve.scalar_tensor_tensor(sbs[:, :], zb[i % 2][:, 0:SBW], 0.0, sba[:, 2, :], ALU.max, ALU.add))
                    if i >= 1:
                        dve.wait_ge(r_ready, i)
                    dve.tensor_tensor(sbl[:, :], sbs[:, :], sbm[:, :], ALU.mult).then_inc(l_ready, 1)
                if i < 5:
                    operand_lo(A_MIX1, i)
                if i >= 1:
                    dve.wait_ge(r_ready, i)
                    if i >= 2:
                        dve.wait_ge(w_ready, i - 1)
                    dve.tensor_tensor(sbr[:, :], zb[(i - 1) % 2][:, 0:SBW], sbneg[:, :], ALU.add).then_inc(r_masked, 1)
                if 1 <= i < 5:
                    split_ahead(OUT1 + i - 1)
            split_ahead(OUT1 + 4)
            dve.wait_ge(hstd, 4)
            link(dve.reciprocal(sq[:, 3:6, NMETA:], sq[:, 3:6, NMETA:]))
            for k in range(3, 6):
                head_norms(k, COL["fox_out_gain"])
            for i in range(5, KC):
                operand_lo(A_MIX1, i)
            for n in range(OUT1 + 5, MLP1):
                split_ahead(n)
            acc_add(ACC_OUT1, MLP1 - 1, N_NORM2, A_NORM2)
            rstd_ready(N_NORM2)

            def swiglu(f, n, q=0):
                dve.wait_ge(slab_used, n + 1 + 12 * q)
                dve.tensor_tensor(hidg[:, f % 2, :], gemm_bank[0][:, NMETA:T1], rstd[:, NMETA:], ALU.mult).then_inc(gemm_evac, 1)
                split_ahead(n, 3 * q)
                dve.wait_ge(slab_used, n + 2 + 12 * q)
                dve.tensor_tensor(hidu[:, f % 2, :], gemm_bank[1][:, NMETA:T1], rstd[:, NMETA:], ALU.mult).then_inc(gemm_evac, 1)
                dve.wait_ge(gemm_evac, E_MLP1 + 2 * f + 2 + 8 * q)
                dve.wait_ge(act_hid, f + 1 + 4 * q)
                dve.tensor_tensor(hid2[:, f % 2, :], hidu[:, f % 2, :], hid[:, f % 2, :], ALU.mult).then_inc(prod_ready, 1)
                dve.wait_ge(hid_hi, f + 1 + 4 * q)
                dve.tensor_tensor(hidlo[:, f % 2, :], hid2[:, f % 2, :], hidhi[:, f % 2, :].bitcast(F32),
                                  ALU.subtract).then_inc(hid_lo, 1)
                split_ahead(n + 1, 3 * q)
                if f >= 1:
                    split_ahead(n + 2, 3 * q)
            swiglu(0, MLP1)
            swiglu(1, MLP1 + 2)
            with dve.Fori(0, (FF1 - 2) // 4) as it:
                for j in range(4):
                    swiglu(2 + j, MLP1 + 5 + 3 * j, it)
            split_ahead(MLP1 + 3 * FF1 - 1)
            acc_add(ACC_MLP1, IN2 - 1, N_MIX0, A_MIX0)

            dve.wait_ge(std_ready, ST0[N_MIX0] + 1)
            link(dve.reciprocal(r1[:, :], std[:, NMETA:]))
            link(dve.tensor_tensor(rstd[:, NMETA:], r1[:, :], r1[:, :], ALU.mult))
            dve.tensor_tensor(std[:, NMETA:], half(stat_bank, 1), rstd[:, NMETA:], ALU.mult).then_inc(var2_ready, 1)
            dve.wait_ge(std_ready, ST0[N_MIX0] + 2)
            link(dve.reciprocal(rstd[:, NMETA:], std[:, NMETA:]))
            link(dve.tensor_tensor(rstd[:, NMETA:], rstd[:, NMETA:], r1[:, :], ALU.mult))

            taps = [(t, k) for t in range(CONV_T) for k in range(CONV_D)]
            at = [0]

            def conv_taps(count):
                for _ in range(count):
                    if at[0] == len(taps):
                        return
                    t, k = taps[at[0]]
                    c = COL["ab_conv_w_2"] + CONV_C * t + k
                    w, src = par[:, c:c + 1], zpad[:, k, t:t + SEQ]
                    if t == 0:
                        dve.wait_ge(z_pad, k + 1)
                        ins = dve.tensor_scalar(cv[:, k, :], src, w, None, ALU.mult)
                    else:
                        dve.wait_ge(conv, at[0] + 1 - CONV_D)
                        ins = dve.scalar_tensor_tensor(cv[:, k, :], src, w, cv[:, k, :], ALU.mult, ALU.add)
                    ins.then_inc(conv, 1)
                    at[0] += 1
            for c in range(20):
                take(IN2 + c, c % 2, c, QSCALE if 8 <= c < 12 else 1.0)
                if 2 <= c < 10:
                    k = c - 2
                    g = COL["final_norm"] + k
                    dve.scalar_tensor_tensor(h[:, k, NMETA:], h[:, k, NMETA:], par[:, g:g + 1], r1[:, :],
                                             ALU.mult, ALU.mult).then_inc(h_final, 1)
                if c >= 10:
                    conv_taps(2)

            def alibi_bias(u, dst):
                n = MOBA_N[u % 2]
                slope = 2.0 ** (-8.0 * (u // 2 + 1) / MOBA_HEADS)
                return dve.scalar_tensor_tensor(dst, dist[:, u % 2, 0:n], -slope, gemm_bank[u % 2][:, 0:n],
                                                ALU.mult, ALU.add)
            for u in range(MOBA_U + 2):
                softmax_step(u, MOBA_U, FOX_U, MOBA_N, alibi_bias)
                if u >= 6 and u % 4 == 2:
                    pair = u // 4 - 1
                    operand_lo(A_CAT2, pair)
                    if pair:
                        split_ahead(OUT2 + pair - 1)
                conv_taps(3)
            operand_lo(A_CAT2, 3)
            split_ahead(OUT2 + 2)
            conv_taps(len(taps))

            dve.wait_ge(ln_mean, 1)
            for k in range(CONV_C):
                dve.scalar_tensor_tensor(cv[:, k, :], gemm_bank[0][:, 0:SEQ], -1.0 / (CONV_C * P), cv[:, k, :],
                                         ALU.mult, ALU.add).then_inc(ln_dev, 1)
            split_ahead(OUT2 + 3)
            dve.wait_ge(ln_std, 1)
            link(dve.reciprocal(r1[:, :], std[:, NMETA:]))
            for k in range(CONV_C):
                dve.tensor_tensor(cv[:, k, :], cv[:, k, :], r1[:, :], ALU.mult).then_inc(ln_norm, 1)
            for k in range(CONV_C):
                operand_lo(A_CAT2, 4 + k)
            for n in range(OUT2 + 4, MLP2):
                split_ahead(n)
            acc_add(ACC_OUT2, MLP2 - 1, N_MLP0, A_MLP0)
            rstd_ready(N_MLP0)

            def squared_relu(f, n, e0, m0, q=0):
                dve.wait_ge(slab_used, n + 1 + 4 * q)
                dve.scalar_tensor_tensor(hid[:, f % 2, :], gemm_bank[f % 2][:, NMETA:T1], 0.0, rstd[:, NMETA:],
                                         ALU.max, ALU.mult).then_inc(gemm_evac, 1)
                split_ahead(n, q)
                dve.wait_ge(gemm_evac, e0 + f + 1 + 2 * q)
                dve.tensor_tensor(hid2[:, f % 2, :], hid[:, f % 2, :], hid[:, f % 2, :], ALU.mult).then_inc(prod_ready, 1)
                dve.wait_ge(prod_ready, m0 + f + 1 + 2 * q)
                dve.wait_ge(hid_hi, m0 + f + 1 + 2 * q)
                dve.tensor_tensor(hidlo[:, f % 2, :], hid2[:, f % 2, :], hidhi[:, f % 2, :].bitcast(F32),
                                  ALU.subtract).then_inc(hid_lo, 1)
                if f >= 1:
                    split_ahead(n + 1, q)

            def squared_relu_mlp(base, e0, m0):
                squared_relu(0, base, e0, m0)
                squared_relu(1, base + 1, e0, m0)
                last = (FF2 - 2) // 2 - 1
                with dve.Fori(0, last) as it:
                    for j in range(2):
                        squared_relu(2 + j, base + 3 + 2 * j, e0, m0, it)
                for j in range(2):
                    squared_relu(2 + j, base + 3 + 2 * j, e0, m0, last)
                split_ahead(base + 2 * FF2 - 1)
            squared_relu_mlp(MLP2, E_MLP2, FF1)
            acc_add(ACC_MLP2, IN3 - 1, N_MIXC, A_MIXC)

            c = COL["c_lambda_2"]
            link(dve.memset(proj[:, 8:16, NMETA - LRU_T + 1:NMETA], 0.0))
            rstd_ready(N_MIXC)
            dve.wait_ge(lam_ln, 1)
            link(dve.tensor_scalar(lam[:, 0, :], par[:, c:c + KC], -1.0, 0.0, ALU.mult, ALU.max))
            link(dve.tensor_tensor(lam[:, 1, :], lam[:, 0, :], lam[:, 2, :], ALU.add))
            dve.tensor_scalar(lam[:, 3, :], lam[:, 1, :], -LRU_C, None, ALU.mult).then_inc(lam_ready, 1)

            def decay_steps(js):
                for j in js:
                    dve.wait_ge(lru_aa, j + 1)
                    dve.scalar_tensor_tensor(sq[:, j, NMETA:], sq[:, j, NMETA:], 1.0, t8[:, j, :], ALU.add, ALU.mult)\
                       .then_inc(lru_m2, 1)

            chunks = 0
            for i, c in enumerate(IN3_ORDER):
                if type(c) is int:
                    take(IN3 + chunks, chunks % 2, c)
                    chunks += 1
                if i < KC:
                    dve.wait_ge(tap0, i + 1)
                    for t in range(LRU_T - 1):
                        w = COL["c_conv_w_2"] + KC * t + i
                        x0 = NMETA - LRU_T + 1 + t
                        ins = dve.scalar_tensor_tensor(af[:, i, :], proj[:, 8 + i, x0:x0 + SEQ], par[:, w:w + 1],
                                                       af[:, i, :], ALU.mult, ALU.add)
                        if t < LRU_T - 2:
                            link(ins)
                    ins.then_inc(af_ready, 1)
                if c == 3:
                    decay_steps(range(0, 2))
                if c in (4, 5, 6):
                    decay_steps(range(2 * c - 6, 2 * c - 4))
            for j in range(KC):
                dve.wait_ge(lru_root, j + 1)
                dve.wait_ge(lru_ix, j + 1)
                link(dve.tensor_tensor(y[:, j, :], y[:, j, :], sq[:, j, NMETA:], ALU.mult))
                link(dve.tensor_tensor_scan(t8[:, j, :], proj[:, 8 + j, NMETA:], y[:, j, :], 0.0, ALU.mult, ALU.add))
                dve.wait_ge(lru_gelu, j + 1)
                dve.tensor_tensor(af[:, j, :], t8[:, j, :], proj[:, j, NMETA:], ALU.mult).then_inc(af_ready, 1)
                if j >= 1:
                    operand_lo(A_LRU, j - 1)
                if j >= 2:
                    split_ahead(OUT3 + j - 2)
            operand_lo(A_LRU, KC - 1)
            split_ahead(MLP3 - 2)
            split_ahead(MLP3 - 1)
            acc_add(ACC_OUT3, MLP3 - 1, N_MLPC, A_MLPC)
            rstd_ready(N_MLPC)
            squared_relu_mlp(MLP3, E_MLP3, FF1 + FF2)
            acc_add(ACC_MLP3, NSLABS - 1, N_FINAL, None)
            rstd_ready(N_FINAL)
            for k in range(KC):
                g = GAIN[N_FINAL] + k
                dve.scalar_tensor_tensor(y[:, k, :], h[:, k, NMETA:], par[:, g:g + 1], rstd[:, NMETA:],
                                         ALU.mult, ALU.mult).then_inc(fin_ready, 1)

        @block.tensor
        def _(pe):
            def three(dst, n, j, xh, xl, start=False, stop=False):
                hi, lo = whi[:, n % R, j, :], wlo[:, n % R, j, :]
                pe.matmul(dst, hi, xh, start=start, stop=False, skip_group_check=True)
                pe.matmul(dst, hi, xl, start=False, stop=False, skip_group_check=True)
                return pe.matmul(dst, lo, xh, start=False, stop=stop, skip_group_check=True)

            def slab_ready(n, q=0):
                pe.wait_ge(lo_done, n + 1 + R * q)

            def column(n, b, q=0, s=None, lo=NMETA):
                slab_ready(n, q)
                for k in range(KC):
                    if s is not None:
                        pe.wait_ge(alo_ready, KC * s + k + 1)
                    ins = three(gemm_bank[b][:, lo:T1], n, k, ahi[:, k, lo:], alo[:, k, lo:], k == 0, k == KC - 1)
                ins.then_inc(slab_used, 1)

            def row(n, xh, xl, q=0, first=False, last=False):
                slab_ready(n, q)
                for j in range(KC):
                    ins = three(half(acc_bank[j // 2], j), n, j, xh, xl, start=first and j % 2 == 0, stop=last)
                    if last and j % 2 and j < KC - 1:
                        ins.then_inc(acc_ready, 1)
                ins.then_inc(slab_used, 1)

            def operand_row(n0, s, i):
                pe.wait_ge(alo_ready, KC * s + i + 1)
                row(n0 + i, ahi[:, i, NMETA:], alo[:, i, NMETA:], first=(i == 0), last=(i == KC - 1))

            def hidden_row(f, n, m, q=0, first=False, last=False):
                pe.wait_ge(hid_lo, m + 1)
                row(n, hidhi[:, f % 2, :], hidlo[:, f % 2, :], q, first, last)

            def stats(i, lo=NMETA):
                s0 = SQ0[i] // 2
                for part, buf in enumerate((sq[:, :, lo:], t8[:, :, :]) if i == N_MIX0 else (sq[:, :, lo:],)):
                    dst = half(stat_bank, part) if lo else stat_bank[:, 0:T1]
                    for j in range(KC // 2):
                        pe.wait_ge(sum_ready, s0 + 4 * part + j + 1)
                        ins = pe.matmul(dst, ones[:, :], buf[:, 2 * j, :], start=(j == 0), stop=(j == KC // 2 - 1))
                ins.then_inc(stat_ready, 1)

            def values(g, m, chunks, t0, dst):
                for j, c in enumerate(chunks):
                    ins = pe.transpose(dst[0:m, P * j:P * j + P], proj[:, c, t0:t0 + m], ident[:, :])
                ins.then_inc(vT, 1)

            def softmax_step(u, units, u0, qc, kc, k0, keys, tiles, s_banks, t_banks, o_banks, extra, pair_free):
                if u < units:
                    hd, t = u // 2, u % 2
                    b = HD * (hd % 2)
                    if u >= 2:
                        pe.wait_ge(s_biased, u0 + u - 1)
                    n = keys[t]
                    dst = s_banks[t][:, 0:n]
                    ins = pe.matmul(dst, proj[b:b + HD, qc + hd // 2, NMETA + P * t:NMETA + P * t + P],
                                    proj[b:b + HD, kc + hd // 2, k0:k0 + n], start=True, stop=not extra)
                    if extra:
                        ins = extra(hd, t, dst, n)
                    ins.then_inc(s_ready, 1)
                if 1 <= u <= units:
                    v = u - 1
                    pe.wait_ge(p_normed, u0 + v + 1)
                    if v >= len(t_banks):
                        pe.wait_ge(pT_copied, u0 + v + 1 - len(t_banks))
                    for j, m in enumerate(tiles[v % 2]):
                        ins = pe.transpose(t_banks[v % len(t_banks)][0:m, P * j:P * j + P],
                                           prob[:, v % 2, P * j:P * j + m], ident[:, :])
                    ins.then_inc(pT, 1)
                if u >= 2:
                    v = u - 2
                    hd, t, pair = v // 2, v % 2, v // 4
                    b = HD * (hd % 2)
                    pe.wait_ge(pT_copied, u0 + v + 1)
                    if v % 4 == 0:
                        pair_free(pair)
                    for j, m in enumerate(tiles[t]):
                        ins = pe.matmul(o_banks[pair % len(o_banks)][b:b + HD, P * t:P * t + P],
                                        vtok[0:m, j, HD * hd:HD * hd + HD], probT[0:m, t, P * j:P * j + P],
                                        start=(j == 0), stop=(j == len(tiles[t]) - 1))
                    ins.then_inc(o_ready, 1)

            for n in range(IN1, IN1 + FOX_READY + 1):
                if n >= IN1 + 2:
                    pe.wait_ge(gemm_evac, E_IN1 + n - IN1 - 1)
                column(n, (n - IN1) % 2, s=A_NORM1 if n == IN1 else None, lo=0)
                if n == IN1:
                    pe.wait_ge(consts, 1)
                    stats(N_NORM1, 0)
            pe.wait_ge(consts, consts_done)
            pe.wait_ge(gemm_evac, E_IN1 + FOX_READY)
            for g in range(3):
                if g == 2:
                    pe.wait_ge(v_ready, 1)
                values(g, (P, P, NMETA)[g], range(VF, VF + 3), P * g, acc_bank[2 + g % 2])
            pe.wait_ge(cum_ready, 1)
            pe.wait_ge(v_ready, 3)

            def forgetting(hd, t, dst, n):
                pe.matmul(dst, cum[:, NMETA + P * t:NMETA + P * t + P], sel[:, hd, 0:n], start=False, stop=False)
                return pe.matmul(dst, nsel[:, hd, :], cum[:, 0:n], start=False, stop=True)

            def fox_bank(pair):
                if pair >= 2:
                    pe.wait_ge(o_copied, pair - 1)
            for u in range(FOX_U + 2):
                softmax_step(u, FOX_U, 0, QF, KF, 0, FOX_N, FOX_TILES, acc_bank[0:2], acc_bank[2:4],
                             (stat_bank, aux_bank), forgetting, fox_bank)
                n = IN1 + FOX_READY + 1 + u
                if n < OUT1:
                    pe.wait_ge(gemm_evac, E_IN1 + n - IN1 - 1)
                    column(n, (n - IN1) % 2, lo=0)
            pe.wait_ge(pool_d, 2)
            pe.wait_ge(small_loaded, 32)
            pe.wait_ge(gemm_evac, E_IN1 + 21)
            for g in range(4):
                b, c = HD * (g % 2), g // 2
                ins = pe.matmul(gemm_bank[1][b:b + HD, SEQ * c:SEQ * c + SEQ], poolw[b:b + HD, c, :], pd[b:b + HD, c, :],
                                start=True, stop=True)
            ins.then_inc(pool_mixed, 1)
            pe.wait_ge(pT_copied, FOX_U)
            for g in range(3, 6):
                if g == 5:
                    pe.wait_ge(v_ready, 4)
                values(g, (P, P, NMETA)[g - 3], range(VS, VS + 3), P * (g - 3), acc_bank[2 + g % 2])
            for j in range(3):
                pe.wait_ge(hsq, j + 1)
                pe.matmul(half(acc_bank[j // 2], j), block64[:, :], sq[:, j, NMETA:], start=True, stop=True).then_inc(hstat, 1)

            pe.wait_ge(o_copied, 3)
            pe.wait_ge(v_ready, 6)
            zb = (stat_bank, aux_bank)

            def sb_scores(i):
                b, ch = HD * (i % 2), i // 2
                if i >= 2:
                    pe.wait_ge(r_masked, i - 1)
                for j in range(3):
                    k0 = T1 * (KS + ch) + P * j
                    ins = pe.matmul(zb[i % 2][:, SBC[j]:SBC[j] + SBN[j]], flat[b:b + HD, k0:k0 + P],
                                    proj[b:b + HD, QS + ch, NMETA + SBQ[j]:T1], start=(j == 0), stop=False,
                                    skip_group_check=True)
                ins.then_inc(z_ready, 1)

            def sb_sums(i):
                pe.wait_ge(l_ready, i + 1)
                for a in range(3):
                    for j in range(a, 3):
                        m = P if j < 2 else NMETA
                        c = SBC[a] + SBQ[j] - SBQ[a]
                        ins = pe.matmul(zb[i % 2][:, c:c + SBN[j]], (tri if a == j else ones)[0:m, :],
                                        sbl[0:m, SBC[j]:SBC[j] + SBN[j]], start=False, stop=False, skip_group_check=True)
                ins.then_inc(r_ready, 1)

            def sb_values(i):
                pe.wait_ge(w_ready, i + 1)
                if i >= 2 and i % 2 == 0:
                    pe.wait_ge(sbo_copied, i // 2)
                b = HD * (i % 2)
                for j in range(3):
                    m = P if j < 2 else NMETA
                    ins = pe.matmul(gemm_bank[0][b:b + HD, SBQ[j]:SEQ], vtok[0:m, j, FOX_W + HD * i:FOX_W + HD * i + HD],
                                    sbp[0:m, SBC[j]:SBC[j] + SBN[j]], start=(j == 0), stop=(j == 2),
                                    skip_group_check=True)
                ins.then_inc(sbo_ready, 1)
            sb_scores(0)
            pe.wait_ge(hstd, 2)
            for i in range(SB_HEADS + 1):
                if i + 1 < SB_HEADS:
                    sb_scores(i + 1)
                if i < SB_HEADS:
                    sb_sums(i)
                if i >= 1:
                    sb_values(i - 1)
                if i < 5:
                    operand_row(OUT1, A_MIX1, i)
            for j in range(3):
                pe.wait_ge(hsq, 4 + j)
                pe.matmul(half(hsum[j // 2], j), block64[:, :], sq[:, 3 + j, NMETA:], start=True, stop=True).then_inc(hstat, 1)
            for i in range(5, KC):
                operand_row(OUT1, A_MIX1, i)

            def gate_up(f, n, q=0, s=None):
                if f >= 1:
                    pe.wait_ge(gemm_evac, E_MLP1 + 2 * f - 1 + 8 * q)
                column(n, 0, 3 * q, s)
                if s is not None:
                    stats(N_NORM2)
                if f >= 1:
                    pe.wait_ge(gemm_evac, E_MLP1 + 2 * f + 8 * q)
                column(n + 1, 1, 3 * q)
            gate_up(0, MLP1, s=A_NORM2)
            gate_up(1, MLP1 + 2)
            hidden_row(0, MLP1 + 4, 0, first=True)
            with pe.Fori(0, (FF1 - 2) // 4) as it:
                for j in range(4):
                    gate_up(2 + j, MLP1 + 5 + 3 * j, it)
                    hidden_row(1 + j, MLP1 + 7 + 3 * j, it * 4 + 1 + j, it * 3)
            hidden_row(FF1 - 1, MLP1 + 3 * FF1 - 1, FF1 - 1, last=True)

            for c in range(20):
                if c >= 2:
                    pe.wait_ge(gemm_evac, E_IN2 + c - 1)
                column(IN2 + c, c % 2, s=A_MIX0 if c == 0 else None)
                if c == 0:
                    stats(N_MIX0)
            pe.wait_ge(gemm_evac, E_IN2 + 20)
            for g in range(2):
                values(6 + g, P, range(16, 20), NMETA + P * g, (stat_bank, aux_bank)[g])
            pe.wait_ge(v_ready, 8)

            def moba_bank(pair):
                if pair >= 1:
                    pe.wait_ge(af_ready, KC * F_CAT2 + pair)
            for u in range(MOBA_U + 2):
                softmax_step(u, MOBA_U, FOX_U, 8, 12, NMETA, MOBA_N, MOBA_TILES, gemm_bank, [stat_bank], [aux_bank],
                             None, moba_bank)
                if u >= 7 and u % 4 == 3:
                    pair = u // 4 - 1
                    operand_row(OUT2, A_CAT2, pair)
            pe.wait_ge(conv, CONV_T * CONV_D)
            pe.wait_ge(pconv, (CONV_T - 1) * (CONV_C - CONV_D))
            for k in range(CONV_C):
                ins = pe.matmul(gemm_bank[0][:, 0:SEQ], ones[:, :], cv[:, k, :], start=(k == 0), stop=(k == CONV_C - 1))
            ins.then_inc(ln_mean, 1)
            operand_row(OUT2, A_CAT2, 3)
            for k in range(CONV_C):
                pe.wait_ge(ln_sq, k + 1)
                ins = pe.matmul(gemm_bank[1][:, 0:SEQ], ones[:, :], sq[:, k, NMETA:], start=(k == 0), stop=(k == CONV_C - 1))
            ins.then_inc(ln_var, 1)
            for i in range(4, KC):
                operand_row(OUT2, A_CAT2, i)

            def squared_relu_mlp(base, e0, m0, s, i):
                column(base, 0, s=s)
                stats(i)
                column(base + 1, 1)
                hidden_row(0, base + 2, m0, first=True)
                with pe.Fori(0, (FF2 - 2) // 2) as it:
                    for j in range(2):
                        pe.wait_ge(gemm_evac, it * 2 + (e0 + j + 1))
                        column(base + 3 + 2 * j, j, it)
                        hidden_row(1 + j, base + 4 + 2 * j, it * 2 + (m0 + 1 + j), it)
                hidden_row(FF2 - 1, base + 2 * FF2 - 1, m0 + FF2 - 1, last=True)
            squared_relu_mlp(MLP2, E_MLP2, FF1, A_MLP0, N_MLP0)

            chunks = 0
            for i, c in enumerate(IN3_ORDER):
                if type(c) is int:
                    if chunks >= 2:
                        pe.wait_ge(gemm_evac, E_IN3 + chunks - 1)
                    column(IN3 + chunks, chunks % 2, s=A_MIXC if i == 0 else None)
                    chunks += 1
                    if i == 0:
                        stats(N_MIXC)
                    continue
                pe.wait_ge(gatew_loaded, 32)
                for j in range(KC):
                    if c == "r":
                        pe.wait_ge(af_ready, KC * F_CONV + j + 1)
                    else:
                        pe.wait_ge(lru_gate, j // 2 * 2 + 2)
                    ins = pe.matmul(half(acc_bank[j // 2], j), gatew[:, "ri".index(c), j, :], af[:, j, :],
                                    start=True, stop=True)
                    if j % 2:
                        ins.then_inc(lru_sum, 1)
            pe.wait_ge(lru_gate, 2 * KC)
            for i in range(KC):
                operand_row(OUT3, A_LRU, i)
            squared_relu_mlp(MLP3, E_MLP3, FF1 + FF2, A_MLPC, N_MLPC)
            stats(N_FINAL)


def lay_out(a, np):
    def column(w, c0, width=P):
        s = np.zeros((P, KC, P), np.float32)
        s[:, :, 0:width] = w[:, c0:c0 + width].reshape(KC, P, width).transpose(1, 0, 2)
        return s.reshape(P, DM)

    def columns(w, order):
        return [column(w, P * c) for c in order]

    def rows(w, order=None):
        return [w[P * k:P * k + P] for k in (order or range(w.shape[0] // P))]

    def behind(ups, downs):
        s = list(ups[0])
        for u, d in zip(ups[1:], downs):
            s += [*u, d]
        return s + [downs[-1]]

    w_in = a["w_in"][0]
    fl0 = POOL_W + 3 * FOX_W
    s = [column(w_in, fl0, FOX_HEADS)]
    s += [column(w_in, POOL_W + P * c) for c in range(9)]
    s += [column(w_in, P * c) for c in range(2)]
    s += [column(w_in, fl0 + FOX_HEADS + P * c) for c in range(9)]
    s += rows(a["w_out"][0])
    s += behind(list(zip(columns(a["w_gate"][0], range(FF1)), columns(a["w_up"][0], range(FF1)))), rows(a["w_down"][0]))
    s += columns(a["ab_w_in_2"][0], range(20))
    s += rows(a["ab_w_out_2"][0], OUT2_ORDER)
    mlp = [behind([(u,) for u in columns(a["w_up_2"][i], range(FF2))], rows(a["w_down_2"][i])) for i in range(2)]
    s += mlp[0]
    s += columns(a["c_w_in_2"][0], [c for c in IN3_ORDER if type(c) is int])
    s += rows(a["c_w_out_2"][0])
    s += mlp[1]
    x = np.concatenate([a["meta_tokens"], a["x"][0]])
    return {
        "slabs": np.stack(s).reshape(NSLABS, P, KC, P),
        "xT": np.ascontiguousarray(x.T.reshape(KC, P, T1).transpose(1, 0, 2)),
        "par": np.ascontiguousarray(np.concatenate([a[name].reshape(-1, P) for name, _ in PAR]).T),
        "fbias": np.ascontiguousarray(a["forget_bias"].T),
        "poolw": np.ascontiguousarray(a["pool_w"][0].reshape(2, 2 * HD, HD).transpose(1, 0, 2)),
        "gatew": np.stack([a["c_w_r_2"][0].transpose(1, 0, 2), a["c_w_i_2"][0].transpose(1, 0, 2)]),
    }


def kernel(**inputs):
    import numpy as np
    import concourse.bacc as bacc
    from concourse.bass_utils import run_bass_kernel_spmd as run

    nc = bacc.Bacc("TRN2", target_bir_lowering=False, num_devices=1)
    arrays = {f"in_{k}": v for k, v in lay_out({k: np.asarray(v) for k, v in inputs.items()}, np).items()}
    args = [nc.dram_tensor(k, v.shape, mybir.dt.from_np(v.dtype), kind="ExternalInput").ap() for k, v in arrays.items()]
    out = nc.dram_tensor("out", (P, KC, SEQ), F32, kind="ExternalOutput").ap()
    build(nc, *args, out)
    r = run(nc, [arrays], core_ids=[0])
    return np.ascontiguousarray(r.results[0]["out"].transpose(2, 1, 0)).reshape(1, SEQ, DM)
```

```python
from contextlib import ExitStack

import concourse.bass as bass
from concourse import mybir

F32 = mybir.dt.float32
F32R = mybir.dt.float32r
ALU = mybir.AluOpType
ACT = mybir.ActivationFunctionType
AX = mybir.AxisListType.X

P = 128
DM = 1024
KC = DM // P
SEQ = 256
NMETA = 16
T1 = NMETA + SEQ
EPS = 1e-6
BIG = 1.0e30

FOX_HEADS = SB_HEADS = 6
HD = 64
QSCALE = HD ** -0.5
POOL_W = 256
FOX_W = FOX_HEADS * HD
MOBA_HEADS = 8
CONV_T = 31
CONV_C = 4
CONV_STEP = 3
LRU_T = 4
LRU_C = 8.0

FF1 = 2816 // P
FF2 = 4096 // P

R = 4
LOOKAHEAD = R - 1
FINAL_D = 5
WARM_UP = 24

IN1 = 0
OUT1 = IN1 + 21
MLP1 = OUT1 + KC
IN2 = MLP1 + 3 * FF1
MLP2 = IN2 + 20 + KC
IN3 = MLP2 + 2 * FF2
OUT3 = IN3 + 16
MLP3 = OUT3 + KC
NSLABS = MLP3 + 2 * FF2
EARLY = tuple(n + i for n in (IN1, MLP1, IN2, MLP2, IN3, MLP3) for i in range(2))
QF, KF, VF, PU, QS, KS, VS = 0, 3, 6, 9, 11, 14, 17
FOX_READY = 10
OUT1_STEP = {0: 0, 1: 1, 2: 2, 3: 3}
IN2_FIRST = (0, 4, 2, 6, 1, 5, 3, 7, 8, 12, 16)
GLU_ORDER = (0, 2, 1, 3)
IN2_STEP = {1: 9, 2: 13, 3: 17, 4: 10, 6: 14, 7: 18, 8: 11, 10: 15, 11: 19}
OUT2_STEP = {13: 0, 15: 1}
CAT2_STEP = {12: 0, 14: 1, 16: 2, 18: 3}
OUT2 = IN2 + 20
OUT2_ORDER = (4, 5, 6, 7, 0, 1, 2, 3)
IN3_ORDER = tuple(range(8, 16)) + tuple(range(8))

def taps(k0, k1, ahead):
    return [(t, k0) for t in range(ahead)] + \
           [x for t in range(CONV_T - ahead) for x in ((t, k1), (t + ahead, k0))] + \
           [(t, k1) for t in range(CONV_T - ahead, CONV_T)]


CONV_AHEAD = 6
DVE_TAPS, ACT_TAPS = taps(0, 1, CONV_AHEAD), taps(2, 3, CONV_AHEAD)

E_IN1 = 0
E_MLP1 = E_IN1 + 21
E_IN2 = E_MLP1 + 2 * FF1
E_MLP2 = E_IN2 + 20
E_IN3 = E_MLP2 + FF2
E_MLP3 = E_IN3 + 16

(ACC_OUT1, ACC_MLP1, ACC_OUT2, ACC_MLP2, ACC_OUT3, ACC_MLP3) = range(6)
(A_NORM1, A_MIX1, A_NORM2, A_MIX0, A_CAT2, A_MLP0, A_MIXC, A_LRU, A_MLPC) = range(9)
(F_MIX1, F_CAT2, F_CONV, F_LRU) = range(4)
(N_NORM1, N_NORM2, N_MIX0, N_MLP0, N_MIXC, N_MLPC, N_FINAL) = range(7)
RS0 = (0, 1, 2, 4, 5, 6, 7)

PAR = (("norm1", KC), ("norm2", KC), ("final_norm", KC), ("mix_norm_2", 2 * KC), ("mlp_norm_2", 2 * KC),
       ("final_norm_2", KC), ("c_conv_b_2", KC), ("c_b_r_2", KC), ("c_b_i_2", KC), ("c_lambda_2", KC),
       ("pool_scale", 2), ("fox_out_gain", 3), ("sb_out_gain", 3), ("ab_ln_g_2", CONV_C), ("ab_ln_b_2", CONV_C),
       ("ab_conv_w_2", CONV_T * CONV_C), ("c_conv_w_2", LRU_T * KC))
COL = {name: sum(n for _, n in PAR[:i]) for i, (name, _) in enumerate(PAR)}
PAR_N = sum(n for _, n in PAR)
G_PROD = PAR_N
GAIN = {N_NORM1: COL["norm1"], N_NORM2: COL["norm2"], N_MIX0: G_PROD, N_MLP0: COL["mlp_norm_2"],
        N_MIXC: COL["mix_norm_2"] + KC, N_MLPC: COL["mlp_norm_2"] + KC, N_FINAL: COL["final_norm_2"]}

SBQ = (0, 112, 240)
SBC = (0, 256, 400)
SBN = (256, 144, 16)
SBW = 416

FOX_U = 2 * FOX_HEADS
MOBA_U = 2 * MOBA_HEADS
FOX_N = (NMETA + P, NMETA + SEQ)
FOX_TILES = ((P, NMETA), (P, P, NMETA))
MOBA_N = (P, 2 * P)
MOBA_TILES = ((P,), (P, P))


def build(nc, slabs, xT, par_in, fbias_in, poolw_in, gatew_in, out):
    with ExitStack() as ctx:
        def sb(name, shape, dt=F32):
            return ctx.enter_context(nc.sbuf_tensor(name, shape, dt))

        def sem(name):
            return ctx.enter_context(nc.semaphore(name))

        bank = [ctx.enter_context(nc.psum_tensor(f"bank{i}", [P, 512], F32)) for i in range(8)]
        gemm_bank = bank[0:2]
        acc_bank = bank[2:6]
        stat_bank = bank[6]
        aux_bank = bank[7]
        def col_bank(i):
            return aux_bank if i == 2 else gemm_bank[i % 2]

        raw = sb("raw", [P, R, KC, P])
        whi = sb("whi", [P, R, KC, P], F32R)
        wlo = sb("wlo", [P, R, KC, P], F32R)
        h = sb("h", [P, KC, T1])
        af = sb("af", [P, KC, SEQ])
        ahi = sb("ahi", [P, KC, T1], F32R)
        alo = sb("alo", [P, KC, T1], F32R)
        sq = sb("sq", [P, KC, T1])
        gg = sb("gg", [P, KC])
        gmat = sb("gmat", [P, KC, P])
        std = sb("std", [P, T1])
        rstd = sb("rstd", [P, T1])
        r1 = sb("r1", [P, SEQ])
        proj = sb("proj", [P, 20, T1])
        hid = sb("hid", [P, 2, SEQ])
        hid2 = sb("hid2", [P, 2, SEQ])
        hidhi = sb("hidhi", [P, 2, SEQ], F32R)
        hidlo = sb("hidlo", [P, 2, SEQ], F32R)
        par = sb("par", [P, PAR_N + KC])
        fbias = sb("fbias", [FOX_HEADS, 1])
        poolw = sb("poolw", [P, 2, HD])
        ident = sb("ident", [P, P])
        ones = sb("ones", [P, P])
        block64 = sb("block64", [P, P])
        tri = sb("tri", [P, P])
        eps = sb("eps", [P, 1])
        eps2 = sb("eps2", [P, 1])
        zero6 = sb("zero6", [FOX_HEADS, T1])
        nsel = sb("nsel", [FOX_HEADS, FOX_HEADS, P])
        fmask = sb("fmask", [P, 2, T1])
        sbneg = sb("sbneg", [P, SBW])
        sbm = sb("sbm", [P, SBW])
        dist = sb("dist", [P, 2, SEQ])
        lf = sb("lf", [FOX_HEADS, 5, T1])
        cum = sb("cum", [FOX_HEADS, T1])
        cumT = sb("cumT", [P, 2 * FOX_HEADS])
        vtok = sb("vtok", [P, 3, 2 * FOX_W])
        win = sb("win", [P, 2, T1])
        win2 = sb("win2", [P, 2, T1])
        pd = sb("pd", [P, 2, SEQ])
        ssb = sb("ssb", [P, 2, T1])
        nmax = sb("nmax", [P, 16])
        rsum = sb("rsum", [P, 16])
        rinv = sb("rinv", [P, 16])
        prob = sb("prob", [P, 3, T1])
        hidg = ssb[:, :, 0:SEQ]
        hidu = prob[:, 0:2, 0:SEQ]
        probT = sb("probT", [P, 2, 3 * P])
        y = sb("y", [P, KC, SEQ])
        sba = sb("sba", [P, 3, SBW])
        sbs = sb("sbs", [P, SBW])
        sbl = sb("sbl", [P, SBW])
        sbr = sb("sbr", [P, SBW])
        sbp = sb("sbp", [P, SBW])
        zpad = sb("zpad", [P, CONV_C, CONV_T - 1 + SEQ])
        t8 = sb("t8", [P, KC, SEQ])
        cv = t8[:, 0:CONV_C, :]
        cpr = t8[:, CONV_C:KC, :]
        lam = sb("lam", [P, 4, KC])

        raw_loaded = [sem(f"raw_loaded{s}") for s in range(R)]
        hi_done, lo_done, slab_used = sem("hi_done"), sem("lo_done"), sem("slab_used")
        gemm_evac, acc_ready, prod_ready = sem("gemm_evac"), sem("acc_ready"), sem("prod_ready")
        x_loaded = [sem(f"x_loaded{i}") for i in range(KC // 2)]
        par_loaded, small_loaded = sem("par_loaded"), sem("small_loaded")
        consts, gprod = sem("consts"), sem("gprod")
        h_ready = sem("h_ready")
        sq_ready, sum_ready, stat_ready, rstd_ready = sem("sq_ready"), sem("sum_ready"), sem("stat_ready"), sem("rstd_ready")
        var2_ready = sem("var2_ready")
        af_ready, ahi_ready, alo_ready = sem("af_ready"), sem("ahi_ready"), sem("alo_ready")
        act_hid, hid_hi, hid_lo = sem("act_hid"), sem("hid_hi"), sem("hid_lo")
        fl_x, fl_ln, cum_ready, cum_t = sem("fl_x"), sem("fl_ln"), sem("cum_ready"), sem("cum_t")
        vT, v_ready = sem("vT"), sem("v_ready")
        s_ready, s_biased, m_ready, p_ready = sem("s_ready"), sem("s_biased"), sem("m_ready"), sem("p_ready")
        p_normed, pT, pT_copied, o_ready = sem("p_normed"), sem("pT"), sem("pT_copied"), sem("o_ready")
        o_copied = sem("o_copied")
        z_ready, z_ln, l_ready, r_ready = sem("z_ready"), sem("z_ln"), sem("l_ready"), sem("r_ready")
        r_masked, w_ready, sbo_ready, sbo_copied = sem("r_masked"), sem("w_ready"), sem("sbo_ready"), sem("sbo_copied")
        pool_d, pool_mixed = sem("pool_d"), sem("pool_mixed")
        hsq, hstat, hstd = sem("hsq"), sem("hstat"), sem("hstd")
        glu, z_pad, conv, cprod, cused = sem("glu"), sem("z_pad"), sem("conv"), sem("cprod"), sem("cused")
        ln_mean, ln_dev, ln_sq, ln_var = sem("ln_mean"), sem("ln_dev"), sem("ln_sq"), sem("ln_var")
        ln_std, ln_norm = sem("ln_std"), sem("ln_norm")
        gatew_loaded = sem("gatew_loaded")
        lam_ln, lam_ready, tap0 = sem("lam_ln"), sem("lam_ready"), sem("tap0")
        lru_sum, lru_gate, lru_exp, lru_aa, lru_m2 = sem("lru_sum"), sem("lru_gate"), sem("lru_exp"), sem("lru_aa"), sem("lru_m2")
        lru_root, lru_gelu, lru_ix = sem("lru_root"), sem("lru_gelu"), sem("lru_ix")
        dve_chain, act_chain, pool_chain = sem("dve_chain"), sem("act_chain"), sem("pool_chain")
        scaled, fin_ready, fin_pool, stored = sem("scaled"), sem("fin_ready"), sem("fin_pool"), sem("stored")

        gatew = vtok[:, :, :].rearrange("p a b -> p (a b)")[:, 0:2 * DM].rearrange("p (g c t) -> p g c t", g=2, c=KC)
        flat = proj[:, :, :].rearrange("p c t -> p (c t)")
        sb_v_bank = (gemm_bank[0], acc_bank[0], acc_bank[1])
        hsum = (gemm_bank[1], stat_bank)
        consts_done = 16

        def half(b, j):
            return b[:, SEQ * (j % 2):SEQ * (j % 2) + SEQ]

        block = ctx.enter_context(nc.Block())

        @block.sync
        def _(sp):
            for c in range(0, KC, 2):
                sp.dma_start(h[:, c:c + 2, :], xT[:, c:c + 2, :]).then_inc(x_loaded[c // 2], 16)
            for s in range(R):
                sp.dma_start(raw[:, s, :, :], slabs[s]).then_inc(raw_loaded[s], 16)
            with sp.Fori(1, NSLABS // R) as it:
                for s in range(R):
                    sp.wait_ge(lo_done, it * R + (s + 1 - R))
                    sp.dma_start(raw[:, s, :, :], slabs[it * R + s]).then_inc(raw_loaded[s], 16)
            for n in range(NSLABS // R * R, NSLABS):
                sp.wait_ge(lo_done, n + 1 - R)
                sp.dma_start(raw[:, n % R, :, :], slabs[n]).then_inc(raw_loaded[n % R], 16)
            for c in range(0, KC, 2):
                sp.wait_ge(fin_ready, min(c + 2, FINAL_D))
                if c + 2 > FINAL_D:
                    sp.wait_ge(fin_pool, c + 2 - FINAL_D)
                sp.dma_start(out[:, c:c + 2, :], y[:, c:c + 2, :]).then_inc(stored, 16)
            sp.wait_ge(stored, 16 * KC // 2)

        @block.gpsimd
        def _(pool):
            n = [0]

            def step(ins):
                n[0] += 1
                ins.then_inc(pool_chain, 1)
                pool.wait_ge(pool_chain, n[0])

            def select(buf, op, fill, base, pattern, cm):
                pool.affine_select(out=buf, in_=buf, compare_op=op, fill=fill, base=base,
                                   pattern=pattern, channel_multiplier=cm).then_inc(consts, 1)

            def pair_sums(i, lo=NMETA):
                for j in range(KC // 2):
                    pool.wait_ge(sq_ready, KC * i + 2 * j + 2)
                    a, b = sq[:, 2 * j, lo:], sq[:, 2 * j + 1, lo:]
                    pool.tensor_tensor(t8[:, j, :] if i == N_MIX0 else a, a, b, ALU.add).then_inc(sum_ready, 1)

            pool.memset(ones[:, :], 1.0).then_inc(consts, 1)
            pool.memset(eps[:, :], EPS).then_inc(consts, 1)
            pool.memset(eps2[:, :], EPS * EPS).then_inc(consts, 1)
            pair_sums(N_NORM1, 0)
            step(pool.memset(ident[:, :], 0.0))
            select(ident[:, :], ALU.not_equal, 1.0, 0, [[-1, P]], 1)
            step(pool.memset(nsel[:, :, :], 0.0))
            select(nsel[:, :, :], ALU.not_equal, -1.0, 0, [[-1, FOX_HEADS], [0, P]], 1)
            step(pool.memset(block64[:, :], 0.0))
            step(pool.memset(block64[0:HD, 0:HD], 1.0))
            step(pool.memset(block64[HD:P, HD:P], 1.0))
            pool.memset(zero6[:, :], 0.0).then_inc(consts, 1)
            step(pool.memset(tri[:, :], 1.0))
            select(tri[:, :], ALU.is_ge, 0.0, 0, [[-1, P]], 1)
            step(pool.memset(fmask[:, :, :], 0.0))
            select(fmask[:, :, :], ALU.is_ge, -BIG, NMETA, [[P, 2], [-1, T1]], 1)
            step(pool.memset(sbneg[:, :], 0.0))
            step(pool.memset(sbm[:, :], -1.0))
            for i in range(3):
                for buf, fill in ((sbneg, -BIG), (sbm, 0.0)):
                    select(buf[:, SBC[i]:SBC[i] + SBN[i]], ALU.is_gt, fill, NMETA + SBQ[i] - P * i,
                           [[1, SBN[i]]], -1)
            step(pool.iota(dist[:, :, :], pattern=[[P, 2], [-1, SEQ]], base=0, channel_multiplier=1,
                           allow_small_or_imprecise_dtypes=True))
            select(dist[:, :, :], ALU.is_ge, BIG, 0, [[P, 2], [-1, SEQ]], 1)
            pool.memset(zpad[:, :, 0:CONV_T - 1], 0.0).then_inc(consts, 1)
            pool.wait_ge(gemm_evac, E_IN1 + 1 + PU + 2)
            u_ = proj[:, PU:PU + 2, :]
            step(pool.tensor_tensor(win[:, :, 1:], u_[:, :, 1:], u_[:, :, 0:T1 - 1], ALU.add))
            step(pool.tensor_tensor(win2[:, :, 3:], win[:, :, 3:], win[:, :, 1:T1 - 2], ALU.add))
            step(pool.tensor_tensor(win[:, 1, 7:], win2[:, 1, 7:], win2[:, 1, 3:T1 - 4], ALU.add))
            pool.tensor_tensor(win2[:, 1, 15:], win[:, 1, 15:], win[:, 1, 7:T1 - 8], ALU.add).then_inc(pool_d, 1)

            pair_sums(N_NORM2)
            pair_sums(N_MIX0)
            def gated(i):
                k = GLU_ORDER[i]
                pool.wait_ge(glu, i + 1)
                pool.tensor_tensor(zpad[:, k, CONV_T - 1:], proj[:, k, NMETA:], sq[:, k, NMETA:], ALU.mult).then_inc(z_pad, 1)
            gated(0)
            gated(1)
            for i, (t, k) in enumerate(ACT_TAPS):
                if i == 2:
                    gated(2)
                if i == CONV_AHEAD:
                    gated(3)
                if t == 0:
                    pool.sem_inc(cused, 1)
                    continue
                pool.wait_ge(cprod, i + 1)
                last = max(x for x in range(i) if ACT_TAPS[x][1] == k)
                pool.wait_ge(cused, last + 1)
                pool.tensor_tensor(cv[:, k, :], cv[:, k, :], cpr[:, i % 4, :], ALU.add).then_inc(cused, 1)
            pool.wait_ge(o_ready, FOX_U + MOBA_U)
            for g in range(2):
                pool.dma_start(gatew[:, g, :, :], gatew_in[g]).then_inc(gatew_loaded, 16)
            pair_sums(N_MLP0)
            pair_sums(N_MIXC)
            for j in range(KC):
                pool.wait_ge(lru_gate, 2 * j + 2)
                pool.tensor_tensor(y[:, j, :], y[:, j, :], af[:, j, :], ALU.mult).then_inc(lru_ix, 1)
            for j in range(KC):
                pool.wait_ge(lru_exp, j + 1)
                pool.tensor_tensor(sq[:, j, NMETA:], proj[:, 8 + j, NMETA:], proj[:, 8 + j, NMETA:], ALU.mult).then_inc(lru_aa, 1)
            pair_sums(N_MLPC)
            pool.wait_ge(rstd_ready, RS0[N_FINAL] + 1)
            for k in range(FINAL_D, KC):
                pool.wait_ge(scaled, k + 1 - FINAL_D)
                pool.tensor_tensor(y[:, k, :], af[:, k, :], rstd[:, NMETA:], ALU.mult).then_inc(fin_pool, 1)

        @block.scalar
        def _(act):
            chain = [0]

            def link(ins):
                chain[0] += 1
                ins.then_inc(act_chain, 1)
                act.wait_ge(act_chain, chain[0])

            act.dma_start(par[:, 0:PAR_N], par_in).then_inc(par_loaded, 16)
            act.dma_start(fbias[:, :], fbias_in).then_inc(small_loaded, 16)
            act.dma_start(poolw[:, :, :], poolw_in).then_inc(small_loaded, 16)

            def split(n, q=0):
                act.wait_ge(raw_loaded[n % R], 16 * (n // R + 1 + q))
                if n >= R:
                    act.wait_ge(slab_used, n + R * q - R + 1)
                act.activation(whi[:, n % R, :, :], raw[:, n % R, :, :], ACT.Copy).then_inc(hi_done, 1)

            def split_ahead(n, q=0):
                if n not in EARLY and n + LOOKAHEAD < NSLABS:
                    split(n + LOOKAHEAD, q)

            def split_early(n):
                split(n + LOOKAHEAD)
                split(n + 1 + LOOKAHEAD)

            def residual_hi(i, lo=NMETA):
                for k in range(KC):
                    if i == N_NORM1:
                        act.wait_ge(x_loaded[k // 2], 16)
                    else:
                        act.wait_ge(h_ready, KC * (i - 1) + k + 1)
                    if i < N_FINAL:
                        g = GAIN[i] + k
                        act.activation(ahi[:, k, lo:], h[:, k, lo:], ACT.Copy, scale=par[:, g:g + 1]).then_inc(ahi_ready, 1)
                    else:
                        act.activation(sq[:, k, lo:], h[:, k, lo:], ACT.Square).then_inc(sq_ready, 1)

            def squares(lo=NMETA):
                for k in range(0, KC, 2):
                    act.activation(sq[:, k:k + 2, lo:], h[:, k:k + 2, lo:], ACT.Square).then_inc(sq_ready, 2)

            def exp_ln_tables():
                act.add_instruction(mybir.InstLoadActFuncSet(name=nc.get_next_instruction_name(), act_func_set_id=6))

            def inverse_root(dst, tmp, src, n, least=eps):
                link(act.activation(tmp, src, ACT.Ln, bias=least[:, 0:1], scale=1.0 / n))
                return act.activation(dst, tmp, ACT.Exp, scale=-0.5)

            def norm_factor(i, src, lo=NMETA):
                act.wait_ge(stat_ready, i + 1)
                inverse_root(rstd[:, lo:], std[:, lo:], src, DM).then_inc(rstd_ready, 1)

            def operand_hi(s, f, k):
                act.wait_ge(af_ready, KC * f + k + 1)
                act.activation(ahi[:, k, NMETA:], af[:, k, :], ACT.Copy).then_inc(ahi_ready, 1)

            def values(g, m, dst, src):
                act.wait_ge(vT, g + 1)
                act.activation(dst, src[0:m, 0:dst.shape[1]], ACT.Copy).then_inc(v_ready, 1)

            def head_factors(k, sums):
                first, last = sq[:, k:k + 2, NMETA:], sq[:, k + 2, NMETA:]
                inverse_root(first, first, sums[0][:, :].rearrange("p (a b) -> p a b", a=2), HD).then_inc(hstd, 1)
                inverse_root(last, last, sums[1][:, 0:SEQ], HD).then_inc(hstd, 1)

            def softmax_step(u, units, u0, keys, tiles, t_banks):
                if 2 <= u <= units + 1:
                    v = u - 2
                    act.wait_ge(pT, u0 + v + 1)
                    if v >= 2:
                        act.wait_ge(o_ready, u0 + v - 1)
                    full = P * sum(m == P for m in tiles[v % 2])
                    src = t_banks[v % len(t_banks)]
                    ins = act.activation(probT[:, v % 2, 0:full], src[:, 0:full], ACT.Copy)
                    if tiles[v % 2][-1] < P:
                        m = tiles[v % 2][-1]
                        ins = act.activation(probT[0:m, v % 2, full:full + P], src[0:m, full:full + P], ACT.Copy)
                    ins.then_inc(pT_copied, 1)
                if u < units:
                    act.wait_ge(m_ready, u0 + u + 1)
                    if u >= 3:
                        act.wait_ge(pT, u0 + u - 2)
                    n = keys[u % 2]
                    act.activation(prob[:, u % 3, 0:n], ssb[:, u % 2, 0:n], ACT.Exp, bias=nmax[:, u:u + 1],
                                   accum_out=rsum[:, u:u + 1]).then_inc(p_ready, 1)

            exp_ln_tables()
            act.wait_ge(par_loaded, 16)
            residual_hi(N_NORM1, 0)
            split(0)
            split(1)
            squares(0)
            split(2)
            split_early(IN1)
            act.wait_ge(consts, 3)
            norm_factor(N_NORM1, stat_bank[:, 0:T1], 0)
            for n in range(IN1, IN1 + FOX_READY):
                split_ahead(n)
                if n == IN1 + 2:
                    act.wait_ge(fl_x, 1)
                    link(act.activation(lf[:, 1, :], lf[:, 0, :], ACT.Abs))
                    link(act.activation(lf[:, 2, :], lf[:, 1, :], ACT.Exp, scale=-1.0))
                    act.activation(lf[:, 3, :], lf[:, 2, :], ACT.Ln, bias=1.0).then_inc(fl_ln, 1)
            split_ahead(IN1 + FOX_READY)
            for g in range(3):
                m = (P, P, NMETA)[g]
                values(g, m, vtok[0:m, g, 0:FOX_W], acc_bank[2 + g % 2])

            zb = (stat_bank, aux_bank)

            def sb_values(j):
                m = (P, P, NMETA)[j]
                values(3 + j, m, vtok[0:m, j, FOX_W:2 * FOX_W], sb_v_bank[j])

            def sb_logarithm(i):
                act.wait_ge(z_ready, i + 1)
                if i >= 1:
                    act.wait_ge(l_ready, i)
                link(act.activation(sba[:, 0, :], zb[i % 2][:, 0:SBW], ACT.Abs))
                link(act.activation(sba[:, 1, :], sba[:, 0, :], ACT.Exp, scale=-1.0))
                act.activation(sba[:, 2, :], sba[:, 1, :], ACT.Ln, bias=1.0).then_inc(z_ln, 1)

            for u in range(FOX_U + 3):
                if 1 <= u <= 10:
                    split_ahead(IN1 + FOX_READY + u)
                softmax_step(u, FOX_U, 0, FOX_N, FOX_TILES, acc_bank[2:4])
                if u >= 6 and u % 4 == 2:
                    pair = u // 4 - 1
                    act.wait_ge(o_ready, 4 * pair + 4)
                    act.activation(y[:, 2 + pair, :], (stat_bank, aux_bank)[pair % 2][:, 0:SEQ], ACT.Copy).then_inc(o_copied, 1)
                    act.wait_ge(o_copied, pair + 1)
                    act.activation(sq[:, pair, NMETA:], y[:, 2 + pair, :], ACT.Square).then_inc(hsq, 1)
                if u == FOX_U:
                    sb_values(0)
            sb_values(1)
            sb_values(2)
            sb_logarithm(0)
            act.wait_ge(hstat, 3)
            head_factors(0, acc_bank[2:4])

            for i in range(SB_HEADS + 2):
                if 1 <= i < SB_HEADS:
                    sb_logarithm(i)
                if i < 5:
                    operand_hi(A_MIX1, F_MIX1, i)
                    if i:
                        split_ahead(OUT1 + i - 1)
                if i >= 3 and i % 2:
                    pair = (i - 3) // 2
                    act.wait_ge(sbo_ready, 2 * pair + 2)
                    act.activation(y[:, 5 + pair, :], gemm_bank[0][:, 0:SEQ], ACT.Copy).then_inc(sbo_copied, 1)
                    act.wait_ge(sbo_copied, pair + 1)
                    act.activation(sq[:, 3 + pair, NMETA:], y[:, 5 + pair, :], ACT.Square).then_inc(hsq, 1)
                if 1 <= i <= SB_HEADS:
                    act.wait_ge(r_masked, i)
                    if i >= 2:
                        act.wait_ge(sbo_ready, i - 1)
                    act.activation(sbp[:, :], sbr[:, :], ACT.Exp).then_inc(w_ready, 1)
            split_ahead(OUT1 + 4)
            act.wait_ge(hstat, 6)
            head_factors(3, hsum)
            for i in range(5, KC):
                operand_hi(A_MIX1, F_MIX1, i)
            for n in range(OUT1 + 5, MLP1):
                split_ahead(n)
            residual_hi(N_NORM2)
            squares()
            split_early(MLP1)
            norm_factor(N_NORM2, stat_bank[:, 0:SEQ])

            def swiglu(f, n, q=0):
                split_ahead(n, 3 * q)
                act.wait_ge(gemm_evac, E_MLP1 + 2 * f + 1 + 8 * q)
                act.activation(hid[:, f % 2, :], hidg[:, f % 2, :], ACT.Silu).then_inc(act_hid, 1)
                act.wait_ge(prod_ready, f + 1 + 4 * q)
                act.activation(hidhi[:, f % 2, :], hid2[:, f % 2, :], ACT.Copy).then_inc(hid_hi, 1)
                split_ahead(n + 1, 3 * q)
                if f >= 1:
                    split_ahead(n + 2, 3 * q)
            swiglu(0, MLP1)
            swiglu(1, MLP1 + 2)
            with act.Fori(0, (FF1 - 2) // 4) as it:
                for j in range(4):
                    swiglu(2 + j, MLP1 + 5 + 3 * j, it)
            split_ahead(MLP1 + 3 * FF1 - 1)

            exp_ln_tables()
            residual_hi(N_MIX0)
            squares()
            split_early(IN2)
            act.wait_ge(var2_ready, 1)
            inverse_root(rstd[:, NMETA:], std[:, NMETA:], std[:, NMETA:], DM, eps2).then_inc(rstd_ready, 1)
            act.wait_ge(rstd_ready, RS0[N_MIX0] + 1)
            inverse_root(r1[:, :], std[:, NMETA:], half(stat_bank, 0), DM).then_inc(rstd_ready, 1)

            done = [0]

            def conv_products(count):
                for i in range(done[0], min(done[0] + count, len(ACT_TAPS))):
                    t, k = ACT_TAPS[i]
                    act.wait_ge(z_pad, GLU_ORDER.index(k) + 1)
                    if i >= 4:
                        act.wait_ge(cused, i - 3)
                    dst = cv[:, k, :] if t == 0 else cpr[:, i % 4, :]
                    w = COL["ab_conv_w_2"] + CONV_C * t + k
                    act.activation(dst, zpad[:, k, t:t + SEQ], ACT.Copy, scale=par[:, w:w + 1]).then_inc(cprod, 1)
                done[0] += count

            for i in range(len(IN2_FIRST)):
                split_ahead(IN2 + i)
                if i in (1, 3, 5, 7):
                    k = GLU_ORDER[i // 2]
                    act.wait_ge(gemm_evac, E_IN2 + i + 1)
                    act.activation(sq[:, k, NMETA:], proj[:, 4 + k, NMETA:], ACT.Sigmoid).then_inc(glu, 1)
                if i >= 5:
                    conv_products(2 if i < 8 else 3)
            exp_ln_tables()
            n = IN2 + len(IN2_FIRST)
            for u in range(MOBA_U + 3):
                if u in IN2_STEP or u in OUT2_STEP:
                    split_ahead(n)
                    n += 1
                softmax_step(u, MOBA_U, FOX_U, MOBA_N, MOBA_TILES, [stat_bank])
                if u % 4 == 0 and u < MOBA_U:
                    pair = u // 4
                    act.wait_ge(vT, 7 + pair)
                    act.activation(vtok[:, 0:2, P * pair:P * pair + P],
                                   acc_bank[2][:, 0:2 * P].rearrange("p (g d) -> p g d", g=2), ACT.Copy).then_inc(v_ready, 1)
                if u >= 6 and u % 4 == 2:
                    pair = u // 4 - 1
                    act.wait_ge(o_ready, FOX_U + 4 * pair + 4)
                    act.activation(af[:, pair, :], aux_bank[:, 0:SEQ], ACT.Copy).then_inc(af_ready, 1)
                if u == max(IN2_STEP) + 1:
                    act.wait_ge(slab_used, OUT2)
                if u in CAT2_STEP:
                    operand_hi(A_CAT2, F_CAT2, CAT2_STEP[u])
                conv_products(CONV_STEP if u < MOBA_U - 1 else len(ACT_TAPS))
                if u == MOBA_U:
                    for k in range(CONV_C):
                        act.wait_ge(ln_dev, k + 1)
                        act.activation(sq[:, k, NMETA:], cv[:, k, :], ACT.Square).then_inc(ln_sq, 1)
            split_ahead(OUT2 + 2)
            act.wait_ge(ln_var, 1)
            inverse_root(r1[:, :], std[:, NMETA:], gemm_bank[1][:, 0:SEQ], CONV_C * P).then_inc(ln_std, 1)
            split_ahead(OUT2 + 3)
            for k in range(CONV_C):
                g, b = COL["ab_ln_g_2"] + k, COL["ab_ln_b_2"] + k
                act.wait_ge(ln_norm, k + 1)
                act.activation(af[:, 4 + k, :], cv[:, k, :], ACT.Silu, scale=par[:, g:g + 1], bias=par[:, b:b + 1]).then_inc(af_ready, 1)
                operand_hi(A_CAT2, F_CAT2, 4 + k)
            for n in range(OUT2 + 4, MLP2):
                split_ahead(n)
            exp_ln_tables()
            link(act.activation(lam[:, 0, :], par[:, COL["c_lambda_2"]:COL["c_lambda_2"] + KC], ACT.Abs))
            link(act.activation(lam[:, 1, :], lam[:, 0, :], ACT.Exp, scale=-1.0))
            act.activation(lam[:, 2, :], lam[:, 1, :], ACT.Ln, bias=1.0).then_inc(lam_ln, 1)
            residual_hi(N_MLP0)
            squares()
            split_early(MLP2)
            norm_factor(N_MLP0, stat_bank[:, 0:SEQ])

            def squared_relu(f, n, e0, q=0):
                split_ahead(n, q)
                act.wait_ge(gemm_evac, e0 + f + 1 + 2 * q)
                if f == 2:
                    act.wait_ge(slab_used, n + 2)
                act.activation(hidhi[:, f % 2, :], hid[:, f % 2, :], ACT.Square).then_inc(hid_hi, 1)
                if f >= 2:
                    split_ahead(n + 1, q)

            def squared_relu_mlp(base, e0):
                for f in range(3):
                    squared_relu(f, base + f, e0)
                split_ahead(base + 4)
                with act.Fori(0, (FF2 - 3) // 2) as it:
                    for j in range(2):
                        squared_relu(3 + j, base + 5 + 2 * j, e0, it)
                squared_relu(FF2 - 1, base + 2 * FF2 - 3, e0)
                split_ahead(base + 2 * FF2 - 1)
            squared_relu_mlp(MLP2, E_MLP2)
            residual_hi(N_MIXC)
            squares()
            split_early(IN3)
            norm_factor(N_MIXC, stat_bank[:, 0:SEQ])

            def gates(k):
                act.wait_ge(lru_sum, k + 1)
                for g, (dst, name) in enumerate(((sq[:, k, NMETA:], "c_b_r_2"), (y[:, k, :], "c_b_i_2"))):
                    b = COL[name] + k
                    act.activation(dst, half(acc_bank[k % 4], g), ACT.Sigmoid, bias=par[:, b:b + 1]).then_inc(lru_gate, 1)
                if k == 0:
                    act.wait_ge(lam_ready, 1)
                act.wait_ge(lru_gate, 2 * k + 1)
                act.activation(t8[:, k, :], sq[:, k, NMETA:], ACT.Tanh, scale=lam[:, 3, k:k + 1])

            def gelus(j0, j1):
                act.wait_ge(gemm_evac, E_IN3 + KC + j1)
                act.activation(proj[:, j0:j1, NMETA:], proj[:, j0:j1, NMETA:], ACT.Gelu_apprx_tanh).then_inc(lru_gelu, j1 - j0)

            for i in range(2 * KC):
                if IN3 + i < OUT3 - 1:
                    split_ahead(IN3 + i)
                if i < KC:
                    w, b = COL["c_conv_w_2"] + KC * (LRU_T - 1) + i, COL["c_conv_b_2"] + i
                    act.wait_ge(gemm_evac, E_IN3 + i + 1)
                    act.activation(af[:, i, :], proj[:, 8 + i, NMETA:], ACT.Identity, scale=par[:, w:w + 1],
                                   bias=par[:, b:b + 1]).then_inc(tap0, 1)
                if 2 <= i < KC + 2:
                    gates(i - 2)
                if i == 10:
                    for j in range(KC):
                        act.activation(proj[:, 8 + j, NMETA:], sq[:, j, NMETA:], ACT.Exp, scale=lam[:, 3, j:j + 1])\
                           .then_inc(lru_exp, 1)
                if i in (12, 13):
                    j = 4 * (i - 12)
                    act.wait_ge(lru_m2, j + 4)
                    act.activation(sq[:, j:j + 4, NMETA:], sq[:, j:j + 4, NMETA:], ACT.Sqrt, scale=-1.0)\
                       .then_inc(lru_root, 4)
                if i == 14:
                    gelus(0, 3)
            act.wait_ge(slab_used, OUT3)
            for j in range(KC):
                operand_hi(A_LRU, F_LRU, j)
                split_ahead(OUT3 + j - 1)
                if j == 0:
                    gelus(3, 6)
                if j == 1:
                    gelus(6, KC)
            split_ahead(MLP3 - 1)
            exp_ln_tables()
            residual_hi(N_MLPC)
            squares()
            split_early(MLP3)
            norm_factor(N_MLPC, stat_bank[:, 0:SEQ])
            squared_relu_mlp(MLP3, E_MLP3)
            residual_hi(N_FINAL)
            for k in range(FINAL_D, KC):
                g = GAIN[N_FINAL] + k
                act.activation(af[:, k, :], h[:, k, NMETA:], ACT.Copy, scale=par[:, g:g + 1]).then_inc(scaled, 1)
            norm_factor(N_FINAL, stat_bank[:, 0:SEQ])

        @block.vector
        def _(dve):
            chain = [0]

            def link(ins):
                chain[0] += 1
                ins.then_inc(dve_chain, 1)
                dve.wait_ge(dve_chain, chain[0])

            def split(n, q=0):
                dve.wait_ge(hi_done, n + 1 + R * q)
                dve.tensor_tensor(wlo[:, n % R, :, :], raw[:, n % R, :, :], whi[:, n % R, :, :].bitcast(F32),
                                  ALU.subtract).then_inc(lo_done, 1)

            def split_ahead(n, q=0):
                if n not in EARLY and n + LOOKAHEAD < NSLABS:
                    split(n + LOOKAHEAD, q)

            def split_early(n):
                split(n + LOOKAHEAD)
                split(n + 1 + LOOKAHEAD)

            def operand_lo(s, k):
                dve.wait_ge(ahi_ready, KC * s + k + 1)
                dve.tensor_tensor(alo[:, k, NMETA:], af[:, k, :], ahi[:, k, NMETA:].bitcast(F32), ALU.subtract)\
                   .then_inc(alo_ready, 1)

            def residual_lo(i, s, k, lo=NMETA):
                g = GAIN[i] + k
                dve.wait_ge(ahi_ready, KC * s + k + 1)
                dve.scalar_tensor_tensor(alo[:, k, lo:], h[:, k, lo:], par[:, g:g + 1], ahi[:, k, lo:].bitcast(F32),
                                         ALU.mult, ALU.subtract).then_inc(alo_ready, 1)

            def acc_add(m, n, i, s):
                for j in range(KC):
                    if j < KC - 2:
                        dve.wait_ge(acc_ready, 3 * m + j // 2 + 1)
                    else:
                        dve.wait_ge(slab_used, n + 1)
                    dve.tensor_tensor(h[:, j, NMETA:], half(acc_bank[j // 2], j), h[:, j, NMETA:], ALU.add)\
                       .then_inc(h_ready, 1)
                if s is not None:
                    for j in range(KC):
                        residual_lo(i, s, j)

            def take(n, src, d, scale=1.0, lo=NMETA, ahead=True):
                dve.wait_ge(slab_used, n + 1)
                dve.scalar_tensor_tensor(proj[:, d, lo:], src[:, lo:T1], scale, rstd[:, lo:],
                                         ALU.mult, ALU.mult).then_inc(gemm_evac, 1)
                if ahead:
                    split_ahead(n)

            def softmax_step(u, units, u0, keys, biased, between=lambda: None):
                if u < units:
                    n = keys[u % 2]
                    dve.wait_ge(s_ready, u0 + u + 1)
                    if u >= 2:
                        dve.wait_ge(p_ready, u0 + u - 1)
                    biased(u, ssb[:, u % 2, 0:n]).then_inc(s_biased, 1)
                    dve.wait_ge(s_biased, u0 + u + 1)
                    dve.tensor_reduce(nmax[:, u:u + 1], ssb[:, u % 2, 0:n], AX, ALU.max, negate=True)\
                       .then_inc(m_ready, 1)
                    between()
                    dve.wait_ge(p_ready, u0 + u + 1)
                    link(dve.reciprocal(rinv[:, u:u + 1], rsum[:, u:u + 1]))
                    dve.tensor_scalar(prob[:, u % 3, 0:n], prob[:, u % 3, 0:n], rinv[:, u:u + 1], None, ALU.mult)\
                       .then_inc(p_normed, 1)

            dve.wait_ge(par_loaded, 16)
            g0, g1 = COL["final_norm"], COL["mix_norm_2"]
            dve.tensor_tensor(par[:, G_PROD:G_PROD + KC], par[:, g0:g0 + KC], par[:, g1:g1 + KC], ALU.mult).then_inc(gprod, 1)
            link(dve.tensor_tensor(gg[:, :], par[:, g0:g0 + KC], par[:, g0:g0 + KC], ALU.mult))
            for k in range(KC):
                residual_lo(N_NORM1, A_NORM1, k, 0)
            for n in range(LOOKAHEAD):
                split(n)
            split_early(IN1)
            dve.wait_ge(rstd_ready, RS0[N_NORM1] + 1)
            dve.wait_ge(small_loaded, 32)
            dve.wait_ge(slab_used, IN1 + 1)
            dve.tensor_tensor(lf[:, 4, :], gemm_bank[0][0:FOX_HEADS, 0:T1], rstd[0:FOX_HEADS, :], ALU.mult).then_inc(gemm_evac, 1)
            dve.wait_ge(gemm_evac, E_IN1 + 1)
            dve.tensor_scalar(lf[:, 0, :], lf[:, 4, :], fbias[:, 0:1], None, ALU.add).then_inc(fl_x, 1)
            split_ahead(IN1)
            for n in range(IN1 + 1, IN1 + FOX_READY + 1):
                take(n, col_bank(n - IN1), n - IN1 - 1, QSCALE if n - IN1 - 1 < KF else 1.0, 0)
                if n == IN1 + 6:
                    dve.wait_ge(fl_ln, 1)
                    link(dve.scalar_tensor_tensor(lf[:, 1, :], lf[:, 0, :], 0.0, lf[:, 3, :], ALU.min, ALU.subtract))
                    dve.wait_ge(consts, consts_done)
                    dve.tensor_tensor_scan(cum[:, :], lf[:, 1, :], zero6[:, :], 0.0, ALU.add, ALU.add).then_inc(cum_ready, 1)
                if n in (IN1 + 7, IN1 + 8):
                    for k in range(4 * (n - IN1 - 7), 4 * (n - IN1 - 6)):
                        dve.tensor_scalar(gmat[:, k, :], ones[:, :], gg[:, k:k + 1], None, ALU.mult).then_inc(gprod, 1)

            def fox_bias(u, dst):
                n = FOX_N[u % 2]
                c = FOX_HEADS * (u % 2) + u // 2
                return dve.scalar_tensor_tensor(dst, acc_bank[u % 2][:, 0:n], cumT[:, c:c + 1], fmask[:, u % 2, 0:n],
                                                ALU.add, ALU.add)
            dve.wait_ge(cum_t, 1)
            dve.tensor_scalar(cumT[:, :], aux_bank[:, 0:2 * FOX_HEADS], 1.0, None, ALU.mult).then_inc(cum_t, 1)
            dve.wait_ge(cum_t, 2)
            for u in range(FOX_U + 1):
                softmax_step(u, FOX_U, 0, FOX_N, fox_bias)
                n = IN1 + FOX_READY + u
                if u >= 1 and n < OUT1:
                    d = n - IN1 - 1
                    take(n, gemm_bank[(n - IN1) % 2], d, QSCALE if QS <= d < KS else 1.0, 0)
                if u == 6:
                    dve.wait_ge(pool_d, 1)
                    for w, buf, p0, c in ((2, win, 0, 0), (4, win2, HD, 0), (8, win, 0, 1), (16, win2, HD, 1)):
                        ins = dve.scalar_tensor_tensor(pd[p0:p0 + HD, c, :], buf[p0:p0 + HD, c, NMETA:], 1.0 / w,
                                                       proj[p0:p0 + HD, PU + c, NMETA:], ALU.mult, ALU.subtract)
                    ins.then_inc(pool_d, 1)

            zb = (stat_bank, aux_bank)

            def minus_softplus(i):
                dve.wait_ge(z_ln, i + 1)
                link(dve.scalar_tensor_tensor(sbs[:, :], zb[i % 2][:, 0:SBW], 0.0, sba[:, 2, :], ALU.max, ALU.add))
                if i >= 1:
                    dve.wait_ge(r_ready, i)
                dve.tensor_tensor(sbl[:, :], sbs[:, :], sbm[:, :], ALU.mult).then_inc(l_ready, 1)

            dve.wait_ge(pool_mixed, 1)
            for c in range(2):
                g = COL["pool_scale"] + c
                dve.tensor_scalar(af[:, c, :], half(gemm_bank[1], c), par[:, g:g + 1], None, ALU.mult).then_inc(af_ready, 1)

            def head_norms(k, gcol):
                dve.scalar_tensor_tensor(af[:, 2 + k, :], y[:, 2 + k, :], par[:, gcol + k:gcol + k + 1],
                                         sq[:, k, NMETA:], ALU.mult, ALU.mult).then_inc(af_ready, 1)
            minus_softplus(0)
            dve.wait_ge(hstd, 2)
            for k in range(3):
                head_norms(k, COL["fox_out_gain"])

            for i in range(SB_HEADS + 1):
                if 1 <= i < SB_HEADS:
                    minus_softplus(i)
                if i < 5:
                    operand_lo(A_MIX1, i)
                if i >= 1:
                    dve.wait_ge(r_ready, i)
                    if i >= 2:
                        dve.wait_ge(w_ready, i - 1)
                    dve.tensor_tensor(sbr[:, :], zb[(i - 1) % 2][:, 0:SBW], sbneg[:, :], ALU.add).then_inc(r_masked, 1)
                if 1 <= i < 5:
                    split_ahead(OUT1 + i - 1)
            split_ahead(OUT1 + 4)
            dve.wait_ge(hstd, 4)
            for k in range(3, 6):
                head_norms(k, COL["fox_out_gain"])
            for i in range(5, KC):
                operand_lo(A_MIX1, i)
            for n in range(OUT1 + 5, MLP1):
                split_ahead(n)
            acc_add(ACC_OUT1, MLP1 - 1, N_NORM2, A_NORM2)
            split_early(MLP1)
            dve.wait_ge(rstd_ready, RS0[N_NORM2] + 1)

            def swiglu(f, n, q=0):
                dve.wait_ge(slab_used, n + 1 + 12 * q)
                src = aux_bank if f == 1 else gemm_bank[0]
                dve.tensor_tensor(hidg[:, f % 2, :], src[:, NMETA:T1], rstd[:, NMETA:], ALU.mult).then_inc(gemm_evac, 1)
                split_ahead(n, 3 * q)
                dve.wait_ge(slab_used, n + 2 + 12 * q)
                dve.tensor_tensor(hidu[:, f % 2, :], gemm_bank[1][:, NMETA:T1], rstd[:, NMETA:], ALU.mult).then_inc(gemm_evac, 1)
                dve.wait_ge(gemm_evac, E_MLP1 + 2 * f + 2 + 8 * q)
                dve.wait_ge(act_hid, f + 1 + 4 * q)
                dve.tensor_tensor(hid2[:, f % 2, :], hidu[:, f % 2, :], hid[:, f % 2, :], ALU.mult).then_inc(prod_ready, 1)
                dve.wait_ge(hid_hi, f + 1 + 4 * q)
                dve.tensor_tensor(hidlo[:, f % 2, :], hid2[:, f % 2, :], hidhi[:, f % 2, :].bitcast(F32),
                                  ALU.subtract).then_inc(hid_lo, 1)
                split_ahead(n + 1, 3 * q)
                if f >= 1:
                    split_ahead(n + 2, 3 * q)
            swiglu(0, MLP1)
            swiglu(1, MLP1 + 2)
            with dve.Fori(0, (FF1 - 2) // 4) as it:
                for j in range(4):
                    swiglu(2 + j, MLP1 + 5 + 3 * j, it)
            split_ahead(MLP1 + 3 * FF1 - 1)
            acc_add(ACC_MLP1, IN2 - 1, N_MIX0, A_MIX0)
            split_early(IN2)

            dve.wait_ge(stat_ready, N_MIX0 + 1)
            link(dve.tensor_scalar(std[:, NMETA:], half(stat_bank, 0), EPS, None, ALU.mult))
            dve.tensor_tensor(std[:, NMETA:], half(stat_bank, 1), std[:, NMETA:], ALU.add).then_inc(var2_ready, 1)
            dve.wait_ge(rstd_ready, RS0[N_MIX0] + 1)

            at = [0]

            def conv_taps(count):
                for i in range(at[0], min(at[0] + count, len(DVE_TAPS))):
                    t, k = DVE_TAPS[i]
                    c = COL["ab_conv_w_2"] + CONV_C * t + k
                    w, src = par[:, c:c + 1], zpad[:, k, t:t + SEQ]
                    if t == 0:
                        dve.wait_ge(z_pad, GLU_ORDER.index(k) + 1)
                        ins = dve.tensor_scalar(cv[:, k, :], src, w, None, ALU.mult)
                    else:
                        dve.wait_ge(conv, max(x for x in range(i) if DVE_TAPS[x][1] == k) + 1)
                        ins = dve.scalar_tensor_tensor(cv[:, k, :], src, w, cv[:, k, :], ALU.mult, ALU.add)
                    ins.then_inc(conv, 1)
                at[0] += count

            def final_residual(k):
                if k == 0:
                    dve.wait_ge(rstd_ready, RS0[N_MIX0] + 2)
                g = COL["final_norm"] + k
                dve.scalar_tensor_tensor(h[:, k, NMETA:], h[:, k, NMETA:], par[:, g:g + 1], r1[:, :],
                                         ALU.mult, ALU.mult)
            for i, c in enumerate(IN2_FIRST):
                take(IN2 + i, col_bank(i), c, QSCALE if 8 <= c < 12 else 1.0)
                if i < 4:
                    final_residual(2 * i)
                    final_residual(2 * i + 1)
                else:
                    conv_taps(3)

            def alibi_bias(u, dst):
                n = MOBA_N[u % 2]
                slope = 2.0 ** (-8.0 * (u // 2 + 1) / MOBA_HEADS)
                return dve.scalar_tensor_tensor(dst, dist[:, u % 2, 0:n], -slope, gemm_bank[u % 2][:, 0:n],
                                                ALU.mult, ALU.add)
            n = IN2 + len(IN2_FIRST)
            for u in range(MOBA_U + 3):
                softmax_step(u, MOBA_U, FOX_U, MOBA_N, alibi_bias, lambda: conv_taps(1))
                if u in IN2_STEP:
                    c = IN2_STEP[u]
                    take(n, acc_bank[n % 2], c, QSCALE if 8 <= c < 12 else 1.0)
                    n += 1
                if u in OUT2_STEP:
                    split_ahead(n)
                    n += 1
                if u in CAT2_STEP:
                    operand_lo(A_CAT2, CAT2_STEP[u])
                conv_taps(2 if u < MOBA_U - 1 else len(DVE_TAPS))
                if u == MOBA_U:
                    dve.wait_ge(ln_mean, 1)
                    for k in range(CONV_C):
                        dve.scalar_tensor_tensor(cv[:, k, :], gemm_bank[0][:, 0:SEQ], -1.0 / (CONV_C * P), cv[:, k, :],
                                                 ALU.mult, ALU.add).then_inc(ln_dev, 1)
            split_ahead(OUT2 + 2)
            dve.wait_ge(ln_std, 1)
            for k in range(CONV_C):
                dve.tensor_tensor(cv[:, k, :], cv[:, k, :], r1[:, :], ALU.mult).then_inc(ln_norm, 1)
            split_ahead(OUT2 + 3)
            for k in range(CONV_C):
                operand_lo(A_CAT2, 4 + k)
            for n in range(OUT2 + 4, MLP2):
                split_ahead(n)
            acc_add(ACC_OUT2, MLP2 - 1, N_MLP0, A_MLP0)
            split_early(MLP2)
            dve.wait_ge(rstd_ready, RS0[N_MLP0] + 1)

            def squared_relu(f, n, e0, m0, q=0):
                dve.wait_ge(slab_used, n + 1 + 4 * q)
                dve.scalar_tensor_tensor(hid[:, f % 2, :], col_bank(f)[:, NMETA:T1], 0.0, rstd[:, NMETA:],
                                         ALU.max, ALU.mult).then_inc(gemm_evac, 1)
                split_ahead(n, q)
                dve.wait_ge(gemm_evac, e0 + f + 1 + 2 * q)
                dve.tensor_tensor(hid2[:, f % 2, :], hid[:, f % 2, :], hid[:, f % 2, :], ALU.mult).then_inc(prod_ready, 1)
                dve.wait_ge(prod_ready, m0 + f + 1 + 2 * q)
                dve.wait_ge(hid_hi, m0 + f + 1 + 2 * q)
                dve.tensor_tensor(hidlo[:, f % 2, :], hid2[:, f % 2, :], hidhi[:, f % 2, :].bitcast(F32),
                                  ALU.subtract).then_inc(hid_lo, 1)
                if f >= 2:
                    split_ahead(n + 1, q)

            def squared_relu_mlp(base, e0, m0):
                for f in range(3):
                    squared_relu(f, base + f, e0, m0)
                split_ahead(base + 4)
                with dve.Fori(0, (FF2 - 3) // 2) as it:
                    for j in range(2):
                        squared_relu(3 + j, base + 5 + 2 * j, e0, m0, it)
                squared_relu(FF2 - 1, base + 2 * FF2 - 3, e0, m0)
                split_ahead(base + 2 * FF2 - 1)
            squared_relu_mlp(MLP2, E_MLP2, FF1)
            link(dve.memset(proj[:, 8:16, NMETA - LRU_T + 1:NMETA], 0.0))
            dve.wait_ge(lam_ln, 1)
            c = COL["c_lambda_2"]
            link(dve.tensor_scalar(lam[:, 0, :], par[:, c:c + KC], -1.0, 0.0, ALU.mult, ALU.max))
            link(dve.tensor_tensor(lam[:, 1, :], lam[:, 0, :], lam[:, 2, :], ALU.add))
            dve.tensor_scalar(lam[:, 3, :], lam[:, 1, :], -LRU_C, None, ALU.mult).then_inc(lam_ready, 1)
            acc_add(ACC_MLP2, IN3 - 1, N_MIXC, A_MIXC)
            split_early(IN3)

            dve.wait_ge(rstd_ready, RS0[N_MIXC] + 1)

            def decay_steps(js):
                for j in js:
                    dve.wait_ge(lru_aa, j + 1)
                    dve.scalar_tensor_tensor(sq[:, j, NMETA:], sq[:, j, NMETA:], 1.0, t8[:, j, :], ALU.add, ALU.mult)\
                       .then_inc(lru_m2, 1)

            def recur(j):
                dve.wait_ge(lru_root, j + 1)
                dve.wait_ge(lru_ix, j + 1)
                link(dve.tensor_tensor(y[:, j, :], y[:, j, :], sq[:, j, NMETA:], ALU.mult))
                link(dve.tensor_tensor_scan(t8[:, j, :], proj[:, 8 + j, NMETA:], y[:, j, :], 0.0, ALU.mult, ALU.add))

            for i, c in enumerate(IN3_ORDER):
                take(IN3 + i, col_bank(i), c, ahead=IN3 + i < OUT3 - 1)
                if 1 <= i <= KC:
                    k = i - 1
                    dve.wait_ge(tap0, k + 1)
                    for t in range(LRU_T - 1):
                        w = COL["c_conv_w_2"] + KC * t + k
                        x0 = NMETA - LRU_T + 1 + t
                        ins = dve.scalar_tensor_tensor(af[:, k, :], proj[:, 8 + k, x0:x0 + SEQ], par[:, w:w + 1],
                                                       af[:, k, :], ALU.mult, ALU.add)
                        if t < LRU_T - 2:
                            link(ins)
                    ins.then_inc(af_ready, 1)
                if i in (11, 12):
                    decay_steps(range(4 * (i - 11), 4 * (i - 10)))
                if i == 13:
                    recur(0)

            def gated_output(j):
                dve.wait_ge(lru_gelu, j + 1)
                dve.tensor_tensor(af[:, j, :], t8[:, j, :], proj[:, j, NMETA:], ALU.mult).then_inc(af_ready, 1)
            gated_output(0)
            recur(1)
            for j in range(KC):
                if j + 1 < KC:
                    gated_output(j + 1)
                operand_lo(A_LRU, j)
                split_ahead(OUT3 + j - 1)
                if j + 2 < KC:
                    recur(j + 2)
            split_ahead(MLP3 - 1)
            acc_add(ACC_OUT3, MLP3 - 1, N_MLPC, A_MLPC)
            split_early(MLP3)
            dve.wait_ge(rstd_ready, RS0[N_MLPC] + 1)
            squared_relu_mlp(MLP3, E_MLP3, FF1 + FF2)
            acc_add(ACC_MLP3, NSLABS - 1, N_FINAL, None)
            dve.wait_ge(h_ready, KC * (ACC_MLP3 + 1))
            for k in range(FINAL_D):
                g = GAIN[N_FINAL] + k
                ins = dve.tensor_scalar(af[:, k, :], h[:, k, NMETA:], par[:, g:g + 1], None, ALU.mult)
            link(ins)
            dve.wait_ge(rstd_ready, RS0[N_FINAL] + 1)
            for k in range(FINAL_D):
                dve.tensor_tensor(y[:, k, :], af[:, k, :], rstd[:, NMETA:], ALU.mult).then_inc(fin_ready, 1)

        @block.tensor
        def _(pe):
            def three(dst, n, j, xh, xl, start=False, stop=False):
                hi, lo = whi[:, n % R, j, :], wlo[:, n % R, j, :]
                pe.matmul(dst, hi, xh, start=start, stop=False, skip_group_check=True)
                pe.matmul(dst, hi, xl, start=False, stop=False, skip_group_check=True)
                return pe.matmul(dst, lo, xh, start=False, stop=stop, skip_group_check=True)

            def slab_ready(n, q=0):
                pe.wait_ge(lo_done, n + 1 + R * q)

            def column(n, bank, q=0, lo=NMETA):
                slab_ready(n, q)
                for k in range(KC):
                    ins = three(bank[:, lo:T1], n, k, ahi[:, k, lo:], alo[:, k, lo:], k == 0, k == KC - 1)
                ins.then_inc(slab_used, 1)

            def first_columns(n, s, lo=NMETA):
                slab_ready(n + 1)
                for k in range(KC):
                    pe.wait_ge(ahi_ready, KC * s + k + 1)
                    for b in range(2):
                        dst, slot = gemm_bank[b][:, lo:T1], (n + b) % R
                        for w in (whi, wlo):
                            pe.matmul(dst, w[:, slot, k, :], ahi[:, k, lo:], start=(k == 0 and w is whi), stop=False,
                                      skip_group_check=True)
                for b in range(2):
                    dst, slot = gemm_bank[b][:, lo:T1], (n + b) % R
                    for k in range(KC):
                        if b == 0:
                            pe.wait_ge(alo_ready, KC * s + k + 1)
                        ins = pe.matmul(dst, whi[:, slot, k, :], alo[:, k, lo:], start=False, stop=(k == KC - 1),
                                        skip_group_check=True)
                    ins.then_inc(slab_used, 1)

            def row(n, xh, xl, q=0, first=False, last=False):
                slab_ready(n, q)
                for j in range(KC):
                    ins = three(half(acc_bank[j // 2], j), n, j, xh, xl, start=first and j % 2 == 0, stop=last)
                    if last and j % 2 and j < KC - 1:
                        ins.then_inc(acc_ready, 1)
                ins.then_inc(slab_used, 1)

            def operand_row(n0, s, i):
                pe.wait_ge(alo_ready, KC * s + i + 1)
                row(n0 + i, ahi[:, i, NMETA:], alo[:, i, NMETA:], first=(i == 0), last=(i == KC - 1))

            def hidden_row(f, n, m, q=0, first=False, last=False):
                pe.wait_ge(hid_lo, m + 1)
                row(n, hidhi[:, f % 2, :], hidlo[:, f % 2, :], q, first, last)

            def stats(i, lo=NMETA):
                dst = half(stat_bank, 0) if lo else stat_bank[:, 0:T1]
                if i == N_MIX0:
                    pe.wait_ge(gprod, 1 + KC)
                    for k in range(KC):
                        pe.wait_ge(sq_ready, KC * i + k + 1)
                        pe.matmul(half(stat_bank, 1), gmat[:, k, :], sq[:, k, lo:], start=(k == 0), stop=(k == KC - 1))
                if i == N_FINAL:
                    for k in range(KC):
                        pe.wait_ge(sq_ready, KC * i + k + 1)
                        ins = pe.matmul(dst, ones[:, :], sq[:, k, lo:], start=(k == 0), stop=(k == KC - 1))
                    ins.then_inc(stat_ready, 1)
                    return
                for j in range(KC // 2):
                    pe.wait_ge(sum_ready, KC // 2 * i + j + 1)
                    src = t8[:, j, :] if i == N_MIX0 else sq[:, 2 * j, lo:]
                    ins = pe.matmul(dst, ones[:, :], src, start=(j == 0), stop=(j == KC // 2 - 1))
                ins.then_inc(stat_ready, 1)

            def values(g, m, chunks, t0, dst):
                for j, c in enumerate(chunks):
                    ins = pe.transpose(dst[0:m, P * j:P * j + P], proj[:, c, t0:t0 + m], ident[:, :])
                ins.then_inc(vT, 1)

            def softmax_step(u, units, u0, qc, kc, k0, keys, tiles, s_banks, t_banks, o_banks, extra, pair_free):
                if u < units:
                    hd, t = u // 2, u % 2
                    b = HD * (hd % 2)
                    if u >= 2:
                        pe.wait_ge(s_biased, u0 + u - 1)
                    n = keys[t]
                    dst = s_banks[t][:, 0:n]
                    ins = pe.matmul(dst, proj[b:b + HD, qc + hd // 2, NMETA + P * t:NMETA + P * t + P],
                                    proj[b:b + HD, kc + hd // 2, k0:k0 + n], start=True, stop=not extra)
                    if extra:
                        ins = extra(hd, t, dst, n)
                    ins.then_inc(s_ready, 1)
                if 2 <= u <= units + 1:
                    v = u - 2
                    pe.wait_ge(p_normed, u0 + v + 1)
                    if v >= len(t_banks):
                        pe.wait_ge(pT_copied, u0 + v + 1 - len(t_banks))
                    for j, m in enumerate(tiles[v % 2]):
                        ins = pe.transpose(t_banks[v % len(t_banks)][0:m, P * j:P * j + P],
                                           prob[:, v % 3, P * j:P * j + m], ident[:, :])
                    ins.then_inc(pT, 1)
                if u >= 3:
                    v = u - 3
                    hd, t, pair = v // 2, v % 2, v // 4
                    b = HD * (hd % 2)
                    pe.wait_ge(pT_copied, u0 + v + 1)
                    if v % 4 == 0:
                        pair_free(pair)
                    for j, m in enumerate(tiles[t]):
                        ins = pe.matmul(o_banks[pair % len(o_banks)][b:b + HD, P * t:P * t + P],
                                        vtok[0:m, j, HD * hd:HD * hd + HD], probT[0:m, t, P * j:P * j + P],
                                        start=(j == 0), stop=(j == len(tiles[t]) - 1))
                    ins.then_inc(o_ready, 1)

            pe.wait_ge(consts, 1)
            for _ in range(WARM_UP):
                pe.matmul(gemm_bank[0][:, 0:P], ones[:, :], ones[:, :], start=True, stop=True)

            first_columns(IN1, A_NORM1, 0)
            stats(N_NORM1, 0)
            for n in range(IN1 + 2, IN1 + FOX_READY + 1):
                if n > IN1 + 2:
                    pe.wait_ge(gemm_evac, E_IN1 + n - IN1 - 1)
                column(n, col_bank(n - IN1), lo=0)
            pe.wait_ge(consts, consts_done)
            pe.wait_ge(gemm_evac, E_IN1 + FOX_READY)
            for g in range(3):
                if g == 2:
                    pe.wait_ge(v_ready, 1)
                values(g, (P, P, NMETA)[g], range(VF, VF + 3), P * g, acc_bank[2 + g % 2])
            pe.wait_ge(cum_ready, 1)
            for t in range(2):
                ins = pe.transpose(aux_bank[:, FOX_HEADS * t:FOX_HEADS * t + FOX_HEADS],
                                   cum[:, NMETA + P * t:NMETA + P * t + P], ident[0:FOX_HEADS, 0:FOX_HEADS])
            ins.then_inc(cum_t, 1)
            pe.wait_ge(v_ready, 3)

            def forgetting(hd, t, dst, n):
                return pe.matmul(dst, nsel[:, hd, :], cum[:, 0:n], start=False, stop=True)

            zb = (stat_bank, aux_bank)

            def sb_scores(i):
                b, ch = HD * (i % 2), i // 2
                if i >= 2:
                    pe.wait_ge(r_masked, i - 1)
                for j in range(3):
                    k0 = T1 * (KS + ch) + P * j
                    ins = pe.matmul(zb[i % 2][:, SBC[j]:SBC[j] + SBN[j]], flat[b:b + HD, k0:k0 + P],
                                    proj[b:b + HD, QS + ch, NMETA + SBQ[j]:T1], start=(j == 0), stop=False,
                                    skip_group_check=True)
                ins.then_inc(z_ready, 1)

            def fox_bank(pair):
                if pair == 1:
                    pe.wait_ge(cum_t, 2)
                if pair >= 2:
                    pe.wait_ge(o_copied, pair - 1)
            for u in range(FOX_U + 3):
                softmax_step(u, FOX_U, 0, QF, KF, 0, FOX_N, FOX_TILES, acc_bank[0:2], acc_bank[2:4],
                             (stat_bank, aux_bank), forgetting, fox_bank)
                n = IN1 + FOX_READY + u
                if u >= 1 and n < OUT1:
                    pe.wait_ge(gemm_evac, E_IN1 + n - IN1 - 1)
                    column(n, gemm_bank[(n - IN1) % 2], lo=0)
                if u == FOX_U - 1:
                    pe.wait_ge(pool_d, 2)
                    pe.wait_ge(small_loaded, 32)
                    pe.wait_ge(gemm_evac, E_IN1 + 21)
                    for g in range(4):
                        b, c = HD * (g % 2), g // 2
                        ins = pe.matmul(gemm_bank[1][b:b + HD, SEQ * c:SEQ * c + SEQ], poolw[b:b + HD, c, :],
                                        pd[b:b + HD, c, :], start=True, stop=True)
                    ins.then_inc(pool_mixed, 1)
                    values(3, P, range(VS, VS + 3), 0, sb_v_bank[0])
                if u == FOX_U:
                    pe.wait_ge(s_biased, FOX_U)
                    values(4, P, range(VS, VS + 3), P, sb_v_bank[1])
                    values(5, NMETA, range(VS, VS + 3), 2 * P, sb_v_bank[2])
            pe.wait_ge(o_copied, 3)
            sb_scores(0)
            for j in range(3):
                pe.wait_ge(hsq, j + 1)
                pe.matmul(half(acc_bank[2 + j // 2], j), block64[:, :], sq[:, j, NMETA:], start=True, stop=True).then_inc(hstat, 1)

            def sb_sums(i):
                pe.wait_ge(l_ready, i + 1)
                for a in range(3):
                    for j in range(a, 3):
                        m = P if j < 2 else NMETA
                        c = SBC[a] + SBQ[j] - SBQ[a]
                        ins = pe.matmul(zb[i % 2][:, c:c + SBN[j]], (tri if a == j else ones)[0:m, :],
                                        sbl[0:m, SBC[j]:SBC[j] + SBN[j]], start=False, stop=False, skip_group_check=True)
                ins.then_inc(r_ready, 1)

            def sb_values(i):
                pe.wait_ge(w_ready, i + 1)
                if i >= 2 and i % 2 == 0:
                    pe.wait_ge(sbo_copied, i // 2)
                b = HD * (i % 2)
                for j in range(3):
                    m = P if j < 2 else NMETA
                    ins = pe.matmul(gemm_bank[0][b:b + HD, SBQ[j]:SEQ], vtok[0:m, j, FOX_W + HD * i:FOX_W + HD * i + HD],
                                    sbp[0:m, SBC[j]:SBC[j] + SBN[j]], start=(j == 0), stop=(j == 2),
                                    skip_group_check=True)
                ins.then_inc(sbo_ready, 1)
            pe.wait_ge(v_ready, 6)
            pe.wait_ge(hstd, 2)
            for i in range(SB_HEADS + 1):
                if i + 1 < SB_HEADS:
                    sb_scores(i + 1)
                if i < SB_HEADS:
                    sb_sums(i)
                if i >= 1:
                    sb_values(i - 1)
                if i in OUT1_STEP:
                    operand_row(OUT1, A_MIX1, OUT1_STEP[i])
            for j in range(3):
                pe.wait_ge(hsq, 4 + j)
                pe.matmul(half(hsum[j // 2], j), block64[:, :], sq[:, 3 + j, NMETA:], start=True, stop=True).then_inc(hstat, 1)
            for i in range(4, KC):
                operand_row(OUT1, A_MIX1, i)

            def gate_up(f, n, q=0):
                if f > 1:
                    pe.wait_ge(gemm_evac, E_MLP1 + 2 * f - 1 + 8 * q)
                column(n, aux_bank if f == 1 else gemm_bank[0], 3 * q)
                pe.wait_ge(gemm_evac, E_MLP1 + 2 * f + 8 * q)
                column(n + 1, gemm_bank[1], 3 * q)
            first_columns(MLP1, A_NORM2)
            stats(N_NORM2)
            gate_up(1, MLP1 + 2)
            hidden_row(0, MLP1 + 4, 0, first=True)
            with pe.Fori(0, (FF1 - 2) // 4) as it:
                for j in range(4):
                    gate_up(2 + j, MLP1 + 5 + 3 * j, it)
                    hidden_row(1 + j, MLP1 + 7 + 3 * j, it * 4 + 1 + j, it * 3)
            hidden_row(FF1 - 1, MLP1 + 3 * FF1 - 1, FF1 - 1, last=True)

            first_columns(IN2, A_MIX0)
            stats(N_MIX0)
            for i in range(2, len(IN2_FIRST)):
                if i > 2:
                    pe.wait_ge(gemm_evac, E_IN2 + i - 1)
                column(IN2 + i, col_bank(i))
            n, taken = IN2 + len(IN2_FIRST), E_IN2 + len(IN2_FIRST)

            def moba_bank(pair):
                pe.wait_ge(v_ready, 7 + pair)
                if pair >= 1:
                    pe.wait_ge(af_ready, KC * F_CAT2 + pair)
            for u in range(MOBA_U + 3):
                new_pair = u % 4 == 0 and u < MOBA_U
                if new_pair:
                    pe.wait_ge(gemm_evac, taken - (1 if u else 0))
                softmax_step(u, MOBA_U, FOX_U, 8, 12, NMETA, MOBA_N, MOBA_TILES, gemm_bank, [stat_bank], [aux_bank],
                             None, moba_bank)
                if new_pair:
                    pe.wait_ge(gemm_evac, taken)
                    for g in range(2):
                        ins = pe.transpose(acc_bank[2][:, P * g:P * g + P],
                                           proj[:, 16 + u // 4, NMETA + P * g:NMETA + P * g + P], ident[:, :])
                    ins.then_inc(vT, 1)
                if u in IN2_STEP:
                    pe.wait_ge(gemm_evac, taken - 1)
                    column(n, acc_bank[n % 2])
                    n, taken = n + 1, taken + 1
                if u in OUT2_STEP:
                    operand_row(OUT2, A_CAT2, OUT2_STEP[u])
                    n += 1
                if u == MOBA_U:
                    pe.wait_ge(conv, len(DVE_TAPS))
                    pe.wait_ge(cused, len(ACT_TAPS))
                    pe.wait_ge(s_biased, FOX_U + MOBA_U)
                    for k in range(CONV_C):
                        ins = pe.matmul(gemm_bank[0][:, 0:SEQ], ones[:, :], cv[:, k, :], start=(k == 0),
                                        stop=(k == CONV_C - 1))
                    ins.then_inc(ln_mean, 1)
            operand_row(OUT2, A_CAT2, 2)
            for k in range(CONV_C):
                pe.wait_ge(ln_sq, k + 1)
                ins = pe.matmul(gemm_bank[1][:, 0:SEQ], ones[:, :], sq[:, k, NMETA:], start=(k == 0), stop=(k == CONV_C - 1))
            ins.then_inc(ln_var, 1)
            for i in range(3, KC):
                operand_row(OUT2, A_CAT2, i)

            def squared_relu_mlp(base, e0, m0, s, i):
                first_columns(base, s)
                stats(i)
                column(base + 2, col_bank(2))
                hidden_row(0, base + 3, m0, first=True)
                hidden_row(1, base + 4, m0 + 1)

                def column_and_row(f, n, q=0):
                    pe.wait_ge(gemm_evac, q * 2 + (e0 + f - 1))
                    column(n, gemm_bank[f % 2], q)
                    hidden_row(f - 1, n + 1, q * 2 + (m0 + f - 1), q)
                with pe.Fori(0, (FF2 - 3) // 2) as it:
                    for j in range(2):
                        column_and_row(3 + j, base + 5 + 2 * j, it)
                column_and_row(FF2 - 1, base + 2 * FF2 - 3)
                hidden_row(FF2 - 1, base + 2 * FF2 - 1, m0 + FF2 - 1, last=True)
            squared_relu_mlp(MLP2, E_MLP2, FF1, A_MLP0, N_MLP0)

            first_columns(IN3, A_MIXC)
            stats(N_MIXC)
            for i in range(2, 2 * KC):
                if i > 2:
                    pe.wait_ge(gemm_evac, E_IN3 + i - 1)
                column(IN3 + i, col_bank(i))
                k = i - 2
                if k < KC:
                    if k == 0:
                        pe.wait_ge(gatew_loaded, 32)
                    pe.wait_ge(af_ready, KC * F_CONV + k + 1)
                    if k >= 4:
                        pe.wait_ge(lru_gate, 2 * (k - 3))
                    for g in range(2):
                        ins = pe.matmul(half(acc_bank[k % 4], g), gatew[:, g, k, :], af[:, k, :], start=True, stop=True)
                    ins.then_inc(lru_sum, 1)
            pe.wait_ge(lru_gate, 2 * KC)
            for i in range(KC):
                operand_row(OUT3, A_LRU, i)
            squared_relu_mlp(MLP3, E_MLP3, FF1 + FF2, A_MLPC, N_MLPC)
            stats(N_FINAL)


def lay_out(a, np):
    def column(w, c0, width=P):
        s = np.zeros((P, KC, P), np.float32)
        s[:, :, 0:width] = w[:, c0:c0 + width].reshape(KC, P, width).transpose(1, 0, 2)
        return s.reshape(P, DM)

    def columns(w, order):
        return [column(w, P * c) for c in order]

    def rows(w, order=None):
        return [w[P * k:P * k + P] for k in (order or range(w.shape[0] // P))]

    def behind(ups, downs):
        s = list(ups[0])
        for u, d in zip(ups[1:], downs):
            s += [*u, d]
        return s + [downs[-1]]

    w_in = a["w_in"][0]
    fl0 = POOL_W + 3 * FOX_W
    s = [column(w_in, fl0, FOX_HEADS)]
    s += [column(w_in, POOL_W + P * c) for c in range(9)]
    s += [column(w_in, P * c) for c in range(2)]
    s += [column(w_in, fl0 + FOX_HEADS + P * c) for c in range(9)]
    s += rows(a["w_out"][0])
    s += behind(list(zip(columns(a["w_gate"][0], range(FF1)), columns(a["w_up"][0], range(FF1)))), rows(a["w_down"][0]))
    s += columns(a["ab_w_in_2"][0], IN2_FIRST + tuple(IN2_STEP.values()))
    s += rows(a["ab_w_out_2"][0], OUT2_ORDER)
    mlp = []
    for i in range(2):
        ups, downs = columns(a["w_up_2"][i], range(FF2)), rows(a["w_down_2"][i])
        mlp.append(ups[0:3] + downs[0:2])
        for u, d in zip(ups[3:], downs[2:]):
            mlp[i] += [u, d]
        mlp[i].append(downs[-1])
    s += mlp[0]
    s += columns(a["c_w_in_2"][0], IN3_ORDER)
    s += rows(a["c_w_out_2"][0])
    s += mlp[1]
    x = np.concatenate([a["meta_tokens"], a["x"][0]])
    return {
        "slabs": np.stack(s).reshape(NSLABS, P, KC, P),
        "xT": np.ascontiguousarray(x.T.reshape(KC, P, T1).transpose(1, 0, 2)),
        "par": np.ascontiguousarray(np.concatenate([a[name].reshape(-1, P) for name, _ in PAR]).T),
        "fbias": np.ascontiguousarray(a["forget_bias"].T),
        "poolw": np.ascontiguousarray(a["pool_w"][0].reshape(2, 2 * HD, HD).transpose(1, 0, 2)),
        "gatew": np.stack([a["c_w_r_2"][0].transpose(1, 0, 2), a["c_w_i_2"][0].transpose(1, 0, 2)]),
    }


def kernel(**inputs):
    import numpy as np
    import concourse.bacc as bacc
    from concourse.bass_utils import run_bass_kernel_spmd as run

    nc = bacc.Bacc("TRN2", target_bir_lowering=False, num_devices=1)
    arrays = {f"in_{k}": v for k, v in lay_out({k: np.asarray(v) for k, v in inputs.items()}, np).items()}
    args = [nc.dram_tensor(k, v.shape, mybir.dt.from_np(v.dtype), kind="ExternalInput").ap() for k, v in arrays.items()]
    out = nc.dram_tensor("out", (P, KC, SEQ), F32, kind="ExternalOutput").ap()
    build(nc, *args, out)
    r = run(nc, [arrays], core_ids=[0])
    return np.ascontiguousarray(r.results[0]["out"].transpose(2, 1, 0)).reshape(1, SEQ, DM)
```
